# Optimizing a Trainium2 kernel written in Bass

```python
import jax, jax.numpy as jnp
from jax import lax
import numpy as np
import math

D_MODEL = 1024
BATCH = 1
SEQ = 512
DEPTH = 2

CHUNK = 64
SB_BLOCK = 128
EPS = 1e-6
GLA_HEADS = 4
GLA_HEAD_K = 64
GLA_HEAD_V = 128
GLA_DK = GLA_HEADS * GLA_HEAD_K
GLA_DV = GLA_HEADS * GLA_HEAD_V
GLA_GATE_RANK = 16
GLA_GATE_NORMALIZER = 16.0
SB_HEADS = 8
SB_HEAD_DIM = 64
SB_D = SB_HEADS * SB_HEAD_DIM
MIX_WIDTH = GLA_DV + SB_D
IN_WIDTH = 2 * GLA_DK + 2 * GLA_DV + GLA_GATE_RANK + 3 * SB_D
CONV_WIDTH = 31
D_FF = -(-8 * D_MODEL // (3 * 256)) * 256
N_EVEN = (DEPTH + 1) // 2
N_ODD = DEPTH // 2


def _rms_f32(xf, g):
    return xf * lax.rsqrt(jnp.mean(xf * xf, axis=-1, keepdims=True) + EPS) * g.astype(jnp.float32)

def rms_norm(x, g):
    return _rms_f32(x.astype(jnp.float32), g).astype(x.dtype)

def gla_mixer(q, k, v, r, gate_lr, w_gate2, b_gate, g_out):
    f32 = jnp.float32
    B, T, _ = q.shape
    nc = T // CHUNK
    log_a = jax.nn.log_sigmoid((gate_lr @ w_gate2 + b_gate).astype(f32)) / GLA_GATE_NORMALIZER

    def split(t, hd):
        return t.astype(f32).reshape(B, nc, CHUNK, -1, hd).transpose(0, 3, 1, 2, 4)

    qc = split(q, GLA_HEAD_K) * (GLA_HEAD_K ** -0.5)
    kc = split(k, GLA_HEAD_K)
    vc = split(v, GLA_HEAD_V)
    bc = jnp.cumsum(split(log_a, GLA_HEAD_K), axis=3)
    b_end = bc[:, :, :, -1:, :]
    k_end = kc * jnp.exp(b_end - bc)
    scores = jnp.einsum('bhnik,bhnjk->bhnij', qc, k_end)
    intra = jnp.einsum('bhnij,bhnjv->bhniv', scores, vc)
    chunk_update = jnp.einsum('bhnjk,bhnjv->bhnkv', k_end, vc)
    chunk_decay = jnp.exp(b_end[:, :, :, 0, :])

    def step(s, inp):
        a, u = inp
        return a[..., None] * s + u, s

    s0 = jnp.zeros((B, GLA_HEADS, GLA_HEAD_K, GLA_HEAD_V), f32)
    _, s_prev = lax.scan(step, s0, (jnp.moveaxis(chunk_decay, 2, 0), jnp.moveaxis(chunk_update, 2, 0)))
    s_prev = jnp.moveaxis(s_prev, 0, 2)
    inter = jnp.einsum('bhnik,bhnkv->bhniv', qc * jnp.exp(b_end), s_prev)
    o = _rms_f32(intra + inter, g_out)
    o = o.transpose(0, 2, 3, 1, 4).reshape(B, T, GLA_DV)
    return o * jax.nn.silu(r.astype(f32))

def stick_breaking_mixer(q, k, v, g_q, g_k):
    f32 = jnp.float32
    B, T, _ = q.shape

    def heads(t):
        return t.astype(f32).reshape(B, T, SB_HEADS, SB_HEAD_DIM).transpose(0, 2, 1, 3)

    qh = _rms_f32(heads(q), g_q) * (SB_HEAD_DIM ** -0.5)
    kh = _rms_f32(heads(k), g_k)
    vh = heads(v)
    outs = []
    for blk in range(T // SB_BLOCK):
        q0 = blk * SB_BLOCK
        kv_len = q0 + SB_BLOCK
        past = np.arange(kv_len)[None, :] < np.arange(q0, kv_len)[:, None]
        z = jnp.einsum('bhtd,bhsd->bhts', qh[:, :, q0:kv_len], kh[:, :, :kv_len])
        log_keep = jnp.where(past, jax.nn.log_sigmoid(-z), 0.0)
        between = lax.cumsum(log_keep, axis=3, reverse=True) - log_keep
        w = jnp.where(past, jnp.exp(jax.nn.log_sigmoid(z) + between), 0.0)
        outs.append(jnp.einsum('bhts,bhsd->bhtd', w, vh[:, :, :kv_len]))
    o = jnp.concatenate(outs, axis=2)
    return o.transpose(0, 2, 1, 3).reshape(B, T, SB_D)

def hybrid_mixer(h, w_in, w_gate2, b_gate, g_gla, g_q, g_k, w_out):
    proj = h @ w_in
    cuts = np.cumsum([GLA_DK, GLA_DK, GLA_DV, GLA_DV, GLA_GATE_RANK, SB_D, SB_D])
    gq, gk, gv, gr, glr, sq, sk, sv = jnp.split(proj, cuts, axis=-1)
    o_gla = gla_mixer(gq, gk, gv, gr, glr, w_gate2, b_gate, g_gla)
    o_sb = stick_breaking_mixer(sq, sk, sv, g_q, g_k)
    o = jnp.concatenate([o_gla, o_sb], axis=-1).astype(h.dtype)
    return o @ w_out

def conformer_conv(h, w_pw1, b_pw1, w_dw, b_dw, ln_g, ln_b, w_pw2, b_pw2):
    a = h @ w_pw1 + b_pw1
    u = a[..., :D_MODEL] * jax.nn.sigmoid(a[..., D_MODEL:])
    u = lax.conv_general_dilated(u, w_dw[:, None, :].astype(u.dtype), window_strides=(1,),
                                 padding=[(CONV_WIDTH - 1, 0)],
                                 dimension_numbers=('NWC', 'WIO', 'NWC'),
                                 feature_group_count=D_MODEL) + b_dw
    uf = u.astype(jnp.float32)
    mu = jnp.mean(uf, axis=-1, keepdims=True)
    var = jnp.mean(jnp.square(uf - mu), axis=-1, keepdims=True)
    u = ((uf - mu) * lax.rsqrt(var + EPS) * ln_g + ln_b).astype(h.dtype)
    return jax.nn.silu(u) @ w_pw2 + b_pw2

def swiglu(h, wg, wu, wd):
    return (jax.nn.silu(h @ wg) * (h @ wu)) @ wd

def first_inputs(seed: int = 0) -> dict:
    key = jax.random.key(seed)
    ks = iter(jax.random.split(key, 32))

    def nrm(shape, scale):
        return jax.random.normal(next(ks), shape, jnp.float32) * scale

    def gain(shape):
        return 1.0 + nrm(shape, 0.05)

    return {
        "x": nrm((BATCH, SEQ, D_MODEL), 1.0),
        "mix_norm": gain((DEPTH, D_MODEL)),
        "ffn_norm": gain((DEPTH, D_MODEL)),
        "hy_w_in": nrm((N_EVEN, D_MODEL, IN_WIDTH), D_MODEL ** -0.5),
        "hy_w_gate2": nrm((N_EVEN, GLA_GATE_RANK, GLA_DK), GLA_GATE_RANK ** -0.5),
        "hy_b_gate": nrm((N_EVEN, GLA_DK), 0.1),
        "hy_gla_norm": gain((N_EVEN, GLA_HEAD_V)),
        "hy_sb_q_norm": gain((N_EVEN, SB_HEAD_DIM)),
        "hy_sb_k_norm": gain((N_EVEN, SB_HEAD_DIM)),
        "hy_w_out": nrm((N_EVEN, MIX_WIDTH, D_MODEL), MIX_WIDTH ** -0.5),
        "cv_w_pw1": nrm((N_ODD, D_MODEL, 2 * D_MODEL), D_MODEL ** -0.5),
        "cv_b_pw1": nrm((N_ODD, 2 * D_MODEL), 0.02),
        "cv_w_dw": nrm((N_ODD, CONV_WIDTH, D_MODEL), CONV_WIDTH ** -0.5),
        "cv_b_dw": nrm((N_ODD, D_MODEL), 0.02),
        "cv_ln_g": gain((N_ODD, D_MODEL)),
        "cv_ln_b": nrm((N_ODD, D_MODEL), 0.02),
        "cv_w_pw2": nrm((N_ODD, D_MODEL, D_MODEL), D_MODEL ** -0.5),
        "cv_b_pw2": nrm((N_ODD, D_MODEL), 0.02),
        "ffn_w_gate": nrm((DEPTH, D_MODEL, D_FF), D_MODEL ** -0.5),
        "ffn_w_up": nrm((DEPTH, D_MODEL, D_FF), D_MODEL ** -0.5),
        "ffn_w_down": nrm((DEPTH, D_FF, D_MODEL), D_FF ** -0.5),
    }

def first_block(x, mix_norm, ffn_norm, hy_w_in, hy_w_gate2, hy_b_gate, hy_gla_norm,
              hy_sb_q_norm, hy_sb_k_norm, hy_w_out, cv_w_pw1, cv_b_pw1, cv_w_dw, cv_b_dw,
              cv_ln_g, cv_ln_b, cv_w_pw2, cv_b_pw2, ffn_w_gate, ffn_w_up, ffn_w_down):
    h = x
    for layer in range(DEPTH):
        hn = rms_norm(h, mix_norm[layer])
        if layer % 2 == 0:
            i = layer // 2
            mix = hybrid_mixer(hn, hy_w_in[i], hy_w_gate2[i], hy_b_gate[i], hy_gla_norm[i],
                               hy_sb_q_norm[i], hy_sb_k_norm[i], hy_w_out[i])
        else:
            i = layer // 2
            mix = conformer_conv(hn, cv_w_pw1[i], cv_b_pw1[i], cv_w_dw[i], cv_b_dw[i],
                                 cv_ln_g[i], cv_ln_b[i], cv_w_pw2[i], cv_b_pw2[i])
        h = h + mix.astype(h.dtype)
        h = h + swiglu(rms_norm(h, ffn_norm[layer]), ffn_w_gate[layer], ffn_w_up[layer],
                       ffn_w_down[layer]).astype(h.dtype)
    return h


N_MIXERS = 2
HEAD_DIM = 64
V_DIM = 2 * HEAD_DIM
N_HEADS = D_MODEL // V_DIM
QK_WIDTH = N_HEADS * 2 * HEAD_DIM
V_WIDTH = N_HEADS * V_DIM
ROT_DIM = HEAD_DIM // 4
ROPE_THETA = 500000.0
Q_BLOCK = 128
CONV_WIDTH_2 = 3
CONV_DIM = D_MODEL
D_FF_2 = 4 * D_MODEL
N_ATTN = (DEPTH + 1) // 2
N_CONV = DEPTH // 2


def rmsnorm(x, g):
    xf = x.astype(jnp.float32)
    y = xf * lax.rsqrt(jnp.mean(xf * xf, axis=-1, keepdims=True) + EPS)
    return (y * g.astype(jnp.float32)).astype(x.dtype)

def rope_tables(seq_len):
    pos = jnp.arange(seq_len, dtype=jnp.float32)
    inv_freq = ROPE_THETA ** (-jnp.arange(0, ROT_DIM, 2, dtype=jnp.float32) / ROT_DIM)
    ang = pos[:, None] * inv_freq[None, :]
    return jnp.cos(ang), jnp.sin(ang)

def apply_partial_rope(t, cos, sin):
    half = ROT_DIM // 2
    x1 = t[..., :half].astype(jnp.float32)
    x2 = t[..., half:ROT_DIM].astype(jnp.float32)
    c = cos[None, :, None, None, :]
    s = sin[None, :, None, None, :]
    rot = jnp.concatenate([x1 * c - x2 * s, x2 * c + x1 * s], axis=-1).astype(t.dtype)
    return jnp.concatenate([rot, t[..., ROT_DIM:]], axis=-1)

def lambda_init_fn(layer_idx):
    return 0.8 - 0.6 * math.exp(-0.3 * layer_idx)

def diff_attention(x, w_qkv, w_o, lq1, lk1, lq2, lk2, subln_g, lambda_init):
    B, S, _ = x.shape
    qkv = x @ w_qkv
    q = qkv[..., :QK_WIDTH].reshape(B, S, N_HEADS, 2, HEAD_DIM)
    k = qkv[..., QK_WIDTH:2 * QK_WIDTH].reshape(B, S, N_HEADS, 2, HEAD_DIM)
    v = qkv[..., 2 * QK_WIDTH:].reshape(B, S, N_HEADS, V_DIM)
    cos, sin = rope_tables(S)
    q = apply_partial_rope(q, cos, sin) * (HEAD_DIM ** -0.5)
    k = apply_partial_rope(k, cos, sin)
    lam = (jnp.exp(jnp.sum(lq1.astype(jnp.float32) * lk1.astype(jnp.float32)))
           - jnp.exp(jnp.sum(lq2.astype(jnp.float32) * lk2.astype(jnp.float32)))
           + lambda_init)
    n_blocks = S // Q_BLOCK
    qb = q.reshape(B, n_blocks, Q_BLOCK, N_HEADS, 2, HEAD_DIM).transpose(1, 0, 2, 3, 4, 5)
    k32 = k.astype(jnp.float32)
    key_pos = jnp.arange(S)

    def block(args):
        q_i, i = args
        s = jnp.einsum('bqhcd,bkhcd->bhcqk', q_i.astype(jnp.float32), k32)
        q_pos = i * Q_BLOCK + jnp.arange(Q_BLOCK)
        mask = key_pos[None, :] <= q_pos[:, None]
        s = jnp.where(mask, s, -jnp.inf)
        p = jax.nn.softmax(s, axis=-1)
        a = p[:, :, 0] - lam * p[:, :, 1]
        return jnp.einsum('bhqk,bkhe->bqhe', a.astype(v.dtype), v)

    o = lax.map(block, (qb, jnp.arange(n_blocks)))
    o = o.transpose(1, 0, 2, 3, 4).reshape(B, S, N_HEADS, V_DIM)
    o = rmsnorm(o, subln_g) * (1.0 - lambda_init)
    return o.reshape(B, S, V_WIDTH) @ w_o

def short_conv(x, w_in, conv_w, w_out):
    h = x @ w_in
    b_gate = h[..., :CONV_DIM]
    c_gate = h[..., CONV_DIM:2 * CONV_DIM]
    u = c_gate * h[..., 2 * CONV_DIM:]
    up = jnp.pad(u, ((0, 0), (CONV_WIDTH_2 - 1, 0), (0, 0)))
    S = x.shape[1]
    y = (conv_w[0] * up[:, 0:S] + conv_w[1] * up[:, 1:S + 1] + conv_w[2] * up[:, 2:S + 2])
    return (b_gate * y) @ w_out

def sq_relu_mlp(x, w_up, w_down):
    return jnp.square(jax.nn.relu(x @ w_up)) @ w_down

def second_inputs(seed: int = 0) -> dict:
    key = jax.random.key(seed)
    ks = jax.random.split(key, 20)
    f32 = jnp.float32
    D = D_MODEL

    def nrm(k, shape, scale):
        return jax.random.normal(k, shape, f32) * scale

    return {
        "x": nrm(ks[0], (BATCH, SEQ, D), 1.0),
        "attn_w_qkv": nrm(ks[1], (N_ATTN, D, 2 * QK_WIDTH + V_WIDTH), D ** -0.5),
        "attn_w_o": nrm(ks[2], (N_ATTN, V_WIDTH, D), V_WIDTH ** -0.5),
        "attn_lambda_q1": nrm(ks[3], (N_ATTN, HEAD_DIM), 0.1),
        "attn_lambda_k1": nrm(ks[4], (N_ATTN, HEAD_DIM), 0.1),
        "attn_lambda_q2": nrm(ks[5], (N_ATTN, HEAD_DIM), 0.1),
        "attn_lambda_k2": nrm(ks[6], (N_ATTN, HEAD_DIM), 0.1),
        "attn_subln_g": 1.0 + nrm(ks[7], (N_ATTN, V_DIM), 0.02),
        "conv_w_in": nrm(ks[8], (N_CONV, D, 3 * CONV_DIM), D ** -0.5),
        "conv_w": nrm(ks[9], (N_CONV, CONV_WIDTH_2, CONV_DIM), CONV_WIDTH_2 ** -0.5),
        "conv_w_out": nrm(ks[10], (N_CONV, CONV_DIM, D), CONV_DIM ** -0.5),
        "mlp_w_up": nrm(ks[11], (DEPTH, D, D_FF_2), D ** -0.5),
        "mlp_w_down": nrm(ks[12], (DEPTH, D_FF_2, D), D_FF_2 ** -0.5),
        "norm_mixer_pre": 1.0 + nrm(ks[13], (DEPTH, D), 0.02),
        "norm_mixer_post": 1.0 + nrm(ks[14], (DEPTH, D), 0.02),
        "norm_mlp_pre": 1.0 + nrm(ks[15], (DEPTH, D), 0.02),
        "norm_mlp_post": 1.0 + nrm(ks[16], (DEPTH, D), 0.02),
    }

def second_block(x, attn_w_qkv, attn_w_o, attn_lambda_q1, attn_lambda_k1, attn_lambda_q2,
              attn_lambda_k2, attn_subln_g, conv_w_in, conv_w, conv_w_out, mlp_w_up,
              mlp_w_down, norm_mixer_pre, norm_mixer_post, norm_mlp_pre, norm_mlp_post):
    for i in range(DEPTH):
        h = rmsnorm(x, norm_mixer_pre[i])
        j = i // N_MIXERS
        if i % N_MIXERS == 0:
            m = diff_attention(h, attn_w_qkv[j], attn_w_o[j], attn_lambda_q1[j],
                               attn_lambda_k1[j], attn_lambda_q2[j], attn_lambda_k2[j],
                               attn_subln_g[j], lambda_init_fn(i))
        else:
            m = short_conv(h, conv_w_in[j], conv_w[j], conv_w_out[j])
        x = x + rmsnorm(m, norm_mixer_post[i])
        h = rmsnorm(x, norm_mlp_pre[i])
        x = x + rmsnorm(sq_relu_mlp(h, mlp_w_up[i], mlp_w_down[i]), norm_mlp_post[i])
    return x


def setup_inputs(seed=0):
    out = dict(first_inputs(seed))
    for name, value in second_inputs(seed + 1).items():
        if name != "x":
            out[name + "_2"] = value
    return out


def reference(
    x, mix_norm, ffn_norm, hy_w_in, hy_w_gate2, hy_b_gate, hy_gla_norm, hy_sb_q_norm,
    hy_sb_k_norm, hy_w_out, cv_w_pw1, cv_b_pw1, cv_w_dw, cv_b_dw, cv_ln_g, cv_ln_b, cv_w_pw2,
    cv_b_pw2, ffn_w_gate, ffn_w_up, ffn_w_down, attn_w_qkv_2, attn_w_o_2, attn_lambda_q1_2,
    attn_lambda_k1_2, attn_lambda_q2_2, attn_lambda_k2_2, attn_subln_g_2, conv_w_in_2, conv_w_2,
    conv_w_out_2, mlp_w_up_2, mlp_w_down_2, norm_mixer_pre_2, norm_mixer_post_2, norm_mlp_pre_2,
    norm_mlp_post_2,
):
    x = first_block(
        x, mix_norm, ffn_norm, hy_w_in, hy_w_gate2, hy_b_gate, hy_gla_norm, hy_sb_q_norm,
        hy_sb_k_norm, hy_w_out, cv_w_pw1, cv_b_pw1, cv_w_dw, cv_b_dw, cv_ln_g, cv_ln_b,
        cv_w_pw2, cv_b_pw2, ffn_w_gate, ffn_w_up, ffn_w_down,
    )
    return second_block(
        x, attn_w_qkv_2, attn_w_o_2, attn_lambda_q1_2, attn_lambda_k1_2, attn_lambda_q2_2,
        attn_lambda_k2_2, attn_subln_g_2, conv_w_in_2, conv_w_2, conv_w_out_2, mlp_w_up_2,
        mlp_w_down_2, norm_mixer_pre_2, norm_mixer_post_2, norm_mlp_pre_2, norm_mlp_post_2,
    )


_drawn_inputs = setup_inputs


def setup_inputs(seed=0):
    import zlib

    import numpy as np

    out = dict(_drawn_inputs(seed))
    spreads = {}
    factors = {'hy_sb_q_norm': 4.013,
     'hy_sb_k_norm': 4.421,
     'attn_lambda_q2_2': 7.912,
     'attn_lambda_k2_2': 6.676,
     'attn_subln_g_2': 4.758,
     'norm_mixer_post_2': 3.661,
     'norm_mlp_pre_2': 3.684,
     'norm_mlp_post_2': 3.978,
     'attn_lambda_q1_2': 64.0,
     'attn_lambda_k1_2': 8.0}
    for name, (base, spread) in spreads.items():
        noise = np.random.default_rng([zlib.crc32(name.encode()), seed]).standard_normal(out[name].shape)
        drawn = base * np.exp(spread * noise) if base else spread * noise
        out[name] = __import__('jax').numpy.asarray(drawn.astype(out[name].dtype))
    for name, factor in factors.items():
        out[name] = (out[name] * factor).astype(out[name].dtype)
    return out
```

```python
from contextlib import ExitStack

import numpy as np

import concourse.bass as bass
from concourse import mybir

F32 = mybir.dt.float32
F32R = mybir.dt.float32r
ACT = mybir.ActivationFunctionType
ALU = mybir.AluOpType
AX = mybir.AxisListType

P = 128
T = 512
D = 1024
KB = D // P
TB = T // P
EPS = 1e-6
NEG = -1e30
LN_EXP = "natural_log_exp_and_others"
RING = 4
LEAD = 3
TAPS = 31
TAPS_PE = 12
PAD = TAPS - 1
FF_GROUPS = (8, 8, 6)
MLP_GROUPS = 4
SB_HEADS, DA_HEADS, GLA_HEADS, CHUNK = 8, 8, 4, 64
CREDIT = 1
CREDITED = "sb_qn sb_rr da_qn sb_o cv_pe da_o sb_yl da_exp da_aT da_rr da_ot".split()
LAMBDA_INIT = 0.2

T_GK, T_GQ, T_GV, T_GR, T_SV, T_SB, T_WO = 0, 2, 4, 8, 12, 16, 32 - 8
T_FF0 = T_WO + 8
T_PW1 = T_FF0 + 68
T_PW2 = T_PW1 + 16
T_FF1 = T_PW2 + 8
T_DV = T_FF1 + 68
T_DA = T_DV + 8
T_DO = T_DA + 16
T_MLP0 = T_DO + 8
T_SC = T_MLP0 + 64
T_SCO = T_SC + 24
T_MLP1 = T_SCO + 8
NT = T_MLP1 + 64
assert T_SB + 8 == T_WO and NT % RING == 0

_cols = {}
_at = 0
for _name, _n in (("pre", 64), ("post", 32), ("b_pw1", 16), ("w_dw", TAPS * KB), ("b_dw", 8), ("ln_g", 8),
                  ("ln_b", 8), ("b_pw2", 8), ("gla", 1), ("sbq", 1), ("sbk", 1), ("subln", 1),
                  ("conv_w", 24), ("lam", 4)):
    _cols[_name] = _at
    _at += _n
NVEC = _at

_consts = {}
_at = 0
for _name, _n in (("ident", P), ("ones", P), ("blk64", P), ("negtri", P), ("negones", P), ("later64", P),
                  ("neg_sb", P), ("neg_da", P), ("mask_sb", P), ("chunk", 2), ("cos", T), ("sin", T)):
    _consts[_name] = (_at, _n)
    _at += _n
NCONST = _at


class Tile:

    def __init__(self, n, rounds=0):
        self.n, self.rounds = n, rounds
        self.slot = n % RING

    def plus(self, d):
        return Tile(self.n + d, self.rounds)

    @property
    def count(self):
        return self.rounds * RING + (self.n + 1)

    @property
    def loaded(self):
        return self.rounds * 16 + 16 * (self.n // RING + 1)


def build(nc, x_t, stream, w_glr, w_gate, vecs, consts, out_t):
    with ExitStack() as ctx:
        def sem(name):
            return ctx.enter_context(nc.semaphore(name))

        def sb(name, shape, dt=F32, where=ctx):
            return where.enter_context(nc.sbuf_tensor(name, shape, dt))

        ps = ctx.enter_context(nc.psum_tensor("ps", [P, 8, 512], F32))
        flat = ps[:].rearrange("p b c -> p (b c)")

        h = sb("h", [P, KB, T])
        xh, xl = sb("xh", [P, KB, T], F32R), sb("xl", [P, KB, T], F32R)
        yh, yl = sb("yh", [P, KB, T], F32R), sb("yl", [P, KB, T], F32R)
        raw = sb("raw", [P, RING, D])
        whi, wlo = sb("whi", [P, RING, D], F32R), sb("wlo", [P, RING, D], F32R)
        vec = sb("vec", [P, NVEC])
        const = sb("const", [P, NCONST])
        sq = sb("sq", [P, 2, T])
        acc = sb("acc", [P, T])
        lnb = sb("lnb", [P, T])
        rrow = sb("rrow", [P, T])
        lncol = sb("lncol", [P, TB])
        rcol = sb("rcol", [P, TB])
        nlam = sb("nlam", [P, 1])
        lamt = sb("lamt", [P, 2, 2])

        def cst(name, rows=slice(None), cols=None):
            a, n = _consts[name]
            return const[rows, a:a + (cols or n)]

        def col(name, j=0):
            a = _cols[name] + j
            return vec[:, a:a + 1] if isinstance(a, int) else vec[:, bass.ds(a, 1)]

        def arena(**shapes):
            scope = ExitStack()
            with scope:
                return {k: scope.enter_context(nc.sbuf_tensor(k, [P] + list(v[:-1] if v[-1] is F32R else v),
                                                              F32R if v[-1] is F32R else F32))
                        for k, v in shapes.items()}

        A = {}
        hyb = ExitStack()
        with hyb:
            A["sv"] = sb("sv", [P, TB, T], F32, hyb)
            A.update(arena(glr=(T,), wg2=(256,), gq=(2, T), gk=(TB, 256), gv=(TB, T), sr=(4, T), la=(TB, 256),
                           gt=(D,), dec=(2, 8), wgr=(D,), wgh=(D, F32R), wgl=(D, F32R)))
            A.update(arena(_glr=(T,), _wg2=(256,), _gq=(2, T), _gk=(TB, 256), _gv=(TB, T), _sr=(4, T), _la=(TB, 256),
                           _gt=(D,), _dec=(2, 8), S=(8, 2, P)))
            A.update(arena(sraw=(2, 2, T), ssq=(2, T), srr=(2, T), sqn=(2, 2, T), vp=(2, TB, P),
                           sl=(2, 1280), sp=(2, 1280)))
        A.update(arena(tg=(2, T), ts=(2, T), tu=(2, T), th=(2, T)))
        A.update(arena(t1=(2, T), t2=(2, T), t3=(2, T), ub=(2, T + PAD), dg=(2, TAPS_PE, P), wt=(2, TAPS_PE), cv=(KB, T), mu=(T,)))
        A.update(arena(dv=(TB, D), draw=(2, T), dsh=(2, T), dq=(2, 2, T), vh=(2, TB, P), ex=(2, 2, T),
                       da=(2, T), aT=(1280,), dot=(T,), nm=(2, 2), sm=(2, 2), rc=(2, 2),
                       r1=(2, 1)))
        A.update(arena(m=(KB, T), pt=(2, T), mr=(2, T), mh=(2, T), cb=(2, T), cc=(2, T), cx=(2, T), uc=(2, T + 2),
                       cy=(2, T)))

        loaded = [sem(f"weight_loaded{s}") for s in range(RING)]
        whi_ready = sem("whi_ready")
        wlo_ready = sem("wlo_ready")
        tile_done = sem("tile_done")
        evac_done = sem("evac_done")
        x_in = [sem(f"x_in{k}") for k in range(KB)]
        small_in = [sem(f"small_in{k}") for k in range(4)]
        xh_ready, x_ready = sem("xh_ready"), sem("x_ready")
        yh_ready, y_ready = sem("yh_ready"), sem("y_ready")
        sq_ready, acc_ready = sem("sq_ready"), sem("acc_ready")
        sum_ready = sem("sum_ready")
        colsum_ready = sem("colsum_ready")
        ln_ready, rrow_ready, rcol_ready = sem("ln_ready"), sem("rrow_ready"), sem("rcol_ready")
        lncol_ready = sem("lncol_ready")
        h_added = sem("h_added")
        post_t = sem("post_t")
        stored = sem("stored")

        S = {}

        def s(name):
            if name not in S:
                S[name] = sem(name)
            return S[name]

        for n in ("wglr_in wglr_hi wglr_lo glr_done glr_evac gate_x gate_abs gate_exp gate_ln la_ready suf_ready "
                  "kd_ready kend_ready dec_ready upd_ready state_ready state_chain go_ready gsq_ready gsum_ready "
                  "gln_ready grr_ready gt_ready gy_ready gyh_ready row0 "
                  "sb_sq sb_sum sb_ln sb_rr sb_qn sb_vp sb_z sb_abs sb_exp sb_ln2 sb_sp sb_mask sb_acc sb_w "
                  "sb_o sb_yh sb_yl mix_y "
                  "wt_ready pw_sg pw_u pw_zero dg_ready dg_used cv_pe cv_chain cv_done mu_acc mu_sum mu_copied cen_ready ln_t ln_s pw_in "
                  "lam_p lam_s lam_e lam_ready "
                  "da_sh da_shs da_rc da_qn da_vh da_s da_max da_exp da_rcp da_r1 da_t da_a da_T da_aT da_o da_sq da_sum "
                  "da_ln da_rr da_ot m_zero sc_u sc_y sc_zero sc_in").split():
            s(n)
        for f in (0, 1):
            for n in ("silu", "hid"):
                s(f"ff{f}_{n}")
            s(f"mlp{f}_hid")

        block = ctx.enter_context(nc.Block())

        SUM = {"hyb": 0, "ff0": 1, "pw": 2, "lnvar": 3, "ff1": 4, "da": 5, "da_post": 6, "mlp0": 7, "mlp0_post": 8,
               "sc": 9, "sc_post": 10, "mlp1": 11, "mlp1_post": 12}
        PRE = {"hyb": 0, "ff0": 1, "pw": 2, "ff1": 3, "da": 4, "mlp0": 5, "sc": 6, "mlp1": 7}
        POST = {"da": 0, "mlp0": 1, "sc": 2, "mlp1": 3}

        @block.sync
        def _(sp):
            for name in CREDITED:
                sp.sem_inc(s(name), CREDIT)
            sp.dma_start(vec[:], vecs).then_inc(small_in[0], 16)
            for k in range(KB):
                sp.dma_start(h[:, k], x_t[k * P:(k + 1) * P, :]).then_inc(x_in[k], 16)
            sp.dma_start(A["wgr"][:], w_glr).then_inc(s("wglr_in"), 16)
            sp.dma_start(const[:], consts).then_inc(small_in[1], 16)
            sp.dma_start(A["wg2"][0:17, :], w_gate).then_inc(small_in[2], 16)
            for j in range(RING):
                sp.dma_start(raw[:, j], stream[j]).then_inc(loaded[j], 16)
            with sp.Fori(1, NT // RING) as r:
                for j in range(RING):
                    sp.wait_ge(wlo_ready, r * RING + (j + 1 - RING))
                    sp.dma_start(raw[:, j], stream[bass.ds(r * RING + j, 1)].rearrange("a p c -> (a p) c"))\
                      .then_inc(loaded[j], 16)
            for k in range(KB):
                sp.wait_ge(h_added, 8 * 3 + k + 1)
                sp.dma_start(out_t[k * P:(k + 1) * P, :], h[:, k]).then_inc(stored, 16)
            sp.wait_ge(stored, 16 * KB)

        @block.scalar
        def _(act):
            def split_hi(t):
                if t.n + LEAD >= NT:
                    return
                a = t.plus(LEAD)
                act.wait_ge(loaded[a.slot], a.loaded)
                if t.n:
                    act.wait_ge(tile_done, a.count - RING)
                act.activation(whi[:, a.slot], raw[:, a.slot], ACT.Copy).then_inc(whi_ready, 1)

            def square_block(name, k, src):
                q = SUM[name] * KB + k
                if q >= 2:
                    act.wait_ge(acc_ready, q - 1)
                act.activation(sq[:, k % 2], src, ACT.Square).then_inc(sq_ready, 1)

            def pre_block(name, k):
                act.activation(xh[:, k], h[:, k], ACT.Copy, scale=col("pre", 8 * PRE[name] + k)).then_inc(xh_ready, 1)
                square_block(name, k, h[:, k])

            def inv_rms(name, n):
                act.wait_ge(sum_ready, SUM[name] + 1)
                if SUM[name]:
                    act.wait_ge(rrow_ready, SUM[name])
                act.activation(lnb[:], ps[:, 4], ACT.Ln, scale=1.0 / n, bias=EPS).then_inc(ln_ready, 1)
                act.wait_ge(ln_ready, SUM[name] + 1)
                act.activation(rrow[:], lnb[:], ACT.Exp, scale=-0.5).then_inc(rrow_ready, 1)

            def inv_rms_col(n):
                act.wait_ge(colsum_ready, n)
                act.activation(lncol[:], ps[:, 5, 0:TB], ACT.Ln, scale=1.0 / D, bias=EPS).then_inc(lncol_ready, 1)
                act.wait_ge(lncol_ready, n)
                act.activation(rcol[:], lncol[:], ACT.Exp, scale=-0.5).then_inc(rcol_ready, 1)

            def down_tile(t, k, name):
                split_hi(t)
                if name:
                    act.wait_ge(evac_done, t.count)
                    pre_block(name, k)

            def post_stage(which, name):
                for k in range(KB):
                    act.wait_ge(h_added, 8 * POST[which] + k + 1)
                    pre_block(name, k)

            act.preload_act_table_set(LN_EXP)
            act.wait_ge(small_in[0], 16)
            for k in range(KB):
                act.wait_ge(x_in[k], 16)
                pre_block("hyb", k)
            act.wait_ge(s("wglr_in"), 16)
            act.activation(A["wgh"][:], A["wgr"][:], ACT.Copy).then_inc(s("wglr_hi"), 1)
            for j in range(LEAD):
                act.wait_ge(loaded[j], 16)
                act.activation(whi[:, j], raw[:, j], ACT.Copy).then_inc(whi_ready, 1)
            inv_rms("hyb", D)
            inv_rms_col(1)
            for n in (0, 1, 2, 3):
                split_hi(Tile(n))
            act.wait_ge(s("gate_x"), 1)
            act.activation(A["gt"][:], flat[:, 6 * 512:8 * 512], ACT.Abs).then_inc(s("gate_abs"), 1)
            act.wait_ge(s("gate_abs"), 1)
            act.activation(A["gt"][:], A["gt"][:], ACT.Exp, scale=-1.0).then_inc(s("gate_exp"), 1)
            act.wait_ge(s("gate_exp"), 1)
            act.activation(A["gt"][:], A["gt"][:], ACT.Ln, bias=1.0).then_inc(s("gate_ln"), 1)
            for n in range(T_GV, T_GR):
                split_hi(Tile(n))
            act.wait_ge(s("suf_ready"), 1)
            act.activation(A["gt"][:], flat[:, 4 * 512:6 * 512], ACT.Exp, scale=1.0 / 16).then_inc(s("kd_ready"), 1)
            act.activation(A["dec"][:], ps[:, 6, 0:16].rearrange("p (j n) -> p j n", j=2), ACT.Exp,
                           scale=1.0 / 16).then_inc(s("dec_ready"), 1)
            for j in range(4):
                split_hi(Tile(T_GR + j))
                act.wait_ge(evac_done, T_GR + j + 1)
                act.activation(A["sr"][:, j], A["sr"][:, j], ACT.Silu).then_inc(s("row0"), 1)
            for n in range(T_SV, T_SB):
                split_hi(Tile(n))
            for hh in range(GLA_HEADS):
                act.wait_ge(s("go_ready"), hh + 1)
                if hh >= 2:
                    act.wait_ge(s("gsum_ready"), hh - 1)
                act.activation(A["gt"][:, (hh % 2) * T:(hh % 2 + 1) * T], ps[:, hh], ACT.Square)\
                   .then_inc(s("gsq_ready"), 1)
            for hh in range(GLA_HEADS):
                act.wait_ge(s("gsum_ready"), hh + 1)
                if hh:
                    act.wait_ge(s("grr_ready"), hh)
                act.activation(lnb[:], ps[:, 4 + hh], ACT.Ln, scale=1.0 / P, bias=EPS).then_inc(s("gln_ready"), 1)
                act.wait_ge(s("gln_ready"), hh + 1)
                act.activation(A["S"][:, 2 * hh:2 * hh + 2].rearrange("p a j v -> p (a j v)"), lnb[:], ACT.Exp,
                               scale=-0.5).then_inc(s("grr_ready"), 1)
            for hh in range(GLA_HEADS):
                act.wait_ge(s("gy_ready"), hh + 1)
                act.activation(yh[:, hh], A["gv"][:, hh], ACT.Copy).then_inc(yh_ready, 1)

            with act.Fori(0, 2) as i:
                def square_qk(e, c):
                    n = 2 * e + c
                    split_hi(Tile(T_SB + n, i))
                    act.wait_ge(evac_done, i * 4 + (T_SB + n + 1))
                    act.activation(A["ssq"][:, c], A["sraw"][:, e, c], ACT.Square).then_inc(s("sb_sq"), 1)

                def rms_qk(e, c):
                    n = 2 * e + c
                    act.wait_ge(s("sb_sum"), i * 4 + (n + 1))
                    act.wait_ge(s("sb_rr"), i * 4 + n + CREDIT)
                    act.activation(lnb[:], ps[:, c], ACT.Ln, scale=1.0 / 64, bias=EPS).then_inc(s("sb_ln"), 1)
                    act.wait_ge(s("sb_ln"), i * 4 + (n + 1))
                    if c == 0:
                        act.wait_ge(s("sb_qn"), i * 4 + n + CREDIT)
                    act.activation(A["srr"][:, c], lnb[:], ACT.Exp, scale=-0.5,
                                   bias=float(-np.log(8.0)) if c == 0 else 0.0).then_inc(s("sb_rr"), 1)

                def soft(e, hh):
                    n, b = 2 * e + hh, 2 + 3 * hh
                    act.wait_ge(s("sb_z"), i * 4 + (n + 1))
                    act.activation(A["sl"][:, hh], flat[:, b * 512:b * 512 + 1280], ACT.Abs).then_inc(s("sb_abs"), 1)
                    act.wait_ge(s("sb_abs"), i * 4 + (n + 1))
                    act.activation(A["sl"][:, hh], A["sl"][:, hh], ACT.Exp, scale=-1.0).then_inc(s("sb_exp"), 1)
                    act.wait_ge(s("sb_exp"), i * 4 + (n + 1))
                    act.activation(A["sl"][:, hh], A["sl"][:, hh], ACT.Ln, bias=1.0).then_inc(s("sb_ln2"), 1)

                def weights(e, hh):
                    n, b = 2 * e + hh, 2 + 3 * hh
                    act.wait_ge(s("sb_acc"), i * 4 + (n + 1))
                    act.activation(A["sl"][:, hh], flat[:, b * 512:b * 512 + 1280], ACT.Exp).then_inc(s("sb_w"), 1)

                def out_hi(e, hh):
                    n, b, r = 2 * e + hh, 2 + 3 * hh, slice(64 * hh, 64 * hh + 64)
                    act.wait_ge(s("sb_o"), i * 4 + (n + 1) + CREDIT)
                    act.activation(yh[r, bass.ds(i * 2 + (4 + e), 1)].rearrange("p a t -> p (a t)"), ps[r, b],
                                   ACT.Copy).then_inc(s("sb_yh"), 1)

                square_qk(0, 0)
                square_qk(0, 1)
                rms_qk(0, 0)
                rms_qk(0, 1)
                soft(0, 0)
                square_qk(1, 0)
                soft(0, 1)
                square_qk(1, 1)
                weights(0, 0)
                weights(0, 1)
                rms_qk(1, 0)
                rms_qk(1, 1)
                out_hi(0, 0)
                out_hi(0, 1)
                soft(1, 0)
                soft(1, 1)
                weights(1, 0)
                weights(1, 1)
                out_hi(1, 0)
                out_hi(1, 1)

            for k in range(KB):
                down_tile(Tile(T_WO + k), k, "ff0")

            def swiglu(f, t0, following):
                name = f"ff{f}"
                inv_rms(name, D)

                def up(g, i, q0):
                    for u in (0, 1):
                        tg = Tile(t0 + 2 * u, g * 6 + i)
                        split_hi(tg)
                        act.wait_ge(evac_done, tg.count)
                        act.activation(A["ts"][:, u], A["tg"][:, u], ACT.Silu).then_inc(s(name + "_silu"), 1)
                        split_hi(tg.plus(1))
                        done = g * 8 + i * 2 + (u + 1)
                        act.wait_ge(s(name + "_hid"), done)
                        act.activation(yh[:, bass.ds(i * 2 + u, 1)].rearrange("p a t -> p (a t)"), A["th"][:, u],
                                       ACT.Copy).then_inc(yh_ready, 1)

                with act.Fori(0, 2) as g:
                    with act.Fori(0, 4) as i:
                        up(g, i, 0)
                    for k in range(KB):
                        split_hi(Tile(t0 + 16 + k, g * 6))
                with act.Fori(0, 3) as i:
                    up(2, i, 16)
                for k in range(KB):
                    down_tile(Tile(t0 + 60 + k), k, following)

            swiglu(0, T_FF0, "pw")

            inv_rms("pw", D)
            with act.Fori(0, 4) as i:
                for u in (0, 1):
                    split_hi(Tile(T_PW1 + 2 * u, i))
                    t = Tile(T_PW1 + 2 * u + 1, i)
                    split_hi(t)
                    act.wait_ge(evac_done, t.count)
                    act.activation(A["t3"][:, u], A["t2"][:, u], ACT.Sigmoid,
                                   bias=vec[:, bass.ds(i * 2 + (_cols["b_pw1"] + 8 + u), 1)]).then_inc(s("pw_sg"), 1)
            for k in range(KB):
                act.wait_ge(s("cen_ready"), k + 1)
                square_block("lnvar", k, A["cv"][:, k])
            inv_rms("lnvar", D)
            for k in range(KB):
                act.wait_ge(s("ln_t"), k + 1)
                if k >= 2:
                    act.wait_ge(y_ready, Y0["pw"] + k - 1)
                act.activation(A["t2"][:, k % 2], A["t1"][:, k % 2], ACT.Silu, bias=col("ln_b", k))\
                   .then_inc(s("ln_s"), 1)
                act.wait_ge(s("ln_s"), k + 1)
                act.activation(yh[:, k], A["t2"][:, k % 2], ACT.Copy).then_inc(yh_ready, 1)
            for k in range(KB):
                down_tile(Tile(T_PW2 + k), k, "ff1")

            swiglu(1, T_FF1, "da")

            inv_rms("da", D)
            inv_rms_col(2)
            act.wait_ge(s("lam_s"), 1)
            act.activation(lamt[:, 1], ps[:, 6, 0:2], ACT.Exp).then_inc(s("lam_e"), 1)
            with act.Fori(0, 2) as r:
                for j in range(4):
                    split_hi(Tile(T_DV + j, r))
            with act.Fori(0, 4) as i:
                def exps(e, u):
                    n, p, kv = 4 * e + u, u % 2, (u + 1) * P
                    act.wait_ge(s("da_max"), i * 8 + (n + 1))
                    for c in (0, 1):
                        act.activation(A["ex"][:, p, c, 0:kv], ps[:, 2 + 2 * p + c, 0:kv], ACT.Exp,
                                       bias=A["nm"][:, p, c:c + 1], accum_out=A["sm"][:, p, c:c + 1])\
                           .then_inc(s("da_exp"), 1)

                def copy_T(e, u):
                    n, kv, at = 4 * e + u, (u + 1) * P, P * u * (u + 1) // 2
                    act.wait_ge(s("da_T"), i * 8 + (n + 1))
                    act.activation(A["aT"][:, at:at + kv], ps[:, 6, 0:kv], ACT.Copy).then_inc(s("da_aT"), 1)

                def out(e):
                    done = i * 2 + (e + 1)
                    act.wait_ge(s("da_o"), done + CREDIT)
                    act.activation(sq[:, 0], ps[:, 7], ACT.Square).then_inc(s("da_sq"), 1)
                    act.wait_ge(s("da_sum"), done)
                    act.activation(lnb[:], ps[:, 6], ACT.Ln, scale=1.0 / P, bias=EPS).then_inc(s("da_ln"), 1)
                    act.wait_ge(s("da_ln"), done)
                    act.activation(lnb[:], lnb[:], ACT.Exp, scale=-0.5).then_inc(s("da_rr"), 1)
                    act.wait_ge(s("da_ot"), done + CREDIT)
                    act.activation(yh[:, bass.ds(i * 2 + e, 1)].rearrange("p a t -> p (a t)"), A["dot"][:],
                                   ACT.Copy, scale=1.0 - LAMBDA_INIT).then_inc(yh_ready, 1)

                split_hi(Tile(T_DA, i))
                split_hi(Tile(T_DA + 1, i))
                exps(0, 0)
                exps(0, 1)
                split_hi(Tile(T_DA + 2, i))
                copy_T(0, 0)
                exps(0, 2)
                copy_T(0, 1)
                exps(0, 3)
                split_hi(Tile(T_DA + 3, i))
                copy_T(0, 2)
                copy_T(0, 3)
                out(0)
                exps(1, 0)
                exps(1, 1)
                copy_T(1, 0)
                exps(1, 2)
                copy_T(1, 1)
                exps(1, 3)
                copy_T(1, 2)
                copy_T(1, 3)
                out(1)

            def to_m(t0, which, k0=0):
                for k in range(KB):
                    t = Tile(t0 + k)
                    split_hi(t)
                    act.wait_ge(evac_done, t.count)
                    square_block(which + "_post", k, A["m"][:, k])
                inv_rms(which + "_post", D)

            to_m(T_DO, "da")
            post_stage("da", "mlp0")

            def mlp(f, t0):
                name = f"mlp{f}"
                inv_rms(name, D)

                def up(g, i):
                    for j in range(4):
                        t = Tile(t0 + j, g * 4 + i)
                        split_hi(t)
                        act.wait_ge(evac_done, t.count)
                        act.activation(yh[:, bass.ds(i * 4 + j, 1)].rearrange("p a t -> p (a t)"), A["mr"][:, j % 2],
                                       ACT.Square).then_inc(yh_ready, 1)

                with act.Fori(0, MLP_GROUPS - 1) as g:
                    with act.Fori(0, 2) as i:
                        up(g, i)
                    with act.Fori(0, 2) as i:
                        for j in range(4):
                            split_hi(Tile(t0 + 8 + j, g * 4 + i))
                with act.Fori(0, 2) as i:
                    up(MLP_GROUPS - 1, i)
                to_m(t0 + 56, name)

            mlp(0, T_MLP0)
            post_stage("mlp0", "sc")

            inv_rms("sc", D)
            with act.Fori(0, 2) as i:
                for u in range(4):
                    for c in range(3):
                        split_hi(Tile(T_SC + 3 * u + c, i * 3))
                    act.wait_ge(s("sc_y"), i * 4 + (u + 1))
                    act.activation(yh[:, bass.ds(i * 4 + u, 1)].rearrange("p a t -> p (a t)"), A["cy"][:, u % 2],
                                   ACT.Copy).then_inc(yh_ready, 1)
            to_m(T_SCO, "sc")
            post_stage("sc", "mlp1")
            mlp(1, T_MLP1)

        @block.vector
        def _(dve):
            def split_lo(t):
                if t.n + LEAD >= NT:
                    return
                a = t.plus(LEAD)
                dve.wait_ge(whi_ready, a.count)
                dve.tensor_tensor(wlo[:, a.slot], raw[:, a.slot], whi[:, a.slot].bitcast(F32), ALU.subtract)\
                   .then_inc(wlo_ready, 1)

            def pre_lo(name, k):
                dve.wait_ge(xh_ready, 8 * PRE[name] + k + 1)
                dve.scalar_tensor_tensor(xl[:, k], h[:, k], col("pre", 8 * PRE[name] + k), xh[:, k].bitcast(F32),
                                         ALU.mult, ALU.subtract).then_inc(x_ready, 1)

            def scaled(dst, t, bank):
                dve.wait_ge(tile_done, t.count)
                dve.tensor_tensor(dst, ps[:, bank], rrow[:], ALU.mult).then_inc(evac_done, 1)

            def post_norm(which):
                a = POST[which]
                following = {"da": "mlp0", "mlp0": "sc", "sc": "mlp1"}.get(which)
                dve.wait_ge(rrow_ready, SUM[which + "_post"] + 1)
                for k in range(KB):
                    q = 8 * a + k
                    if q >= 2:
                        dve.wait_ge(h_added, q - 1)
                    dve.scalar_tensor_tensor(A["pt"][:, k % 2], A["m"][:, k], col("post", q), rrow[:], ALU.mult,
                                             ALU.mult).then_inc(post_t, 1)
                    if following and k:
                        pre_lo(following, k - 1)
                if following:
                    pre_lo(following, KB - 1)

            dve.memset(A["glr"][0:32, :], 1.0).then_inc(s("glr_evac"), 1)
            dve.wait_ge(small_in[0], 16)
            for k in range(KB):
                pre_lo("hyb", k)
            dve.wait_ge(s("wglr_hi"), 1)
            dve.tensor_tensor(A["wgl"][:], A["wgr"][:], A["wgh"][:].bitcast(F32), ALU.subtract)\
               .then_inc(s("wglr_lo"), 1)
            for j in range(LEAD):
                dve.wait_ge(whi_ready, j + 1)
                dve.tensor_tensor(wlo[:, j], raw[:, j], whi[:, j].bitcast(F32), ALU.subtract).then_inc(wlo_ready, 1)
            dve.wait_ge(rrow_ready, 1)
            dve.wait_ge(s("glr_done"), 1)
            dve.wait_ge(s("glr_evac"), 1)
            dve.tensor_tensor(A["glr"][0:16, :], ps[0:16, 6], rrow[0:16, :], ALU.mult).then_inc(s("glr_evac"), 1)
            split_lo(Tile(0))
            split_lo(Tile(1))
            dve.wait_ge(rcol_ready, 1)
            dve.wait_ge(tile_done, 2)
            for t in range(TB):
                last = dve.tensor_scalar(A["gk"][:, t], ps[:, t, 0:256], rcol[:, t:t + 1], None, ALU.mult)
                if t % 2:
                    last.then_inc(evac_done, 1)
            for j in range(2):
                split_lo(Tile(T_GQ + j))
                dve.wait_ge(tile_done, T_GQ + j + 1)
                dve.scalar_tensor_tensor(A["gq"][:, j], ps[:, 2 + j], 64 ** -0.5, rrow[:], ALU.mult, ALU.mult)\
                   .then_inc(evac_done, 1)
            for n in range(T_GV, T_GR):
                split_lo(Tile(n))
            dve.wait_ge(s("gate_ln"), 1)
            dve.scalar_tensor_tensor(A["la"][:].rearrange("p t k -> p (t k)"), flat[:, 6 * 512:8 * 512], 0.0,
                                     A["gt"][:], ALU.min, ALU.subtract).then_inc(s("la_ready"), 1)
            dve.wait_ge(tile_done, T_GR)
            for t in range(TB):
                dve.tensor_scalar(A["gv"][:, t], ps[:, t], rcol[:, t:t + 1], None, ALU.mult).then_inc(evac_done, 1)
            dve.wait_ge(s("kd_ready"), 1)
            gkf = A["gk"][:].rearrange("p t k -> p (t k)")
            dve.tensor_tensor(gkf, gkf, A["gt"][:], ALU.mult).then_inc(s("kend_ready"), 1)
            for j in range(4):
                split_lo(Tile(T_GR + j))
                scaled(A["sr"][:, j], Tile(T_GR + j), j)
            for n in range(T_SV, T_SB):
                split_lo(Tile(n))
            dve.wait_ge(s("dec_ready"), 1)
            for n in range(8):
                if n % 2 == 0:
                    dve.wait_ge(s("upd_ready"), n // 2 + 1)
                for j in range(2):
                    u = 2 * (n // 2) + j
                    upd = ps[:, 4 + 2 * (n % 2) + u // 4, (u % 4) * P:(u % 4 + 1) * P]
                    if n == 0:
                        dve.tensor_copy(A["S"][:, n, j], upd).then_inc(s("state_ready"), 1)
                    else:
                        dve.wait_ge(s("state_ready"), 2 * (n - 1) + j + 1)
                        dve.scalar_tensor_tensor(A["S"][:, n, j], A["S"][:, n - 1, j], A["dec"][:, j, n:n + 1], upd,
                                                 ALU.mult, ALU.add).then_inc(s("state_ready"), 1)
            dve.wait_ge(tile_done, T_SB)
            for t in range(TB):
                dve.tensor_scalar(A["sv"][:, t], ps[:, t], rcol[:, t:t + 1], None, ALU.mult).then_inc(evac_done, 1)
            for hh in range(GLA_HEADS):
                dve.wait_ge(s("grr_ready"), hh + 1)
                dve.scalar_tensor_tensor(A["gv"][:, hh], ps[:, hh], col("gla"),
                                         A["S"][:, 2 * hh:2 * hh + 2].rearrange("p a j v -> p (a j v)"), ALU.mult,
                                         ALU.mult).then_inc(s("gt_ready"), 1)
                dve.wait_ge(s("gt_ready"), hh + 1)
                dve.wait_ge(s("row0"), 4)
                dve.tensor_tensor(A["gv"][:, hh], A["gv"][:, hh], A["sr"][:, hh], ALU.mult).then_inc(s("gy_ready"), 1)
            for hh in range(GLA_HEADS):
                dve.wait_ge(yh_ready, hh + 1)
                dve.wait_ge(s("gy_ready"), hh + 1)
                dve.tensor_tensor(yl[:, hh], A["gv"][:, hh], yh[:, hh].bitcast(F32), ALU.subtract).then_inc(y_ready, 1)

            with dve.Fori(0, 2) as i:
                def take(e, c):
                    n = 2 * e + c
                    split_lo(Tile(T_SB + n, i))
                    scaled(A["sraw"][:, e, c], Tile(T_SB + n, i), c)

                def norm_qk(e, c):
                    n = 2 * e + c
                    dve.wait_ge(s("sb_rr"), i * 4 + (n + 1) + CREDIT)
                    dve.wait_ge(evac_done, i * 4 + (T_SB + n + 1))
                    dve.scalar_tensor_tensor(A["sqn"][:, e, c], A["sraw"][:, e, c], col("sbk" if c else "sbq"),
                                             A["srr"][:, c], ALU.mult, ALU.mult).then_inc(s("sb_qn"), 1)

                def softplus(e, hh):
                    n, b = 2 * e + hh, 2 + 3 * hh
                    dve.wait_ge(s("sb_ln2"), i * 4 + (n + 1))
                    dve.scalar_tensor_tensor(A["sp"][:, hh], flat[:, b * 512:b * 512 + 1280], 0.0, A["sl"][:, hh],
                                             ALU.max, ALU.add).then_inc(s("sb_sp"), 1)

                def out_lo(e, hh):
                    n, b, r = 2 * e + hh, 2 + 3 * hh, slice(64 * hh, 64 * hh + 64)
                    dve.wait_ge(s("sb_yh"), i * 4 + (n + 1))
                    at = bass.ds(i * 2 + (4 + e), 1)
                    dve.tensor_tensor(yl[r, at].rearrange("p a t -> p (a t)"), ps[r, b],
                                      yh[r, at].rearrange("p a t -> p (a t)").bitcast(F32), ALU.subtract)\
                       .then_inc(s("sb_yl"), 1)

                take(0, 0)
                take(0, 1)
                norm_qk(0, 0)
                norm_qk(0, 1)
                take(1, 0)
                softplus(0, 0)
                take(1, 1)
                softplus(0, 1)
                norm_qk(1, 0)
                norm_qk(1, 1)
                out_lo(0, 0)
                out_lo(0, 1)
                softplus(1, 0)
                softplus(1, 1)
                out_lo(1, 0)
                out_lo(1, 1)

            def add_to_h(t, k, following, bias=None):
                split_lo(t)
                dve.wait_ge(tile_done, t.count)
                if bias:
                    dve.scalar_tensor_tensor(h[:, k], ps[:, t.slot], col(bias, k), h[:, k], ALU.add, ALU.add)\
                       .then_inc(evac_done, 1)
                else:
                    dve.tensor_tensor(h[:, k], ps[:, t.slot], h[:, k], ALU.add).then_inc(evac_done, 1)
                if following:
                    dve.wait_ge(evac_done, t.count)
                    pre_lo(following, k)

            for k in range(KB):
                add_to_h(Tile(T_WO + k), k, "ff0")

            def swiglu(f, t0, following):
                name = f"ff{f}"
                dve.wait_ge(rrow_ready, SUM[name] + 1)

                def up(g, i):
                    for u in (0, 1):
                        tg = Tile(t0 + 2 * u, g * 6 + i)
                        tu = tg.plus(1)
                        split_lo(tg)
                        scaled(A["tg"][:, u], tg, tg.slot)
                        split_lo(tu)
                        scaled(A["tu"][:, u], tu, tu.slot)
                        done = g * 8 + i * 2 + (u + 1)
                        dve.wait_ge(s(name + "_silu"), done)
                        dve.wait_ge(evac_done, tu.count)
                        dve.tensor_tensor(A["th"][:, u], A["ts"][:, u], A["tu"][:, u], ALU.mult)\
                           .then_inc(s(name + "_hid"), 1)
                        dve.wait_ge(yh_ready, g * 8 + i * 2 + (yh0 + u + 1))
                        at = bass.ds(i * 2 + u, 1)
                        dve.wait_ge(s(name + "_hid"), done)
                        dve.tensor_tensor(yl[:, at].rearrange("p a t -> p (a t)"), A["th"][:, u],
                                          yh[:, at].rearrange("p a t -> p (a t)").bitcast(F32), ALU.subtract)\
                           .then_inc(y_ready, 1)

                yh0 = Y0[name]
                with dve.Fori(0, 2) as g:
                    with dve.Fori(0, 4) as i:
                        up(g, i)
                    for k in range(KB):
                        add_to_h(Tile(t0 + 16 + k, g * 6), k, None)
                with dve.Fori(0, 3) as i:
                    up(2, i)
                for k in range(KB):
                    add_to_h(Tile(t0 + 60 + k), k, following)

            swiglu(0, T_FF0, "pw")

            dve.memset(A["ub"][:, :, 0:PAD], 0.0).then_inc(s("pw_zero"), 1)
            dve.wait_ge(rrow_ready, SUM["pw"] + 1)
            own = TAPS - TAPS_PE
            with dve.Fori(0, 4) as i:
                for u in (0, 1):
                    ta = Tile(T_PW1 + 2 * u, i)
                    split_lo(ta)
                    scaled(A["t1"][:, u], ta, ta.slot)
                    split_lo(ta.plus(1))
                    scaled(A["t2"][:, u], ta.plus(1), ta.slot + 1)
                    done = i * 2 + (u + 1)
                    dve.wait_ge(s("pw_sg"), done)
                    dve.wait_ge(evac_done, ta.count)
                    dve.wait_ge(s("pw_zero"), 1)
                    dve.scalar_tensor_tensor(A["ub"][:, u, PAD:], A["t1"][:, u],
                                             vec[:, bass.ds(i * 2 + (_cols["b_pw1"] + u), 1)], A["t3"][:, u],
                                             ALU.add, ALU.mult).then_inc(s("pw_u"), 1)
                    dve.wait_ge(s("pw_u"), done)
                    cvb = A["cv"][:, bass.ds(i * 2 + u, 1)].rearrange("p a t -> p (a t)")

                    def tap(k):
                        return vec[:, bass.ds(i * (2 * TAPS) + (_cols["w_dw"] + u * TAPS + k), 1)]

                    dve.tensor_scalar(cvb, A["ub"][:, u, TAPS_PE:TAPS_PE + T], tap(TAPS_PE),
                                      vec[:, bass.ds(i * 2 + (_cols["b_dw"] + u), 1)], ALU.mult, ALU.add)\
                       .then_inc(s("cv_chain"), 1)
                    for n in range(1, own):
                        k = TAPS_PE + n
                        dve.wait_ge(s("cv_chain"), i * (2 * own) + (u * own + n))
                        dve.scalar_tensor_tensor(cvb, A["ub"][:, u, k:k + T], tap(k), cvb, ALU.mult, ALU.add)\
                           .then_inc(s("cv_chain"), 1)
                    dve.wait_ge(s("cv_chain"), i * (2 * own) + (u * own + own))
                    dve.wait_ge(s("cv_pe"), done + CREDIT)
                    dve.tensor_tensor(cvb, ps[:, 5 + u], cvb, ALU.add).then_inc(s("cv_done"), 1)
            dve.wait_ge(s("mu_sum"), 1)
            dve.wait_ge(s("cv_done"), KB)
            dve.tensor_scalar(A["mu"][:], ps[:, 7], 1.0 / D, None, ALU.mult).then_inc(s("mu_copied"), 1)
            dve.wait_ge(s("mu_copied"), 1)
            for k in range(KB):
                dve.tensor_tensor(A["cv"][:, k], A["cv"][:, k], A["mu"][:], ALU.subtract).then_inc(s("cen_ready"), 1)
            dve.wait_ge(rrow_ready, SUM["lnvar"] + 1)

            def ln_lo(k):
                dve.wait_ge(yh_ready, Y0["pw"] + k + 1)
                dve.tensor_tensor(yl[:, k], A["t2"][:, k % 2], yh[:, k].bitcast(F32), ALU.subtract).then_inc(y_ready, 1)

            for k in range(KB):
                dve.wait_ge(s("cen_ready"), k + 1)
                if k >= 2:
                    dve.wait_ge(s("ln_s"), k - 1)
                dve.scalar_tensor_tensor(A["t1"][:, k % 2], A["cv"][:, k], col("ln_g", k), rrow[:], ALU.mult,
                                         ALU.mult).then_inc(s("ln_t"), 1)
                if k:
                    ln_lo(k - 1)
            ln_lo(KB - 1)
            for k in range(KB):
                add_to_h(Tile(T_PW2 + k), k, "ff1", "b_pw2")

            swiglu(1, T_FF1, "da")

            a = _cols["lam"]
            dve.tensor_tensor(lamt[:, 0], vec[:, a:a + 4:2], vec[:, a + 1:a + 4:2], ALU.mult).then_inc(s("lam_p"), 1)
            dve.wait_ge(s("lam_e"), 1)
            dve.scalar_tensor_tensor(nlam[:], lamt[:, 1, 1:2], -LAMBDA_INIT, lamt[:, 1, 0:1], ALU.add, ALU.subtract)\
               .then_inc(s("lam_ready"), 1)
            dve.wait_ge(rrow_ready, SUM["da"] + 1)
            dve.wait_ge(rcol_ready, 2)
            with dve.Fori(0, 2) as r:
                for j in range(4):
                    split_lo(Tile(T_DV + j, r))
                dve.wait_ge(tile_done, r * 4 + (T_DV + 4))
                for t in range(TB):
                    dve.tensor_scalar(A["dv"][:, t, bass.ds(r * 512, 512)], ps[:, t], rcol[:, t:t + 1], None, ALU.mult)\
                       .then_inc(evac_done, 1)
            swap = [d ^ 8 if d < 16 else d for d in range(32)]
            with dve.Fori(0, 4) as i:
                def rope(e, c):
                    n = 2 * e + c
                    t, done = Tile(T_DA + n, i), i * 4 + (n + 1)
                    split_lo(t)
                    dve.wait_ge(tile_done, t.count)
                    dve.wait_ge(s("da_qn"), i * 4 + max(n - 1, 0) + CREDIT)
                    dve.scalar_tensor_tensor(A["draw"][:, c], ps[:, c], 1.0 if c else 64 ** -0.5, rrow[:], ALU.mult,
                                             ALU.mult).then_inc(evac_done, 1)
                    dve.wait_ge(s("lam_ready"), 1)
                    dve.wait_ge(evac_done, t.count)
                    dve.stream_shuffle(A["dsh"][:, c], A["draw"][:, c], swap).then_inc(s("da_sh"), 1)
                    dve.wait_ge(s("da_sh"), done)
                    dve.tensor_tensor(A["dsh"][:, c], A["dsh"][:, c], cst("sin"), ALU.mult).then_inc(s("da_shs"), 1)

                def row_max(e, u):
                    n, p, kv = 4 * e + u, u % 2, (u + 1) * P
                    dve.wait_ge(s("da_s"), i * 8 + (n + 1))
                    dve.reduce_max(A["nm"][:, p], ps[:, 2 + 2 * p:4 + 2 * p, 0:kv], AX.X, negate=True)\
                       .then_inc(s("da_max"), 1)

                def combine(e, u):
                    n, p, kv = 4 * e + u, u % 2, (u + 1) * P
                    done = i * 8 + (n + 1)
                    dve.wait_ge(s("da_exp"), i * 16 + 2 * (n + 1) + CREDIT)
                    dve.reciprocal(A["rc"][:, p], A["sm"][:, p]).then_inc(s("da_rcp"), 1)
                    dve.wait_ge(s("da_rcp"), done)
                    dve.tensor_tensor(A["r1"][:, p], A["rc"][:, p, 1:2], nlam[:], ALU.mult).then_inc(s("da_r1"), 1)
                    dve.wait_ge(s("da_r1"), done)
                    dve.tensor_scalar(acc[:, 0:kv], A["ex"][:, p, 1, 0:kv], A["r1"][:, p], None, ALU.mult)\
                       .then_inc(s("da_t"), 1)
                    dve.wait_ge(s("da_t"), done)
                    dve.scalar_tensor_tensor(A["da"][:, p, 0:kv], A["ex"][:, p, 0, 0:kv], A["rc"][:, p, 0:1],
                                             acc[:, 0:kv], ALU.mult, ALU.add).then_inc(s("da_a"), 1)

                def out(e):
                    done = i * 2 + (e + 1)
                    dve.wait_ge(s("da_rr"), done + CREDIT)
                    dve.scalar_tensor_tensor(A["dot"][:], ps[:, 7], col("subln"), lnb[:], ALU.mult, ALU.mult)\
                       .then_inc(s("da_ot"), 1)
                    dve.wait_ge(s("da_ot"), done + CREDIT)
                    dve.wait_ge(yh_ready, i * 2 + (Y0["da"] + e + 1))
                    at = bass.ds(i * 2 + e, 1)
                    dve.scalar_tensor_tensor(yl[:, at].rearrange("p a t -> p (a t)"), A["dot"][:], 1.0 - LAMBDA_INIT,
                                             yh[:, at].rearrange("p a t -> p (a t)").bitcast(F32), ALU.mult,
                                             ALU.subtract).then_inc(y_ready, 1)

                dve.wait_ge(s("lam_ready"), 1)
                rope(0, 0)
                rope(0, 1)
                row_max(0, 0)
                row_max(0, 1)
                combine(0, 0)
                rope(1, 0)
                row_max(0, 2)
                combine(0, 1)
                row_max(0, 3)
                combine(0, 2)
                rope(1, 1)
                combine(0, 3)
                out(0)
                row_max(1, 0)
                row_max(1, 1)
                combine(1, 0)
                row_max(1, 2)
                combine(1, 1)
                row_max(1, 3)
                combine(1, 2)
                combine(1, 3)
                out(1)

            def add_to_m(t, k):
                split_lo(t)
                dve.wait_ge(tile_done, t.count)
                dve.tensor_tensor(A["m"][:, k] if isinstance(k, int) else A["m"][:, k].rearrange("p a t -> p (a t)"),
                                  ps[:, t.slot],
                                  A["m"][:, k] if isinstance(k, int) else A["m"][:, k].rearrange("p a t -> p (a t)"),
                                  ALU.add).then_inc(evac_done, 1)

            def set_m(t, k):
                split_lo(t)
                dve.wait_ge(tile_done, t.count)
                dve.tensor_copy(A["m"][:, k], ps[:, t.slot]).then_inc(evac_done, 1)

            for k in range(KB):
                set_m(Tile(T_DO + k), k)
            post_norm("da")

            def mlp(f, t0):
                name = f"mlp{f}"
                yh0 = Y0[name]
                dve.memset(A["m"][:], 0.0).then_inc(s("m_zero"), 1)
                dve.wait_ge(rrow_ready, SUM[name] + 1)

                def up(g, i):
                    for j in range(4):
                        t = Tile(t0 + j, g * 4 + i)
                        split_lo(t)
                        dve.wait_ge(tile_done, t.count)
                        dve.scalar_tensor_tensor(A["mr"][:, j % 2], ps[:, t.slot], 0.0, rrow[:], ALU.max, ALU.mult)\
                           .then_inc(evac_done, 1)
                        dve.wait_ge(evac_done, t.count)
                        dve.tensor_tensor(A["mh"][:, j % 2], A["mr"][:, j % 2], A["mr"][:, j % 2], ALU.mult)\
                           .then_inc(s(name + "_hid"), 1)
                        done = g * 8 + i * 4 + (j + 1)
                        dve.wait_ge(s(name + "_hid"), done)
                        dve.wait_ge(yh_ready, g * 8 + i * 4 + (yh0 + j + 1))
                        at = bass.ds(i * 4 + j, 1)
                        dve.tensor_tensor(yl[:, at].rearrange("p a t -> p (a t)"), A["mh"][:, j % 2],
                                          yh[:, at].rearrange("p a t -> p (a t)").bitcast(F32), ALU.subtract)\
                           .then_inc(y_ready, 1)

                with dve.Fori(0, MLP_GROUPS - 1) as g:
                    with dve.Fori(0, 2) as i:
                        up(g, i)
                    dve.wait_ge(s("m_zero"), f + 1)
                    with dve.Fori(0, 2) as i:
                        for j in range(4):
                            add_to_m(Tile(t0 + 8 + j, g * 4 + i), bass.ds(i * 4 + j, 1))
                with dve.Fori(0, 2) as i:
                    up(MLP_GROUPS - 1, i)
                for k in range(KB):
                    add_to_m(Tile(t0 + 56 + k), k)
                post_norm(name)

            mlp(0, T_MLP0)

            dve.memset(A["uc"][:, :, 0:2], 0.0).then_inc(s("sc_zero"), 1)
            dve.wait_ge(rrow_ready, SUM["sc"] + 1)
            with dve.Fori(0, 2) as i:
                for u in range(4):
                    for c, dst in enumerate(("cb", "cc", "cx")):
                        t = Tile(T_SC + 3 * u + c, i * 3)
                        split_lo(t)
                        scaled(A[dst][:, u % 2], t, t.slot)
                    dve.wait_ge(evac_done, t.count)
                    dve.wait_ge(s("sc_zero"), 1)
                    uc, cy = A["uc"][:, u % 2], A["cy"][:, u % 2]
                    at = i * 16 + 4 * u
                    dve.tensor_tensor(uc[:, 2:], A["cc"][:, u % 2], A["cx"][:, u % 2], ALU.mult).then_inc(s("sc_u"), 1)
                    for k in range(3):
                        dve.wait_ge(s("sc_u"), at + (k + 1))
                        w = vec[:, bass.ds(i * 12 + (_cols["conv_w"] + 3 * u + k), 1)]
                        if k == 0:
                            dve.tensor_scalar(cy, uc[:, 0:T], w, None, ALU.mult).then_inc(s("sc_u"), 1)
                        else:
                            dve.scalar_tensor_tensor(cy, uc[:, k:k + T], w, cy, ALU.mult, ALU.add)\
                               .then_inc(s("sc_u"), 1)
                    dve.wait_ge(s("sc_u"), at + 4)
                    dve.tensor_tensor(cy, cy, A["cb"][:, u % 2], ALU.mult).then_inc(s("sc_y"), 1)
                    dve.wait_ge(yh_ready, i * 4 + (Y0["sc"] + u + 1))
                    dve.wait_ge(s("sc_y"), i * 4 + (u + 1))
                    yat = bass.ds(i * 4 + u, 1)
                    dve.tensor_tensor(yl[:, yat].rearrange("p a t -> p (a t)"), cy,
                                      yh[:, yat].rearrange("p a t -> p (a t)").bitcast(F32), ALU.subtract)\
                       .then_inc(y_ready, 1)
            for k in range(KB):
                set_m(Tile(T_SCO + k), k)
            post_norm("sc")
            mlp(1, T_MLP1)

        @block.gpsimd
        def _(pool):
            def sum_squares(name):
                for k in range(KB):
                    sum_block(name, k)

            def sum_block(name, k):
                q = SUM[name] * KB + k
                pool.wait_ge(sq_ready, q + 1)
                if k == 0:
                    if SUM[name]:
                        pool.wait_ge(sum_ready, SUM[name])
                        pool.wait_ge(acc_ready, q)
                    pool.tensor_copy(acc[:], sq[:, 0]).then_inc(acc_ready, 1)
                else:
                    pool.wait_ge(acc_ready, q)
                    pool.tensor_tensor(acc[:], acc[:], sq[:, k % 2], ALU.add).then_inc(acc_ready, 1)

            def post_stage(which):
                following = {"da": "mlp0", "mlp0": "sc", "sc": "mlp1"}.get(which)
                for k in range(KB):
                    pool.wait_ge(post_t, 8 * POST[which] + k + 1)
                    pool.tensor_tensor(h[:, k], h[:, k], A["pt"][:, k % 2], ALU.add).then_inc(h_added, 1)
                    if following and k:
                        sum_block(following, k - 1)
                if following:
                    sum_block(following, KB - 1)

            sum_squares("hyb")
            with pool.Fori(0, 2) as i:
                def stage(e):
                    if e == 0:
                        pool.wait_ge(s("sb_o"), i * 4 + CREDIT)
                    else:
                        pool.wait_ge(s("sb_o"), i * 4 + 1 + CREDIT)
                    pool.wait_ge(evac_done, T_SB)
                    pool.wait_ge(y_ready, GLA_HEADS)
                    pool.tensor_copy(A["vp"][:, e], A["sv"][:, :, bass.ds(i * 256 + e * 128, P)]).then_inc(s("sb_vp"), 1)

                def mask(e, hh):
                    n = 2 * e + hh
                    pool.wait_ge(s("sb_sp"), i * 4 + (n + 1))
                    for r in (0, 512, 896, 1024):
                        last = pool.tensor_tensor(A["sp"][:, hh, r:r + P], A["sp"][:, hh, r:r + P], cst("mask_sb"),
                                                  ALU.mult)
                    last.then_inc(s("sb_mask"), 1)

                stage(0)
                mask(0, 0)
                mask(0, 1)
                stage(1)
                mask(1, 0)
                mask(1, 1)
            sum_squares("ff0")
            sum_squares("pw")
            with pool.Fori(0, 4) as i:
                for u in (0, 1):
                    pool.wait_ge(s("cv_pe"), i * 2 + CREDIT)
                    pool.tensor_copy(A["wt"][:, u], vec[:, bass.ds(i * (2 * TAPS) + (_cols["w_dw"] + u * TAPS), TAPS_PE)])\
                        .then_inc(s("wt_ready"), 1)
                    pool.wait_ge(s("wt_ready"), i * 2 + (u + 1))
                    shape = [P, TAPS_PE, P]
                    last = pool.tensor_tensor(A["dg"][:, u], cst("ident").unsqueeze(1).to_broadcast(shape),
                                              A["wt"][:, u].unsqueeze(2).to_broadcast(shape), ALU.mult)
                    last.then_inc(s("dg_ready"), 1)
            pool.wait_ge(s("cv_done"), 1)
            pool.tensor_copy(A["mu"][:], A["cv"][:, 0]).then_inc(s("mu_acc"), 1)
            for k in range(1, KB):
                pool.wait_ge(s("cv_done"), k + 1)
                pool.wait_ge(s("mu_acc"), k)
                pool.tensor_tensor(A["mu"][:], A["mu"][:], A["cv"][:, k], ALU.add).then_inc(s("mu_acc"), 1)
            sum_squares("lnvar")
            sum_squares("ff1")
            sum_squares("da")
            with pool.Fori(0, 4) as i:
                def stage(e):
                    pool.wait_ge(s("da_o"), i * 2 + CREDIT)
                    pool.wait_ge(evac_done, T_DA)
                    pool.tensor_copy(A["vh"][:, e], A["dv"][:, :, bass.ds(i * 256 + e * 128, P)])\
                        .then_inc(s("da_vh"), 1)

                def rotated(e, c):
                    n = 2 * e + c
                    done = i * 4 + (n + 1)
                    pool.wait_ge(evac_done, i * 4 + (T_DA + n + 1))
                    pool.wait_ge(s("da_o"), i * 2 + CREDIT)
                    pool.tensor_tensor(A["dq"][:, e, c], A["draw"][:, c], cst("cos"), ALU.mult).then_inc(s("da_rc"), 1)
                    pool.wait_ge(s("da_rc"), done)
                    pool.wait_ge(s("da_shs"), done)
                    pool.tensor_tensor(A["dq"][:, e, c], A["dq"][:, e, c], A["dsh"][:, c], ALU.add)\
                        .then_inc(s("da_qn"), 1)

                for e in (0, 1):
                    rotated(e, 0)
                    rotated(e, 1)
                    stage(e)
            sum_squares("da_post")
            post_stage("da")
            sum_squares("mlp0_post")
            post_stage("mlp0")
            sum_squares("sc_post")
            post_stage("sc")
            sum_squares("mlp1_post")
            post_stage("mlp1")

        @block.tensor
        def _(pe):
            def passes(out, t_hi, t_lo, a_hi, a_lo, first, last, stationary_is_weight=True):
                w = ((t_hi, a_hi), (t_hi, a_lo), (t_lo, a_hi))
                for n, (wt, ac) in enumerate(w):
                    lhs, rhs = (wt, ac) if stationary_is_weight else (ac, wt)
                    mm = pe.matmul(out, lhs, rhs, start=first and n == 0, stop=last and n == 2)
                return mm

            def tile(t, bank, hi, lo, ready=None, base=0, blocks=KB, free=None):
                pe.wait_ge(wlo_ready, t.count)
                if free is None:
                    if t.n >= RING:
                        pe.wait_ge(evac_done, t.count - RING)
                else:
                    pe.wait_ge(evac_done, free)
                w_h = whi[:, t.slot].rearrange("p (k n) -> p k n", k=KB)
                w_l = wlo[:, t.slot].rearrange("p (k n) -> p k n", k=KB)
                for k in range(blocks):
                    if ready is not None:
                        pe.wait_ge(ready, base + (k + 1))
                    mm = passes(ps[:, bank], w_h[:, k], w_l[:, k], hi[:, k], lo[:, k], k == 0, k == blocks - 1)
                mm.then_inc(tile_done, 1)

            def wide(t, j, rows, cols):
                pe.wait_ge(wlo_ready, t.count)
                w_h = whi[:, t.slot].rearrange("p (k n) -> p k n", k=rows)
                w_l = wlo[:, t.slot].rearrange("p (k n) -> p k n", k=rows)
                for tb in range(TB):
                    tok = slice(tb * P, (tb + 1) * P)
                    for k in range(rows):
                        kk = j * rows + k
                        mm = passes(ps[:, tb, 0:cols], w_h[:, k], w_l[:, k], xh[:, kk, tok], xl[:, kk, tok],
                                    kk == 0, kk == KB - 1, stationary_is_weight=False)
                mm.then_inc(tile_done, 1)

            def row_sum(name):
                pe.wait_ge(acc_ready, (SUM[name] + 1) * KB)
                pe.matmul(ps[:, 4], cst("ones"), acc[:], start=True, stop=True).then_inc(sum_ready, 1)

            def col_sum():
                for tb in range(TB):
                    mm = pe.matmul(ps[:, 5, tb:tb + 1], acc[:, tb * P:(tb + 1) * P], cst("ones", cols=1), start=True,
                                   stop=True)
                mm.then_inc(colsum_ready, 1)

            pe.wait_ge(s("wglr_lo"), 1)
            g_h = A["wgh"][:].rearrange("p (k n) -> p k n", k=KB)
            g_l = A["wgl"][:].rearrange("p (k n) -> p k n", k=KB)
            for k in range(KB):
                pe.wait_ge(x_ready, k + 1)
                mm = passes(ps[:, 6], g_h[:, k], g_l[:, k], xh[:, k], xl[:, k], k == 0, k == KB - 1)
            mm.then_inc(s("glr_done"), 1)
            pe.wait_ge(small_in[1], 16)
            pe.wait_ge(acc_ready, KB)
            col_sum()
            row_sum("hyb")
            wide(Tile(0), 0, 4, 256)
            wide(Tile(1), 1, 4, 256)
            tile(Tile(2), 2, xh, xl, free=2)
            tile(Tile(3), 3, xh, xl, free=2)
            pe.wait_ge(s("glr_evac"), 2)
            pe.wait_ge(small_in[2], 16)
            for tb in range(TB):
                mm = pe.matmul(ps[:, 6 + tb // 2, (tb % 2) * 256:(tb % 2 + 1) * 256], A["glr"][0:17, tb * P:(tb + 1) * P],
                               A["wg2"][0:17, :], start=True, stop=True)
            mm.then_inc(s("gate_x"), 1)
            pe.wait_ge(evac_done, T_GV)
            for j in range(4):
                wide(Tile(T_GV + j), j, 2, 512)
            pe.wait_ge(s("la_ready"), 1)
            pe.wait_ge(rcol_ready, 1)
            pe.wait_ge(rrow_ready, 1)
            for tb in range(TB):
                pe.matmul(ps[:, 4 + tb // 2, (tb % 2) * 256:(tb % 2 + 1) * 256], cst("later64"), A["la"][:, tb],
                          start=True, stop=True)
            for j in range(2):
                for tb in range(TB):
                    mm = pe.matmul(ps[:, 6, j * 8 + 2 * tb:j * 8 + 2 * tb + 2], A["la"][:, tb, j * P:(j + 1) * P],
                                   cst("chunk"), start=True, stop=True)
            mm.then_inc(s("suf_ready"), 1)
            for j in range(4):
                tile(Tile(T_GR + j), j, xh, xl)
            pe.wait_ge(s("kend_ready"), 1)
            pe.wait_ge(s("dec_ready"), 1)
            for tb in range(TB):
                for c in range(2):
                    tok = slice(64 * c, 64 * c + 64)
                    for j in range(2):
                        u = 2 * tb + j
                        for e in range(2):
                            hd = 2 * j + e
                            mm = pe.matmul(ps[64 * e:64 * e + 64, 4 + 2 * c + u // 4, (u % 4) * P:(u % 4 + 1) * P],
                                           A["gk"][tok, tb, hd * 64:hd * 64 + 64], A["gv"][tok, tb, hd * P:(hd + 1) * P],
                                           start=True, stop=True)
                            mm_last = mm
            mm_last.then_inc(s("upd_ready"), 4)
            pe.wait_ge(evac_done, T_SV)
            for j in range(4):
                wide(Tile(T_SV + j), j, 2, 512)
            pe.wait_ge(evac_done, T_SB)
            pe.wait_ge(s("state_ready"), 16)
            for hd in range(GLA_HEADS):
                j, r = hd // 2, slice(64 * (hd % 2), 64 * (hd % 2) + 64)
                for n in range(8):
                    tok = slice(n * 64, n * 64 + 64)
                    mm = pe.matmul(ps[:, hd, tok], A["S"][r, n, j], A["gq"][r, j, tok], start=True, stop=True)
                mm.then_inc(s("go_ready"), 1)
            for hd in range(GLA_HEADS):
                pe.wait_ge(s("gsq_ready"), hd + 1)
                pe.matmul(ps[:, 4 + hd], cst("ones"), A["gt"][:, (hd % 2) * T:(hd % 2 + 1) * T], start=True, stop=True)\
                  .then_inc(s("gsum_ready"), 1)

            start_of = {0: 0, 1: 512, 2: 1024, 3: 896}
            pe.wait_ge(y_ready, 4)
            with pe.Fori(0, 2) as i:
                def qk_tile(e, c):
                    n = 2 * e + c
                    pe.wait_ge(s("sb_rr"), i * 4 + max(n - 1, 0) + CREDIT)
                    if n == 1:
                        pass
                    tile(Tile(T_SB + n, i), c, xh, xl, free=i * 4 + (T_SB + n - 1))

                def qk_sum(e, c):
                    n = 2 * e + c
                    pe.wait_ge(s("sb_sq"), i * 4 + (n + 1))
                    pe.matmul(ps[:, c], cst("blk64"), A["ssq"][:, c], start=True, stop=True).then_inc(s("sb_sum"), 1)

                def scores(e, hh):
                    n, b, r = 2 * e + hh, 2 + 3 * hh, slice(64 * hh, 64 * hh + 64)
                    pe.wait_ge(s("sb_qn"), i * 4 + (2 * e + 2) + CREDIT)
                    if n >= 2:
                        pe.wait_ge(s("sb_yl"), i * 4 + (n - 1) + CREDIT)
                    else:
                        pe.wait_ge(s("sb_yl"), i * 4 + CREDIT)
                    for kb in (0, 1, 3, 2):
                        a, w = start_of[kb], 512 - kb * P
                        mm = pe.matmul(flat[:, b * 512 + a:b * 512 + a + w], A["sqn"][r, e, 1, kb * P:(kb + 1) * P],
                                       A["sqn"][r, e, 0, kb * P:512], start=kb != 3, stop=True, skip_group_check=True)
                    mm.then_inc(s("sb_z"), 1)

                def accumulate(e, hh):
                    n, b = 2 * e + hh, 2 + 3 * hh
                    pe.wait_ge(s("sb_mask"), i * 4 + (n + 1))
                    for kb in range(TB):
                        a, w = b * 512 + start_of[kb], 512 - kb * P
                        for k2 in range(kb, TB):
                            off, w2 = (k2 - kb) * P, 512 - k2 * P
                            pe.matmul(flat[:, a + off:a + off + w2], cst("negtri" if k2 == kb else "negones"),
                                      A["sp"][:, hh, start_of[k2]:start_of[k2] + w2], start=False, stop=True,
                                      skip_group_check=True)
                        mm = pe.matmul(flat[:, a:a + P], cst("ident"), cst("neg_sb"), start=False, stop=True,
                                       skip_group_check=True)
                    mm.then_inc(s("sb_acc"), 1)

                def values(e, hh):
                    n, b, r = 2 * e + hh, 2 + 3 * hh, slice(64 * hh, 64 * hh + 64)
                    pe.wait_ge(s("sb_w"), i * 4 + (n + 1))
                    pe.wait_ge(s("sb_vp"), i * 2 + (e + 1))
                    for kb in range(TB):
                        a, w = start_of[kb], 512 - kb * P
                        mm = pe.matmul(ps[r, b, kb * P:512], A["vp"][:, e, kb, r], A["sl"][:, hh, a:a + w],
                                       start=kb == 0, stop=kb == TB - 1)
                    mm.then_inc(s("sb_o"), 1)

                qk_tile(0, 0)
                qk_tile(0, 1)
                qk_sum(0, 0)
                qk_sum(0, 1)
                scores(0, 0)
                scores(0, 1)
                qk_tile(1, 0)
                qk_tile(1, 1)
                accumulate(0, 0)
                accumulate(0, 1)
                qk_sum(1, 0)
                qk_sum(1, 1)
                values(0, 0)
                values(0, 1)
                scores(1, 0)
                scores(1, 1)
                accumulate(1, 0)
                accumulate(1, 1)
                values(1, 0)
                values(1, 1)

            pe.wait_ge(y_ready, 4)
            pe.wait_ge(s("sb_yl"), SB_HEADS + CREDIT)
            pe.wait_ge(s("sb_rr"), SB_HEADS + CREDIT)
            for k in range(KB):
                tile(Tile(T_WO + k), k % RING, yh, yl)

            def swiglu(f, t0, y0):
                name = f"ff{f}"
                tile(Tile(t0), 0, xh, xl, x_ready, 8 * PRE[name])
                row_sum(name)

                def up(t, js):
                    for j in js:
                        tile(t.plus(j), j, xh, xl)

                up(Tile(t0), (1, 2, 3))
                with pe.Fori(1, 4) as i:
                    up(Tile(t0, i), range(4))
                for k in range(KB):
                    tile(Tile(t0 + 16 + k), k % RING, yh, yl, y_ready, y0)
                with pe.Fori(0, 4) as i:
                    up(Tile(t0 + 24, i), range(4))
                for k in range(KB):
                    tile(Tile(t0 + 40 + k), k % RING, yh, yl, y_ready, y0 + 8)
                with pe.Fori(0, 3) as i:
                    up(Tile(t0 + 48, i), range(4))
                for k in range(KB):
                    tile(Tile(t0 + 60 + k), k % RING, yh, yl, y_ready, y0 + 16, FF_GROUPS[2])

            swiglu(0, T_FF0, Y0["ff0"])

            def conv(i, u):
                pe.wait_ge(s("dg_ready"), i * 2 + (u + 1))
                pe.wait_ge(s("pw_u"), i * 2 + (u + 1))
                if u or not isinstance(i, int):
                    pe.wait_ge(s("cv_done"), i * 2 + (u - 1))
                for k in range(TAPS_PE):
                    mm = pe.matmul(ps[:, 5 + u], A["dg"][:, u, k], A["ub"][:, u, k:k + T], start=k == 0,
                                   stop=k == TAPS_PE - 1)
                mm.then_inc(s("cv_pe"), 1)

            tile(Tile(T_PW1), 0, xh, xl, x_ready, 8 * PRE["pw"])
            row_sum("pw")
            tile(Tile(T_PW1 + 1), 1, xh, xl)
            tile(Tile(T_PW1 + 2), 2, xh, xl)
            conv(0, 0)
            tile(Tile(T_PW1 + 3), 3, xh, xl)
            with pe.Fori(1, 4) as i:
                tile(Tile(T_PW1, i), 0, xh, xl)
                conv(i - 1, 1)
                tile(Tile(T_PW1 + 1, i), 1, xh, xl)
                tile(Tile(T_PW1 + 2, i), 2, xh, xl)
                conv(i, 0)
                tile(Tile(T_PW1 + 3, i), 3, xh, xl)
            conv(3, 1)
            pe.wait_ge(s("mu_acc"), KB)
            pe.matmul(ps[:, 7], cst("ones"), A["mu"][:], start=True, stop=True).then_inc(s("mu_sum"), 1)
            row_sum("lnvar")
            for k in range(KB):
                tile(Tile(T_PW2 + k), k % RING, yh, yl, y_ready, Y0["pw"])

            swiglu(1, T_FF1, Y0["ff1"])

            pe.wait_ge(s("lam_p"), 1)
            pe.matmul(ps[:, 6, 0:2], cst("ones"), lamt[:, 0], start=True, stop=True).then_inc(s("lam_s"), 1)
            pe.wait_ge(x_ready, 8 * PRE["da"] + 8)
            row_sum("da")
            col_sum()
            with pe.Fori(0, 2) as r:
                pe.wait_ge(evac_done, r * 4 + T_DV)
                for j in range(4):
                    wide(Tile(T_DV + j, r), j, 2, 512)
            pe.wait_ge(evac_done, T_DA)
            pe.wait_ge(rrow_ready, SUM["da"] + 1)
            pe.wait_ge(rcol_ready, 2)
            with pe.Fori(0, 4) as i:
                def qk(n):
                    tile(Tile(T_DA + n, i), n % 2, xh, xl, free=i * 4 + (T_DA + n - 1))

                def scores(e, u):
                    n, p, kv = 4 * e + u, u % 2, (u + 1) * P
                    pe.wait_ge(s("da_qn"), i * 4 + (2 * e + 2) + CREDIT)
                    if n >= 2:
                        pe.wait_ge(s("da_exp"), i * 16 + 2 * (n - 1) + CREDIT)
                    else:
                        pe.wait_ge(s("da_exp"), i * 16 + CREDIT)
                    for c in (0, 1):
                        r, b = slice(64 * c, 64 * c + 64), 2 + 2 * p + c
                        pe.matmul(ps[:, b, 0:kv], A["dq"][r, e, 0, u * P:(u + 1) * P], A["dq"][r, e, 1, 0:kv],
                                  start=True, stop=True)
                        mm = pe.matmul(ps[:, b, kv - P:kv], cst("ident"), cst("neg_da"), start=False, stop=True,
                                       skip_group_check=True)
                    mm.then_inc(s("da_s"), 1)

                def transposes(e, u):
                    n = 4 * e + u
                    pe.wait_ge(s("da_a"), i * 8 + (n + 1))
                    pe.wait_ge(s("da_aT"), i * 8 + n + CREDIT)
                    if u == 0:
                        pe.wait_ge(s("da_rr"), i * 2 + e + CREDIT)
                    for b in range(u + 1):
                        mm = pe.transpose(ps[:, 6, b * P:(b + 1) * P], A["da"][:, u % 2, b * P:(b + 1) * P], cst("ident"))
                    mm.then_inc(s("da_T"), 1)

                def values(e, u):
                    n, at = 4 * e + u, P * u * (u + 1) // 2
                    pe.wait_ge(s("da_aT"), i * 8 + (n + 1) + CREDIT)
                    if u == 0:
                        pe.wait_ge(s("da_vh"), i * 2 + (e + 1))
                        pe.wait_ge(s("da_ot"), i * 2 + e + CREDIT)
                    for b in range(u + 1):
                        mm = pe.matmul(ps[:, 7, u * P:(u + 1) * P], A["vh"][:, e, b], A["aT"][:, at + b * P:at + b * P + P],
                                       start=b == 0, stop=b == u)
                    if u == 3:
                        mm.then_inc(s("da_o"), 1)

                def norm_sum(e):
                    pe.wait_ge(s("da_sq"), i * 2 + (e + 1))
                    pe.matmul(ps[:, 6], cst("ones"), sq[:, 0], start=True, stop=True).then_inc(s("da_sum"), 1)

                qk(0)
                qk(1)
                for e in (0, 1):
                    scores(e, 0)
                    scores(e, 1)
                    if e == 0:
                        qk(2)
                    transposes(e, 0)
                    scores(e, 2)
                    transposes(e, 1)
                    scores(e, 3)
                    if e == 0:
                        qk(3)
                    transposes(e, 2)
                    values(e, 0)
                    values(e, 1)
                    transposes(e, 3)
                    values(e, 2)
                    values(e, 3)
                    norm_sum(e)

            def to_m(t0, which, y0):
                for k in range(KB):
                    tile(Tile(t0 + k), k % RING, yh, yl, y_ready, y0)
                row_sum(which + "_post")

            pe.wait_ge(y_ready, Y0["da"] + 8)
            to_m(T_DO, "da", Y0["da"])

            def mlp(f, t0, y0):
                name = f"mlp{f}"
                tile(Tile(t0), 0, xh, xl, x_ready, 8 * PRE[name])
                row_sum(name)
                for j in (1, 2, 3):
                    tile(Tile(t0 + j), j, xh, xl)
                for j in range(4):
                    tile(Tile(t0 + 4 + j), j, xh, xl)
                with pe.Fori(0, 2) as i:
                    for j in range(4):
                        tile(Tile(t0 + 8 + j, i), j, yh, yl, y_ready, y0)
                with pe.Fori(1, MLP_GROUPS - 1) as g:
                    with pe.Fori(0, 2) as i:
                        for j in range(4):
                            tile(Tile(t0 + j, g * 4 + i), j, xh, xl)
                    with pe.Fori(0, 2) as i:
                        for j in range(4):
                            tile(Tile(t0 + 8 + j, g * 4 + i), j, yh, yl, y_ready, g * 8 + y0)
                with pe.Fori(0, 2) as i:
                    for j in range(4):
                        tile(Tile(t0 + 48 + j, i), j, xh, xl)
                to_m(t0 + 56, name, y0 + 24)

            mlp(0, T_MLP0, Y0["mlp0"])

            tile(Tile(T_SC), 0, xh, xl, x_ready, 8 * PRE["sc"])
            row_sum("sc")
            for j in range(1, 12):
                tile(Tile(T_SC + j), j % RING, xh, xl)
            for j in range(12, 24):
                tile(Tile(T_SC + j), j % RING, xh, xl)
            to_m(T_SCO, "sc", Y0["sc"])
            mlp(1, T_MLP1, Y0["mlp1"])


Y0 = {"ff0": 4, "pw": 26, "ff1": 34, "da": 56, "mlp0": 64, "sc": 96, "mlp1": 104}


def _narrow(w, k0, n):
    rows = w[k0:k0 + D, n * P:(n + 1) * P]
    if rows.shape[0] < D:
        rows = np.concatenate([rows, np.zeros((D - rows.shape[0], P), rows.dtype)])
    return rows.reshape(KB, P, P).transpose(1, 0, 2).reshape(P, D)


def _wide(w, j, rows, c0, cols):
    return w[j * rows * P:(j + 1) * rows * P, c0:c0 + cols].reshape(rows, P, cols).transpose(1, 0, 2).reshape(P, D)


def _stream(a):
    w = a["hy_w_in"][0]
    c_glr, c_sq, c_sk, c_sv = 1536, 1552, 2064, 2576
    gr, sbw = w[:, 1024:1536], w[:, c_sq:]
    tiles = [_wide(w, j, 4, 256, 256) for j in range(2)]
    tiles += [_narrow(w, 0, j) for j in range(2)]
    tiles += [_wide(w, j, 2, 512, 512) for j in range(4)]
    tiles += [_narrow(gr, 0, j) for j in range(4)]
    tiles += [_wide(w, j, 2, c_sv, 512) for j in range(4)]
    for p in range(4):
        tiles += [_narrow(sbw, 0, p), _narrow(sbw, 0, 4 + p)]
    tiles += [_narrow(a["hy_w_out"][0], 0, n) for n in range(KB)]

    def swiglu(f):
        out, at = [], 0
        for g in FF_GROUPS:
            for q in range(at, at + g):
                out += [_narrow(a["ffn_w_gate"][f], 0, q), _narrow(a["ffn_w_up"][f], 0, q)]
            rows = a["ffn_w_down"][f][at * P:(at + g) * P]
            out += [_narrow(rows, 0, n) for n in range(KB)]
            at += g
        return out

    tiles += swiglu(0)
    for j in range(KB):
        tiles += [_narrow(a["cv_w_pw1"][0], 0, j), _narrow(a["cv_w_pw1"][0], 0, KB + j)]
    tiles += [_narrow(a["cv_w_pw2"][0], 0, n) for n in range(KB)]
    tiles += swiglu(1)
    qkv = a["attn_w_qkv_2"][0]
    for r in range(2):
        tiles += [_wide(qkv, j, 2, 2048 + 512 * r, 512) for j in range(4)]
    for q in range(DA_HEADS):
        tiles += [_narrow(qkv, 0, q), _narrow(qkv, 0, KB + q)]
    tiles += [_narrow(a["attn_w_o_2"][0], 0, n) for n in range(KB)]

    def mlp(f):
        out = []
        for g in range(MLP_GROUPS):
            out += [_narrow(a["mlp_w_up_2"][f], 0, 8 * g + j) for j in range(8)]
            out += [_narrow(a["mlp_w_down_2"][f], g * D, n) for n in range(KB)]
        return out

    tiles += mlp(0)
    for j in range(KB):
        tiles += [_narrow(a["conv_w_in_2"][0], 0, c * KB + j) for c in range(3)]
    tiles += [_narrow(a["conv_w_out_2"][0], 0, n) for n in range(KB)]
    tiles += mlp(1)
    assert len(tiles) == NT
    return np.stack(tiles)


def _vectors(a):
    f = np.zeros((P, NVEC), a["x"].dtype)

    def put(name, v, at=0):
        cols = np.asarray(v).reshape(-1, P).T
        f[:, _cols[name] + at:_cols[name] + at + cols.shape[1]] = cols

    for n, v in enumerate((a["mix_norm"][0], a["ffn_norm"][0], a["mix_norm"][1], a["ffn_norm"][1],
                           a["norm_mixer_pre_2"][0], a["norm_mlp_pre_2"][0], a["norm_mixer_pre_2"][1],
                           a["norm_mlp_pre_2"][1])):
        put("pre", v, 8 * n)
    for n, v in enumerate((a["norm_mixer_post_2"][0], a["norm_mlp_post_2"][0], a["norm_mixer_post_2"][1],
                           a["norm_mlp_post_2"][1])):
        put("post", v, 8 * n)
    put("b_pw1", a["cv_b_pw1"][0])
    f[:, _cols["w_dw"]:_cols["w_dw"] + TAPS * KB] = \
        a["cv_w_dw"][0].reshape(TAPS, KB, P).transpose(2, 1, 0).reshape(P, -1)
    put("b_dw", a["cv_b_dw"][0])
    put("ln_g", a["cv_ln_g"][0])
    put("ln_b", a["cv_ln_b"][0])
    put("b_pw2", a["cv_b_pw2"][0])
    put("gla", a["hy_gla_norm"][0])
    put("sbq", np.tile(a["hy_sb_q_norm"][0], 2))
    put("sbk", np.tile(a["hy_sb_k_norm"][0], 2))
    put("subln", a["attn_subln_g_2"][0])
    f[:, _cols["conv_w"]:_cols["conv_w"] + 24] = a["conv_w_2"][0].reshape(3, KB, P).transpose(2, 1, 0).reshape(P, -1)
    for n, v in enumerate(("q1", "k1", "q2", "k2")):
        f[:64, _cols["lam"] + n] = a[f"attn_lambda_{v}_2"][0]
    return f


def _constants():
    f = np.zeros((P, NCONST), np.float32)
    p, c = np.arange(P)[:, None], np.arange(P)[None, :]

    def put(name, v):
        at, n = _consts[name]
        f[:, at:at + n] = v

    put("ident", p == c)
    put("ones", 1.0)
    put("blk64", p // 64 == c // 64)
    put("negtri", -1.0 * (p >= c))
    put("negones", -1.0)
    put("later64", (p > c) & (p // 64 == c // 64))
    put("neg_sb", np.where(p < c, 0.0, NEG))
    put("neg_da", np.where(c <= p, 0.0, NEG))
    put("mask_sb", p < c)
    put("chunk", p // 64 == np.arange(2)[None, :])
    half = 8
    inv = 500000.0 ** (-np.arange(0, 16, 2, dtype=np.float32) / np.float32(16))
    ang = (np.arange(T, dtype=np.float32)[:, None] * inv[None, :].astype(np.float32)).astype(np.float32)
    cos, sin = np.ones((64, T), np.float32), np.zeros((64, T), np.float32)
    cos[:half] = cos[half:16] = np.cos(ang).T
    sin[:half], sin[half:16] = -np.sin(ang).T, np.sin(ang).T
    put("cos", np.tile(cos, (2, 1)))
    put("sin", np.tile(sin, (2, 1)))
    return f


def kernel(**inputs):
    import concourse.bacc as bacc
    from concourse.bass_utils import run_bass_kernel_spmd

    a = {k: np.asarray(v) for k, v in inputs.items()}
    w_in = a["hy_w_in"][0]
    glr = np.concatenate([w_in[:, 1536:1552], np.zeros((D, P - 16), w_in.dtype)], axis=1)
    arrays = {
        "x_t": np.ascontiguousarray(a["x"][0].T),
        "stream": _stream(a),
        "w_glr": np.ascontiguousarray(_narrow(glr, 0, 0)),
        "w_gate": np.ascontiguousarray(np.concatenate([a["hy_w_gate2"][0], a["hy_b_gate"]], axis=0)),
        "vecs": _vectors(a),
        "consts": _constants(),
    }
    nc = bacc.Bacc("TRN2", target_bir_lowering=False, num_devices=1)
    args = [nc.dram_tensor(n, v.shape, mybir.dt.from_np(v.dtype), kind="ExternalInput").ap() for n, v in arrays.items()]
    out_t = nc.dram_tensor("out_t", (D, T), F32, kind="ExternalOutput").ap()
    build(nc, *args, out_t)
    got = run_bass_kernel_spmd(nc, [arrays], core_ids=[0]).results[0]["out_t"]
    return np.ascontiguousarray(np.asarray(got).T)[None]
```

```python
from contextlib import ExitStack

import numpy as np

import concourse.bass as bass
from concourse import mybir

F32 = mybir.dt.float32
F32R = mybir.dt.float32r
ACT = mybir.ActivationFunctionType
ALU = mybir.AluOpType
AX = mybir.AxisListType

P = 128
T = 512
D = 1024
KB = D // P
TB = T // P
EPS = 1e-6
NEG = -1e30
LN_EXP = "natural_log_exp_and_others"
RING = 4
FIRST = 3
TAPS = 31
TAPS_PE = 12
PAD = TAPS - 1
FF_GROUPS = (8, 8, 6)
MLP_GROUPS = 4
SB_HEADS, DA_HEADS, GLA_HEADS, CHUNK = 8, 8, 4, 64
CREDIT = 1
CREDITED = "sb_qn sb_rr da_qn sb_o cv_pe da_o sb_yl da_exp da_aT da_rr da_ot".split()
LAMBDA_INIT = 0.2

T_GK, T_GQ, T_GV, T_GR, T_SV, T_SB, T_WO = 0, 2, 4, 8, 12, 16, 32 - 8
T_FF0 = T_WO + 8
T_PW1 = T_FF0 + 68
T_PW2 = T_PW1 + 16
T_FF1 = T_PW2 + 8
T_DV = T_FF1 + 68
T_DA = T_DV + 8
T_DO = T_DA + 16
T_MLP0 = T_DO + 8
T_SC = T_MLP0 + 64
T_SCO = T_SC + 24
T_MLP1 = T_SCO + 8
NT = T_MLP1 + 64
assert T_SB + 8 == T_WO and NT % RING == 0

_cols = {}
_at = 0
for _name, _n in (("pre", 64), ("post", 32), ("b_pw1", 16), ("w_dw", TAPS * KB), ("b_dw", 8), ("ln_g", 8),
                  ("ln_b", 8), ("b_pw2", 8), ("gla", 1), ("sbq", 1), ("sbk", 1), ("subln", 1),
                  ("conv_w", 24), ("lam", 4)):
    _cols[_name] = _at
    _at += _n
NVEC = _at

_consts = {}
_at = 0
for _name, _n in (("ident", P), ("ones", P), ("blk64", P), ("negtri", P), ("negones", P), ("later64", P),
                  ("neg_sb", P), ("neg_da", P), ("mask_sb", P), ("chunk", 2), ("cos", T), ("sin", T)):
    _consts[_name] = (_at, _n)
    _at += _n
NCONST = _at


class Tile:

    def __init__(self, n, rounds=0):
        self.n, self.rounds = n, rounds
        self.slot = n % RING

    def plus(self, d):
        return Tile(self.n + d, self.rounds)

    @property
    def count(self):
        return self.rounds * RING + (self.n + 1)

    @property
    def loaded(self):
        return self.rounds * 16 + 16 * (self.n // RING + 1)


def build(nc, x_t, stream, w_glr, w_gate, vecs, consts, out_t):
    with ExitStack() as ctx:
        def sem(name):
            return ctx.enter_context(nc.semaphore(name))

        def sb(name, shape, dt=F32, where=ctx):
            return where.enter_context(nc.sbuf_tensor(name, shape, dt))

        ps = ctx.enter_context(nc.psum_tensor("ps", [P, 8, 512], F32))
        flat = ps[:].rearrange("p b c -> p (b c)")

        h = sb("h", [P, KB, T])
        xh, xl = sb("xh", [P, KB, T], F32R), sb("xl", [P, KB, T], F32R)
        yh, yl = sb("yh", [P, KB, T], F32R), sb("yl", [P, KB, T], F32R)
        raw = sb("raw", [P, RING, D])
        whi, wlo = sb("whi", [P, RING, D], F32R), sb("wlo", [P, RING, D], F32R)
        vec = sb("vec", [P, NVEC])
        const = sb("const", [P, NCONST])
        sq = sb("sq", [P, 2, T])
        acc = sb("acc", [P, T])
        lnb = sb("lnb", [P, T])
        rrow = sb("rrow", [P, T])
        lncol = sb("lncol", [P, TB])
        rcol = sb("rcol", [P, TB])
        nlam = sb("nlam", [P, 1])
        lamt = sb("lamt", [P, 2, 2])

        def cst(name, rows=slice(None), cols=None):
            a, n = _consts[name]
            return const[rows, a:a + (cols or n)]

        def col(name, j=0):
            a = _cols[name] + j
            return vec[:, a:a + 1] if isinstance(a, int) else vec[:, bass.ds(a, 1)]

        def block_of(x, q):
            return x[:, q] if isinstance(q, int) else x[:, bass.ds(q, 1)].rearrange("p a t -> p (a t)")

        def arena(**shapes):
            scope = ExitStack()
            with scope:
                return {k: scope.enter_context(nc.sbuf_tensor(k, [P] + list(v[:-1] if v[-1] is F32R else v),
                                                              F32R if v[-1] is F32R else F32))
                        for k, v in shapes.items()}

        A = {}
        hyb = ExitStack()
        with hyb:
            A["sv"] = sb("sv", [P, TB, T], F32, hyb)
            A.update(arena(glr=(T,), wg2=(256,), gq=(2, T), gk=(TB, 256), gv=(TB, T), sr=(4, T), la=(TB, 256),
                           gt=(D,), dec=(2, 8), wgr=(D,), wgh=(D, F32R), wgl=(D, F32R)))
            A.update(arena(_glr=(T,), _wg2=(256,), _gq=(2, T), _gk=(TB, 256), _gv=(TB, T), _sr=(4, T), _la=(TB, 256),
                           _gt=(D,), _dec=(2, 8), S=(8, 2, P)))
            A.update(arena(sraw=(2, 2, T), ssq=(2, T), srr=(2, T), sqn=(2, 2, T), vp=(2, TB, P),
                           sl=(2, 1280), sp=(2, 1280)))
        A.update(arena(tg=(2, T), ts=(2, T), tu=(2, T), th=(2, T)))
        A.update(arena(t1=(2, T), t2=(2, T), t3=(2, T), ub=(2, T + PAD), dg=(2, TAPS_PE, P), wt=(2, TAPS_PE), cv=(KB, T), mu=(T,)))
        A.update(arena(dv=(TB, D), draw=(2, T), dsh=(2, T), dq=(2, 2, T), vh=(2, TB, P), ex=(2, 2, T),
                       da=(2, T), aT=(1280,), dot=(T,), nm=(2, 2), sm=(2, 2), rc=(2, 2),
                       r1=(2, 1)))
        A.update(arena(m=(KB, T), pt=(2, T), mr=(2, T), mh=(2, T), cb=(2, T), cc=(2, T), cx=(2, T), uc=(2, T + 2),
                       cy=(2, T)))

        loaded = [sem(f"weight_loaded{s}") for s in range(RING)]
        whi_ready = sem("whi_ready")
        wlo_ready = sem("wlo_ready")
        tile_done = sem("tile_done")
        evac_done = sem("evac_done")
        x_in = [sem(f"x_in{k}") for k in range(KB)]
        small_in = [sem(f"small_in{k}") for k in range(4)]
        xh_ready, x_ready = sem("xh_ready"), sem("x_ready")
        yh_ready, y_ready = sem("yh_ready"), sem("y_ready")
        sq_ready, acc_ready = sem("sq_ready"), sem("acc_ready")
        sum_ready = sem("sum_ready")
        colsum_ready = sem("colsum_ready")
        ln_ready, rrow_ready, rcol_ready = sem("ln_ready"), sem("rrow_ready"), sem("rcol_ready")
        lncol_ready = sem("lncol_ready")
        h_added = sem("h_added")
        post_t = sem("post_t")
        stored = sem("stored")

        S = {}

        def s(name):
            if name not in S:
                S[name] = sem(name)
            return S[name]

        for n in ("wglr_in wglr_hi wglr_lo glr_done glr_evac gate_x gate_abs gate_exp gate_ln la_ready suf_ready "
                  "kd_ready kend_ready dec_ready upd_ready state_ready state_chain go_ready gsq_ready gsum_ready "
                  "gln_ready grr_ready gt_ready gy_ready gyh_ready row0 "
                  "sb_sq sb_sum sb_ln sb_rr sb_qn sb_vp sb_z sb_abs sb_exp sb_ln2 sb_sp sb_mask sb_acc sb_w "
                  "sb_o sb_yh sb_yl mix_y "
                  "var_mm cen_sq wt_ready pw_sg pw_u pw_zero dg_ready dg_used cv_pe cv_chain cv_done mu_acc mu_sum mu_copied cen_ready ln_t ln_s pw_in "
                  "lam_p lam_s lam_e lam_ready "
                  "da_sh da_shs da_rc da_qn da_vh da_s da_max da_exp da_rcp da_r1 da_t da_a da_T da_aT da_o da_sq da_sum "
                  "da_ln da_rr da_ot m_zero sc_u sc_y sc_zero sc_in").split():
            s(n)
        for f in (0, 1):
            for n in ("silu", "hid"):
                s(f"ff{f}_{n}")
            s(f"mlp{f}_hid")

        block = ctx.enter_context(nc.Block())

        SUM = {"hyb": 0, "ff0": 1, "pw": 2, "lnvar": 3, "ff1": 4, "da": 5, "da_post": 6, "mlp0": 7, "mlp0_post": 8,
               "sc": 9, "sc_post": 10, "mlp1": 11, "mlp1_post": 12}
        ACC = {n: (q - (q > 3)) * (KB - 1) for n, q in SUM.items() if n != "lnvar"}
        PRE = {"hyb": 0, "ff0": 1, "pw": 2, "ff1": 3, "da": 4, "mlp0": 5, "sc": 6, "mlp1": 7}
        POST = {"da": 0, "mlp0": 1, "sc": 2, "mlp1": 3}

        @block.sync
        def _(sp):
            for name in CREDITED:
                sp.sem_inc(s(name), CREDIT)
            sp.dma_start(vec[:], vecs).then_inc(small_in[0], 16)
            for k in range(KB):
                sp.dma_start(h[:, k], x_t[k * P:(k + 1) * P, :]).then_inc(x_in[k], 16)
            sp.dma_start(A["wgr"][:], w_glr).then_inc(s("wglr_in"), 16)
            sp.dma_start(const[:], consts).then_inc(small_in[1], 16)
            sp.dma_start(A["wg2"][0:17, :], w_gate).then_inc(small_in[2], 16)
            for j in range(RING):
                sp.dma_start(raw[:, j], stream[j]).then_inc(loaded[j], 16)
            with sp.Fori(1, NT // RING) as r:
                for j in range(RING):
                    sp.wait_ge(wlo_ready, r * RING + (j + 1 - RING))
                    sp.dma_start(raw[:, j], stream[bass.ds(r * RING + j, 1)].rearrange("a p c -> (a p) c"))\
                      .then_inc(loaded[j], 16)
            for k in range(KB):
                sp.wait_ge(h_added, 8 * 3 + k + 1)
                sp.dma_start(out_t[k * P:(k + 1) * P, :], h[:, k]).then_inc(stored, 16)
            sp.wait_ge(stored, 16 * KB)

        @block.scalar
        def _(act):
            def split_hi(t):
                if t.n + RING >= NT:
                    return
                a = t.plus(RING)
                act.wait_ge(loaded[a.slot], a.loaded)
                act.wait_ge(tile_done, t.count)
                act.activation(whi[:, a.slot], raw[:, a.slot], ACT.Copy).then_inc(whi_ready, 1)

            def square_block(name, k, src):
                if k < 2 and SUM[name]:
                    act.wait_ge(sum_ready, SUM[name])
                    act.wait_ge(acc_ready, ACC[name])
                elif k >= 2:
                    act.wait_ge(acc_ready, ACC[name] + k - 1)
                act.activation(sq[:, k % 2], src, ACT.Square).then_inc(sq_ready, 1)

            def pre_block(name, k):
                act.activation(xh[:, k], h[:, k], ACT.Copy, scale=col("pre", 8 * PRE[name] + k)).then_inc(xh_ready, 1)
                square_block(name, k, h[:, k])

            def inv_rms(name, n):
                act.preload_act_table_set(LN_EXP)
                act.wait_ge(sum_ready, SUM[name] + 1)
                if SUM[name]:
                    act.wait_ge(rrow_ready, SUM[name])
                act.activation(lnb[:], ps[:, 4], ACT.Ln, scale=1.0 / n, bias=EPS).then_inc(ln_ready, 1)
                act.wait_ge(ln_ready, SUM[name] + 1)
                act.activation(rrow[:], lnb[:], ACT.Exp, scale=-0.5).then_inc(rrow_ready, 1)

            def inv_rms_col(n):
                act.wait_ge(colsum_ready, n)
                act.activation(lncol[:], ps[:, 5, 0:TB], ACT.Ln, scale=1.0 / D, bias=EPS).then_inc(lncol_ready, 1)
                act.wait_ge(lncol_ready, n)
                act.activation(rcol[:], lncol[:], ACT.Exp, scale=-0.5).then_inc(rcol_ready, 1)

            def down_tile(t, k, name):
                if name:
                    act.wait_ge(evac_done, t.count)
                    pre_block(name, k)
                split_hi(t)

            def post_stage(which, name):
                for k in range(KB):
                    act.wait_ge(h_added, 8 * POST[which] + k + 1)
                    pre_block(name, k)

            act.preload_act_table_set(LN_EXP)
            act.wait_ge(s("wglr_in"), 16)
            act.activation(A["wgh"][:], A["wgr"][:], ACT.Copy).then_inc(s("wglr_hi"), 1)
            act.wait_ge(small_in[0], 16)
            for k in range(KB):
                act.wait_ge(x_in[k], 16)
                pre_block("hyb", k)
            for j in range(RING):
                act.wait_ge(loaded[j], 16)
                act.activation(whi[:, j], raw[:, j], ACT.Copy).then_inc(whi_ready, 1)
            inv_rms("hyb", D)
            inv_rms_col(1)
            for n in (0, 1, 2, 3):
                split_hi(Tile(n))
            act.wait_ge(s("gate_x"), 1)
            act.activation(A["gt"][:], flat[:, 6 * 512:8 * 512], ACT.Abs).then_inc(s("gate_abs"), 1)
            act.wait_ge(s("gate_abs"), 1)
            act.activation(A["gt"][:], A["gt"][:], ACT.Exp, scale=-1.0).then_inc(s("gate_exp"), 1)
            act.wait_ge(s("gate_exp"), 1)
            act.activation(A["gt"][:], A["gt"][:], ACT.Ln, bias=1.0).then_inc(s("gate_ln"), 1)
            for n in range(T_GV, T_GR):
                split_hi(Tile(n))
            act.wait_ge(s("suf_ready"), 1)
            act.activation(A["gt"][:], flat[:, 4 * 512:6 * 512], ACT.Exp, scale=1.0 / 16).then_inc(s("kd_ready"), 1)
            act.activation(A["dec"][:], ps[:, 6, 0:16].rearrange("p (j n) -> p j n", j=2), ACT.Exp,
                           scale=1.0 / 16).then_inc(s("dec_ready"), 1)
            for j in range(4):
                act.wait_ge(evac_done, T_GR + j + 1)
                act.activation(A["sr"][:, j], A["sr"][:, j], ACT.Silu).then_inc(s("row0"), 1)
                split_hi(Tile(T_GR + j))
            for n in range(T_SV, T_SB):
                split_hi(Tile(n))
            for hh in range(GLA_HEADS):
                act.wait_ge(s("go_ready"), hh + 1)
                if hh >= 2:
                    act.wait_ge(s("gsum_ready"), hh - 1)
                act.activation(A["gt"][:, (hh % 2) * T:(hh % 2 + 1) * T], ps[:, hh], ACT.Square)\
                   .then_inc(s("gsq_ready"), 1)
            for hh in range(GLA_HEADS):
                act.wait_ge(s("gsum_ready"), hh + 1)
                if hh:
                    act.wait_ge(s("grr_ready"), hh)
                act.activation(lnb[:], ps[:, 4 + hh], ACT.Ln, scale=1.0 / P, bias=EPS).then_inc(s("gln_ready"), 1)
                act.wait_ge(s("gln_ready"), hh + 1)
                act.activation(A["S"][:, 2 * hh:2 * hh + 2].rearrange("p a j v -> p (a j v)"), lnb[:], ACT.Exp,
                               scale=-0.5).then_inc(s("grr_ready"), 1)
            for hh in range(GLA_HEADS):
                act.wait_ge(s("gy_ready"), hh + 1)
                act.activation(yh[:, hh], A["gv"][:, hh], ACT.Copy).then_inc(yh_ready, 1)

            with act.Fori(0, 2) as i:
                def square_qk(e, c):
                    n = 2 * e + c
                    act.wait_ge(evac_done, i * 4 + (T_SB + n + 1))
                    act.activation(A["ssq"][:, c], A["sraw"][:, e, c], ACT.Square).then_inc(s("sb_sq"), 1)
                    split_hi(Tile(T_SB + n, i))

                def rms_qk(e, c):
                    n = 2 * e + c
                    act.wait_ge(s("sb_sum"), i * 4 + (n + 1))
                    act.wait_ge(s("sb_rr"), i * 4 + n + CREDIT)
                    act.activation(lnb[:], ps[:, c], ACT.Ln, scale=1.0 / 64, bias=EPS).then_inc(s("sb_ln"), 1)
                    act.wait_ge(s("sb_ln"), i * 4 + (n + 1))
                    if c == 0:
                        act.wait_ge(s("sb_qn"), i * 4 + n + CREDIT)
                    act.activation(A["srr"][:, c], lnb[:], ACT.Exp, scale=-0.5,
                                   bias=float(-np.log(8.0)) if c == 0 else 0.0).then_inc(s("sb_rr"), 1)

                def soft(e, hh):
                    n, b = 2 * e + hh, 2 + 3 * hh
                    act.wait_ge(s("sb_z"), i * 4 + (n + 1))
                    act.activation(A["sl"][:, hh], flat[:, b * 512:b * 512 + 1280], ACT.Abs).then_inc(s("sb_abs"), 1)
                    act.wait_ge(s("sb_abs"), i * 4 + (n + 1))
                    act.activation(A["sl"][:, hh], A["sl"][:, hh], ACT.Exp, scale=-1.0).then_inc(s("sb_exp"), 1)
                    act.wait_ge(s("sb_exp"), i * 4 + (n + 1))
                    act.activation(A["sl"][:, hh], A["sl"][:, hh], ACT.Ln, bias=1.0).then_inc(s("sb_ln2"), 1)

                def weights(e, hh):
                    n, b = 2 * e + hh, 2 + 3 * hh
                    act.wait_ge(s("sb_acc"), i * 4 + (n + 1))
                    act.activation(A["sl"][:, hh], flat[:, b * 512:b * 512 + 1280], ACT.Exp).then_inc(s("sb_w"), 1)

                def out_hi(e, hh):
                    n, b, r = 2 * e + hh, 2 + 3 * hh, slice(64 * hh, 64 * hh + 64)
                    act.wait_ge(s("sb_o"), i * 4 + (n + 1) + CREDIT)
                    act.activation(yh[r, bass.ds(i * 2 + (4 + e), 1)].rearrange("p a t -> p (a t)"), ps[r, b],
                                   ACT.Copy).then_inc(s("sb_yh"), 1)

                square_qk(0, 0)
                square_qk(0, 1)
                rms_qk(0, 0)
                rms_qk(0, 1)
                soft(0, 0)
                square_qk(1, 0)
                soft(0, 1)
                square_qk(1, 1)
                weights(0, 0)
                weights(0, 1)
                rms_qk(1, 0)
                rms_qk(1, 1)
                out_hi(0, 0)
                out_hi(0, 1)
                soft(1, 0)
                soft(1, 1)
                weights(1, 0)
                weights(1, 1)
                out_hi(1, 0)
                out_hi(1, 1)

            for k in range(KB):
                down_tile(Tile(T_WO + k), k, "ff0")

            def swiglu(f, t0, following):
                name = f"ff{f}"
                inv_rms(name, D)

                def up(g, i, q0):
                    for u in (0, 1):
                        tg = Tile(t0 + 2 * u, g * 6 + i)
                        act.wait_ge(evac_done, tg.count)
                        act.activation(A["ts"][:, u], A["tg"][:, u], ACT.Silu).then_inc(s(name + "_silu"), 1)
                        split_hi(tg)
                        done = g * 8 + i * 2 + (u + 1)
                        act.wait_ge(s(name + "_hid"), done)
                        act.activation(yh[:, bass.ds(i * 2 + u, 1)].rearrange("p a t -> p (a t)"), A["th"][:, u],
                                       ACT.Copy).then_inc(yh_ready, 1)
                        split_hi(tg.plus(1))

                with act.Fori(0, 2) as g:
                    with act.Fori(0, 4) as i:
                        up(g, i, 0)
                    for k in range(KB):
                        split_hi(Tile(t0 + 16 + k, g * 6))
                with act.Fori(0, 3) as i:
                    up(2, i, 16)
                for k in range(KB):
                    down_tile(Tile(t0 + 60 + k), k, following)

            swiglu(0, T_FF0, "pw")

            inv_rms("pw", D)
            with act.Fori(0, 4) as i:
                for u in (0, 1):
                    split_hi(Tile(T_PW1 + 2 * u, i))
                    t = Tile(T_PW1 + 2 * u + 1, i)
                    act.wait_ge(evac_done, t.count)
                    act.activation(A["t3"][:, u], A["t2"][:, u], ACT.Sigmoid,
                                   bias=vec[:, bass.ds(i * 2 + (_cols["b_pw1"] + 8 + u), 1)]).then_inc(s("pw_sg"), 1)
                    split_hi(t)
            for k in range(KB):
                act.wait_ge(s("cen_ready"), k + 1)
                if k >= 2:
                    act.wait_ge(s("var_mm"), k - 1)
                else:
                    act.wait_ge(sum_ready, SUM["lnvar"])
                act.activation(sq[:, k % 2], A["cv"][:, k], ACT.Square).then_inc(s("cen_sq"), 1)
            inv_rms("lnvar", D)
            for k in range(KB):
                act.wait_ge(s("ln_t"), k + 1)
                if k >= 2:
                    act.wait_ge(y_ready, Y0["pw"] + k - 1)
                act.activation(A["t2"][:, k % 2], A["t1"][:, k % 2], ACT.Silu, bias=col("ln_b", k))\
                   .then_inc(s("ln_s"), 1)
                act.wait_ge(s("ln_s"), k + 1)
                act.activation(yh[:, k], A["t2"][:, k % 2], ACT.Copy).then_inc(yh_ready, 1)
            for k in range(KB):
                down_tile(Tile(T_PW2 + k), k, "ff1")

            swiglu(1, T_FF1, "da")

            inv_rms("da", D)
            inv_rms_col(2)
            act.wait_ge(s("lam_s"), 1)
            act.activation(lamt[:, 1], ps[:, 6, 0:2], ACT.Exp).then_inc(s("lam_e"), 1)
            with act.Fori(0, 2) as r:
                for j in range(4):
                    split_hi(Tile(T_DV + j, r))

            def head_pair(i, before, fill):
                def exps(e, u):
                    n, p, kv = 4 * e + u, u % 2, (u + 1) * P
                    act.wait_ge(s("da_max"), i * 8 + (n + 1))
                    for c in (0, 1):
                        act.activation(A["ex"][:, p, c, 0:kv], ps[:, 2 + 2 * p + c, 0:kv], ACT.Exp,
                                       bias=A["nm"][:, p, c:c + 1], accum_out=A["sm"][:, p, c:c + 1])\
                           .then_inc(s("da_exp"), 1)

                def copy_T(e, u):
                    n, kv, at = 4 * e + u, (u + 1) * P, P * u * (u + 1) // 2
                    act.wait_ge(s("da_T"), i * 8 + (n + 1))
                    act.activation(A["aT"][:, at:at + kv], ps[:, 6, 0:kv], ACT.Copy).then_inc(s("da_aT"), 1)

                def out_square(e):
                    act.wait_ge(s("da_o"), i * 2 + (e + 1) + CREDIT)
                    act.activation(sq[:, 0], ps[:, 7], ACT.Square).then_inc(s("da_sq"), 1)

                def out_rms(done):
                    act.wait_ge(s("da_sum"), done)
                    act.activation(lnb[:], ps[:, 6], ACT.Ln, scale=1.0 / P, bias=EPS).then_inc(s("da_ln"), 1)
                    act.wait_ge(s("da_ln"), done)
                    act.activation(lnb[:], lnb[:], ACT.Exp, scale=-0.5).then_inc(s("da_rr"), 1)

                def out_hi(done, q):
                    act.wait_ge(s("da_ot"), done + CREDIT)
                    act.activation(block_of(yh, q), A["dot"][:], ACT.Copy, scale=1.0 - LAMBDA_INIT)\
                       .then_inc(yh_ready, 1)

                act.preload_act_table_set(LN_EXP)
                for e in (0, 1):
                    exps(e, 0)
                    if e or before:
                        out_rms(i * 2 + e)
                    exps(e, 1)
                    if e or before:
                        out_hi(i * 2 + e, i * 2 + (e - 1))
                    copy_T(e, 0)
                    exps(e, 2)
                    if fill:
                        split_hi(Tile(T_DA + 4 + 2 * e, i))
                    copy_T(e, 1)
                    exps(e, 3)
                    copy_T(e, 2)
                    copy_T(e, 3)
                    out_square(e)
                    if fill:
                        split_hi(Tile(T_DA + 4 + 2 * e + 1, i))
                if not fill:
                    out_rms(DA_HEADS)
                    out_hi(DA_HEADS, DA_HEADS - 1)

            for j in range(4):
                split_hi(Tile(T_DA + j))
            head_pair(0, False, True)
            with act.Fori(1, 3) as i:
                head_pair(i, True, True)
            head_pair(3, True, False)

            def to_m(t0, which, k0=0):
                for k in range(KB):
                    t = Tile(t0 + k)
                    act.wait_ge(evac_done, t.count)
                    square_block(which + "_post", k, A["m"][:, k])
                    split_hi(t)
                inv_rms(which + "_post", D)

            to_m(T_DO, "da")
            post_stage("da", "mlp0")

            def mlp(f, t0):
                name = f"mlp{f}"
                inv_rms(name, D)

                def up(g, i):
                    for j in range(4):
                        t = Tile(t0 + j, g * 4 + i)
                        act.wait_ge(evac_done, t.count)
                        act.activation(yh[:, bass.ds(i * 4 + j, 1)].rearrange("p a t -> p (a t)"), A["mr"][:, j % 2],
                                       ACT.Square).then_inc(yh_ready, 1)
                        split_hi(t)

                with act.Fori(0, MLP_GROUPS - 1) as g:
                    with act.Fori(0, 2) as i:
                        up(g, i)
                    with act.Fori(0, 2) as i:
                        for j in range(4):
                            split_hi(Tile(t0 + 8 + j, g * 4 + i))
                with act.Fori(0, 2) as i:
                    up(MLP_GROUPS - 1, i)
                to_m(t0 + 56, name)

            mlp(0, T_MLP0)
            post_stage("mlp0", "sc")

            inv_rms("sc", D)
            with act.Fori(0, 2) as i:
                for u in range(4):
                    for c in range(2):
                        split_hi(Tile(T_SC + 3 * u + c, i * 3))
                    act.wait_ge(s("sc_y"), i * 4 + (u + 1))
                    act.activation(yh[:, bass.ds(i * 4 + u, 1)].rearrange("p a t -> p (a t)"), A["cy"][:, u % 2],
                                   ACT.Copy).then_inc(yh_ready, 1)
                    split_hi(Tile(T_SC + 3 * u + 2, i * 3))
            to_m(T_SCO, "sc")
            post_stage("sc", "mlp1")
            mlp(1, T_MLP1)

        @block.vector
        def _(dve):
            def split_lo(t):
                if t.n + RING >= NT:
                    return
                a = t.plus(RING)
                dve.wait_ge(whi_ready, a.count)
                dve.tensor_tensor(wlo[:, a.slot], raw[:, a.slot], whi[:, a.slot].bitcast(F32), ALU.subtract)\
                   .then_inc(wlo_ready, 1)

            def pre_lo(name, k):
                dve.wait_ge(xh_ready, 8 * PRE[name] + k + 1)
                dve.scalar_tensor_tensor(xl[:, k], h[:, k], col("pre", 8 * PRE[name] + k), xh[:, k].bitcast(F32),
                                         ALU.mult, ALU.subtract).then_inc(x_ready, 1)

            def scaled(dst, t, bank):
                dve.wait_ge(tile_done, t.count)
                dve.tensor_tensor(dst, ps[:, bank], rrow[:], ALU.mult).then_inc(evac_done, 1)

            def post_norm(which):
                a = POST[which]
                following = {"da": "mlp0", "mlp0": "sc", "sc": "mlp1"}.get(which)
                dve.wait_ge(rrow_ready, SUM[which + "_post"] + 1)
                for k in range(KB):
                    q = 8 * a + k
                    if q >= 2:
                        dve.wait_ge(h_added, q - 1)
                    dve.scalar_tensor_tensor(A["pt"][:, k % 2], A["m"][:, k], col("post", q), rrow[:], ALU.mult,
                                             ALU.mult).then_inc(post_t, 1)
                    dve.wait_ge(post_t, q + 1)
                    dve.tensor_tensor(h[:, k], h[:, k], A["pt"][:, k % 2], ALU.add).then_inc(h_added, 1)
                    if following and k:
                        pre_lo(following, k - 1)
                if following:
                    pre_lo(following, KB - 1)

            dve.memset(A["glr"][0:32, :], 1.0).then_inc(s("glr_evac"), 1)
            dve.wait_ge(s("wglr_hi"), 1)
            dve.tensor_tensor(A["wgl"][:], A["wgr"][:], A["wgh"][:].bitcast(F32), ALU.subtract)\
               .then_inc(s("wglr_lo"), 1)
            dve.wait_ge(small_in[0], 16)
            for k in range(KB):
                pre_lo("hyb", k)
            for j in range(RING):
                dve.wait_ge(whi_ready, j + 1)
                dve.tensor_tensor(wlo[:, j], raw[:, j], whi[:, j].bitcast(F32), ALU.subtract).then_inc(wlo_ready, 1)
            dve.wait_ge(rrow_ready, 1)
            dve.wait_ge(s("glr_done"), 1)
            dve.wait_ge(s("glr_evac"), 1)
            dve.tensor_tensor(A["glr"][0:16, :], ps[0:16, 6], rrow[0:16, :], ALU.mult).then_inc(s("glr_evac"), 1)
            dve.wait_ge(rcol_ready, 1)
            dve.wait_ge(tile_done, 2)
            for t in range(TB):
                last = dve.tensor_scalar(A["gk"][:, t], ps[:, t, 0:256], rcol[:, t:t + 1], None, ALU.mult)
                if t % 2:
                    last.then_inc(evac_done, 1)
            split_lo(Tile(0))
            split_lo(Tile(1))
            for j in range(2):
                dve.wait_ge(tile_done, T_GQ + j + 1)
                dve.scalar_tensor_tensor(A["gq"][:, j], ps[:, 2 + j], 64 ** -0.5, rrow[:], ALU.mult, ALU.mult)\
                   .then_inc(evac_done, 1)
                split_lo(Tile(T_GQ + j))
            for n in range(T_GV, T_GR):
                split_lo(Tile(n))
            dve.wait_ge(s("gate_ln"), 1)
            dve.scalar_tensor_tensor(A["la"][:].rearrange("p t k -> p (t k)"), flat[:, 6 * 512:8 * 512], 0.0,
                                     A["gt"][:], ALU.min, ALU.subtract).then_inc(s("la_ready"), 1)
            dve.wait_ge(tile_done, T_GR)
            for t in range(TB):
                dve.tensor_scalar(A["gv"][:, t], ps[:, t], rcol[:, t:t + 1], None, ALU.mult).then_inc(evac_done, 1)
            dve.wait_ge(s("kd_ready"), 1)
            gkf = A["gk"][:].rearrange("p t k -> p (t k)")
            dve.tensor_tensor(gkf, gkf, A["gt"][:], ALU.mult).then_inc(s("kend_ready"), 1)
            for j in range(4):
                scaled(A["sr"][:, j], Tile(T_GR + j), j)
                split_lo(Tile(T_GR + j))
            for n in range(T_SV, T_SB):
                split_lo(Tile(n))
            dve.wait_ge(s("dec_ready"), 1)
            for n in range(8):
                if n % 2 == 0:
                    dve.wait_ge(s("upd_ready"), n // 2 + 1)
                for j in range(2):
                    u = 2 * (n // 2) + j
                    upd = ps[:, 4 + 2 * (n % 2) + u // 4, (u % 4) * P:(u % 4 + 1) * P]
                    if n == 0:
                        dve.tensor_copy(A["S"][:, n, j], upd).then_inc(s("state_ready"), 1)
                    else:
                        dve.wait_ge(s("state_ready"), 2 * (n - 1) + j + 1)
                        dve.scalar_tensor_tensor(A["S"][:, n, j], A["S"][:, n - 1, j], A["dec"][:, j, n:n + 1], upd,
                                                 ALU.mult, ALU.add).then_inc(s("state_ready"), 1)
            dve.wait_ge(tile_done, T_SB)
            for t in range(TB):
                dve.tensor_scalar(A["sv"][:, t], ps[:, t], rcol[:, t:t + 1], None, ALU.mult).then_inc(evac_done, 1)
            for hh in range(GLA_HEADS):
                dve.wait_ge(s("grr_ready"), hh + 1)
                dve.scalar_tensor_tensor(A["gv"][:, hh], ps[:, hh], col("gla"),
                                         A["S"][:, 2 * hh:2 * hh + 2].rearrange("p a j v -> p (a j v)"), ALU.mult,
                                         ALU.mult).then_inc(s("gt_ready"), 1)
                dve.wait_ge(s("gt_ready"), hh + 1)
                dve.wait_ge(s("row0"), 4)
                dve.tensor_tensor(A["gv"][:, hh], A["gv"][:, hh], A["sr"][:, hh], ALU.mult).then_inc(s("gy_ready"), 1)
            for hh in range(GLA_HEADS):
                dve.wait_ge(yh_ready, hh + 1)
                dve.wait_ge(s("gy_ready"), hh + 1)
                dve.tensor_tensor(yl[:, hh], A["gv"][:, hh], yh[:, hh].bitcast(F32), ALU.subtract).then_inc(y_ready, 1)

            with dve.Fori(0, 2) as i:
                def take(e, c):
                    n = 2 * e + c
                    scaled(A["sraw"][:, e, c], Tile(T_SB + n, i), c)
                    split_lo(Tile(T_SB + n, i))

                def norm_qk(e, c):
                    n = 2 * e + c
                    dve.wait_ge(s("sb_rr"), i * 4 + (n + 1) + CREDIT)
                    dve.wait_ge(evac_done, i * 4 + (T_SB + n + 1))
                    dve.scalar_tensor_tensor(A["sqn"][:, e, c], A["sraw"][:, e, c], col("sbk" if c else "sbq"),
                                             A["srr"][:, c], ALU.mult, ALU.mult).then_inc(s("sb_qn"), 1)

                def softplus(e, hh):
                    n, b = 2 * e + hh, 2 + 3 * hh
                    dve.wait_ge(s("sb_ln2"), i * 4 + (n + 1))
                    dve.scalar_tensor_tensor(A["sp"][:, hh], flat[:, b * 512:b * 512 + 1280], 0.0, A["sl"][:, hh],
                                             ALU.max, ALU.add).then_inc(s("sb_sp"), 1)

                def out_lo(e, hh):
                    n, b, r = 2 * e + hh, 2 + 3 * hh, slice(64 * hh, 64 * hh + 64)
                    dve.wait_ge(s("sb_yh"), i * 4 + (n + 1))
                    at = bass.ds(i * 2 + (4 + e), 1)
                    dve.tensor_tensor(yl[r, at].rearrange("p a t -> p (a t)"), ps[r, b],
                                      yh[r, at].rearrange("p a t -> p (a t)").bitcast(F32), ALU.subtract)\
                       .then_inc(s("sb_yl"), 1)

                take(0, 0)
                take(0, 1)
                norm_qk(0, 0)
                norm_qk(0, 1)
                take(1, 0)
                softplus(0, 0)
                take(1, 1)
                softplus(0, 1)
                norm_qk(1, 0)
                norm_qk(1, 1)
                out_lo(0, 0)
                out_lo(0, 1)
                softplus(1, 0)
                softplus(1, 1)
                out_lo(1, 0)
                out_lo(1, 1)

            def add_to_h(t, k, following, bias=None):
                dve.wait_ge(tile_done, t.count)
                if bias:
                    dve.scalar_tensor_tensor(h[:, k], ps[:, t.slot], col(bias, k), h[:, k], ALU.add, ALU.add)\
                       .then_inc(evac_done, 1)
                else:
                    dve.tensor_tensor(h[:, k], ps[:, t.slot], h[:, k], ALU.add).then_inc(evac_done, 1)
                if following:
                    dve.wait_ge(evac_done, t.count)
                    pre_lo(following, k)
                split_lo(t)

            for k in range(KB):
                add_to_h(Tile(T_WO + k), k, "ff0")

            def swiglu(f, t0, following):
                name = f"ff{f}"
                dve.wait_ge(rrow_ready, SUM[name] + 1)

                def up(g, i):
                    for u in (0, 1):
                        tg = Tile(t0 + 2 * u, g * 6 + i)
                        tu = tg.plus(1)
                        scaled(A["tg"][:, u], tg, tg.slot)
                        split_lo(tg)
                        scaled(A["tu"][:, u], tu, tu.slot)
                        done = g * 8 + i * 2 + (u + 1)
                        dve.wait_ge(s(name + "_silu"), done)
                        dve.wait_ge(evac_done, tu.count)
                        dve.tensor_tensor(A["th"][:, u], A["ts"][:, u], A["tu"][:, u], ALU.mult)\
                           .then_inc(s(name + "_hid"), 1)
                        dve.wait_ge(yh_ready, g * 8 + i * 2 + (yh0 + u + 1))
                        at = bass.ds(i * 2 + u, 1)
                        dve.wait_ge(s(name + "_hid"), done)
                        dve.tensor_tensor(yl[:, at].rearrange("p a t -> p (a t)"), A["th"][:, u],
                                          yh[:, at].rearrange("p a t -> p (a t)").bitcast(F32), ALU.subtract)\
                           .then_inc(y_ready, 1)
                        split_lo(tu)

                yh0 = Y0[name]
                with dve.Fori(0, 2) as g:
                    with dve.Fori(0, 4) as i:
                        up(g, i)
                    for k in range(KB):
                        add_to_h(Tile(t0 + 16 + k, g * 6), k, None)
                with dve.Fori(0, 3) as i:
                    up(2, i)
                for k in range(KB):
                    add_to_h(Tile(t0 + 60 + k), k, following)

            swiglu(0, T_FF0, "pw")

            dve.memset(A["ub"][:, :, 0:PAD], 0.0).then_inc(s("pw_zero"), 1)
            dve.wait_ge(rrow_ready, SUM["pw"] + 1)
            own = TAPS - TAPS_PE
            with dve.Fori(0, 4) as i:
                for u in (0, 1):
                    ta = Tile(T_PW1 + 2 * u, i)
                    scaled(A["t1"][:, u], ta, ta.slot)
                    split_lo(ta)
                    scaled(A["t2"][:, u], ta.plus(1), ta.slot + 1)
                    done = i * 2 + (u + 1)
                    dve.wait_ge(s("pw_sg"), done)
                    dve.wait_ge(evac_done, ta.count)
                    dve.wait_ge(s("pw_zero"), 1)
                    dve.scalar_tensor_tensor(A["ub"][:, u, PAD:], A["t1"][:, u],
                                             vec[:, bass.ds(i * 2 + (_cols["b_pw1"] + u), 1)], A["t3"][:, u],
                                             ALU.add, ALU.mult).then_inc(s("pw_u"), 1)
                    split_lo(ta.plus(1))
                    dve.wait_ge(s("pw_u"), done)
                    cvb = A["cv"][:, bass.ds(i * 2 + u, 1)].rearrange("p a t -> p (a t)")

                    def tap(k):
                        return vec[:, bass.ds(i * (2 * TAPS) + (_cols["w_dw"] + u * TAPS + k), 1)]

                    dve.tensor_scalar(cvb, A["ub"][:, u, TAPS_PE:TAPS_PE + T], tap(TAPS_PE),
                                      vec[:, bass.ds(i * 2 + (_cols["b_dw"] + u), 1)], ALU.mult, ALU.add)\
                       .then_inc(s("cv_chain"), 1)
                    for n in range(1, own):
                        k = TAPS_PE + n
                        dve.wait_ge(s("cv_chain"), i * (2 * own) + (u * own + n))
                        dve.scalar_tensor_tensor(cvb, A["ub"][:, u, k:k + T], tap(k), cvb, ALU.mult, ALU.add)\
                           .then_inc(s("cv_chain"), 1)
                    dve.wait_ge(s("cv_chain"), i * (2 * own) + (u * own + own))
                    dve.wait_ge(s("cv_pe"), done + CREDIT)
                    dve.tensor_tensor(cvb, ps[:, 5 + u], cvb, ALU.add).then_inc(s("cv_done"), 1)
            dve.wait_ge(s("mu_sum"), 1)
            dve.wait_ge(s("cv_done"), KB)
            dve.tensor_scalar(A["mu"][:], ps[:, 7], 1.0 / D, None, ALU.mult).then_inc(s("mu_copied"), 1)
            dve.wait_ge(s("mu_copied"), 1)
            for k in range(KB):
                dve.tensor_tensor(A["cv"][:, k], A["cv"][:, k], A["mu"][:], ALU.subtract).then_inc(s("cen_ready"), 1)
            dve.wait_ge(rrow_ready, SUM["lnvar"] + 1)

            def ln_lo(k):
                dve.wait_ge(yh_ready, Y0["pw"] + k + 1)
                dve.tensor_tensor(yl[:, k], A["t2"][:, k % 2], yh[:, k].bitcast(F32), ALU.subtract).then_inc(y_ready, 1)

            for k in range(KB):
                dve.wait_ge(s("cen_ready"), k + 1)
                if k >= 2:
                    dve.wait_ge(s("ln_s"), k - 1)
                dve.scalar_tensor_tensor(A["t1"][:, k % 2], A["cv"][:, k], col("ln_g", k), rrow[:], ALU.mult,
                                         ALU.mult).then_inc(s("ln_t"), 1)
                if k:
                    ln_lo(k - 1)
            ln_lo(KB - 1)
            for k in range(KB):
                add_to_h(Tile(T_PW2 + k), k, "ff1", "b_pw2")

            swiglu(1, T_FF1, "da")

            a = _cols["lam"]
            dve.tensor_tensor(lamt[:, 0], vec[:, a:a + 4:2], vec[:, a + 1:a + 4:2], ALU.mult).then_inc(s("lam_p"), 1)
            dve.wait_ge(s("lam_e"), 1)
            dve.scalar_tensor_tensor(nlam[:], lamt[:, 1, 1:2], -LAMBDA_INIT, lamt[:, 1, 0:1], ALU.add, ALU.subtract)\
               .then_inc(s("lam_ready"), 1)
            dve.wait_ge(rrow_ready, SUM["da"] + 1)
            dve.wait_ge(rcol_ready, 2)
            with dve.Fori(0, 2) as r:
                for j in range(4):
                    split_lo(Tile(T_DV + j, r))
                dve.wait_ge(tile_done, r * 4 + (T_DV + 4))
                for t in range(TB):
                    dve.tensor_scalar(A["dv"][:, t, bass.ds(r * 512, 512)], ps[:, t], rcol[:, t:t + 1], None, ALU.mult)\
                       .then_inc(evac_done, 1)
            swap = [d ^ 8 if d < 16 else d for d in range(32)]

            def rope(c, t, done):
                dve.wait_ge(tile_done, t.count)
                if not isinstance(done, int) or done > 2:
                    dve.wait_ge(s("da_qn"), done - 2 + CREDIT)
                dve.scalar_tensor_tensor(A["draw"][:, c], ps[:, c], 1.0 if c else 64 ** -0.5, rrow[:], ALU.mult,
                                         ALU.mult).then_inc(evac_done, 1)
                dve.wait_ge(s("lam_ready"), 1)
                dve.wait_ge(evac_done, t.count)
                dve.stream_shuffle(A["dsh"][:, c], A["draw"][:, c], swap).then_inc(s("da_sh"), 1)
                dve.wait_ge(s("da_sh"), done)
                dve.tensor_tensor(A["dsh"][:, c], A["dsh"][:, c], cst("sin"), ALU.mult).then_inc(s("da_shs"), 1)
                split_lo(t)

            def head_pair(i, before, fill):
                def row_max(e, u):
                    n, p, kv = 4 * e + u, u % 2, (u + 1) * P
                    dve.wait_ge(s("da_s"), i * 8 + (n + 1))
                    dve.reduce_max(A["nm"][:, p], ps[:, 2 + 2 * p:4 + 2 * p, 0:kv], AX.X, negate=True)\
                       .then_inc(s("da_max"), 1)

                def combine(e, u):
                    n, p, kv = 4 * e + u, u % 2, (u + 1) * P
                    done = i * 8 + (n + 1)
                    dve.wait_ge(s("da_exp"), i * 16 + 2 * (n + 1) + CREDIT)
                    dve.reciprocal(A["rc"][:, p], A["sm"][:, p]).then_inc(s("da_rcp"), 1)
                    dve.wait_ge(s("da_rcp"), done)
                    dve.tensor_tensor(A["r1"][:, p], A["rc"][:, p, 1:2], nlam[:], ALU.mult).then_inc(s("da_r1"), 1)
                    dve.wait_ge(s("da_r1"), done)
                    dve.tensor_scalar(acc[:, 0:kv], A["ex"][:, p, 1, 0:kv], A["r1"][:, p], None, ALU.mult)\
                       .then_inc(s("da_t"), 1)
                    dve.wait_ge(s("da_t"), done)
                    dve.scalar_tensor_tensor(A["da"][:, p, 0:kv], A["ex"][:, p, 0, 0:kv], A["rc"][:, p, 0:1],
                                             acc[:, 0:kv], ALU.mult, ALU.add).then_inc(s("da_a"), 1)

                def out(done):
                    dve.wait_ge(s("da_rr"), done + CREDIT)
                    dve.scalar_tensor_tensor(A["dot"][:], ps[:, 7], col("subln"), lnb[:], ALU.mult, ALU.mult)\
                       .then_inc(s("da_ot"), 1)

                def out_lo(done, q):
                    dve.wait_ge(s("da_ot"), done + CREDIT)
                    dve.wait_ge(yh_ready, done + Y0["da"])
                    dve.scalar_tensor_tensor(block_of(yl, q), A["dot"][:], 1.0 - LAMBDA_INIT,
                                             block_of(yh, q).bitcast(F32), ALU.mult, ALU.subtract)\
                       .then_inc(y_ready, 1)

                for e in (0, 1):
                    row_max(e, 0)
                    row_max(e, 1)
                    if e or before:
                        out(i * 2 + e)
                    combine(e, 0)
                    row_max(e, 2)
                    if e or before:
                        out_lo(i * 2 + e, i * 2 + (e - 1))
                    combine(e, 1)
                    if fill:
                        rope(0, Tile(T_DA + 4 + 2 * e, i), i * 4 + (4 + 2 * e + 1))
                    row_max(e, 3)
                    combine(e, 2)
                    combine(e, 3)
                    if fill:
                        rope(1, Tile(T_DA + 4 + 2 * e + 1, i), i * 4 + (4 + 2 * e + 2))
                if not fill:
                    out(DA_HEADS)
                    out_lo(DA_HEADS, DA_HEADS - 1)

            for n in range(4):
                rope(n % 2, Tile(T_DA + n), n + 1)
            head_pair(0, False, True)
            with dve.Fori(1, 3) as i:
                head_pair(i, True, True)
            head_pair(3, True, False)

            def add_to_m(t, k):
                dve.wait_ge(tile_done, t.count)
                dve.tensor_tensor(A["m"][:, k] if isinstance(k, int) else A["m"][:, k].rearrange("p a t -> p (a t)"),
                                  ps[:, t.slot],
                                  A["m"][:, k] if isinstance(k, int) else A["m"][:, k].rearrange("p a t -> p (a t)"),
                                  ALU.add).then_inc(evac_done, 1)
                split_lo(t)

            def set_m(t, k):
                dve.wait_ge(tile_done, t.count)
                dve.tensor_copy(A["m"][:, k], ps[:, t.slot]).then_inc(evac_done, 1)
                split_lo(t)

            for k in range(KB):
                set_m(Tile(T_DO + k), k)
            post_norm("da")

            def mlp(f, t0):
                name = f"mlp{f}"
                yh0 = Y0[name]
                dve.memset(A["m"][:], 0.0).then_inc(s("m_zero"), 1)
                dve.wait_ge(rrow_ready, SUM[name] + 1)

                def up(g, i):
                    for j in range(4):
                        t = Tile(t0 + j, g * 4 + i)
                        dve.wait_ge(tile_done, t.count)
                        dve.scalar_tensor_tensor(A["mr"][:, j % 2], ps[:, t.slot], 0.0, rrow[:], ALU.max, ALU.mult)\
                           .then_inc(evac_done, 1)
                        dve.wait_ge(evac_done, t.count)
                        dve.tensor_tensor(A["mh"][:, j % 2], A["mr"][:, j % 2], A["mr"][:, j % 2], ALU.mult)\
                           .then_inc(s(name + "_hid"), 1)
                        done = g * 8 + i * 4 + (j + 1)
                        dve.wait_ge(s(name + "_hid"), done)
                        dve.wait_ge(yh_ready, g * 8 + i * 4 + (yh0 + j + 1))
                        at = bass.ds(i * 4 + j, 1)
                        dve.tensor_tensor(yl[:, at].rearrange("p a t -> p (a t)"), A["mh"][:, j % 2],
                                          yh[:, at].rearrange("p a t -> p (a t)").bitcast(F32), ALU.subtract)\
                           .then_inc(y_ready, 1)
                        split_lo(t)

                with dve.Fori(0, MLP_GROUPS - 1) as g:
                    with dve.Fori(0, 2) as i:
                        up(g, i)
                    dve.wait_ge(s("m_zero"), f + 1)
                    with dve.Fori(0, 2) as i:
                        for j in range(4):
                            add_to_m(Tile(t0 + 8 + j, g * 4 + i), bass.ds(i * 4 + j, 1))
                with dve.Fori(0, 2) as i:
                    up(MLP_GROUPS - 1, i)
                for k in range(KB):
                    add_to_m(Tile(t0 + 56 + k), k)
                post_norm(name)

            mlp(0, T_MLP0)

            dve.memset(A["uc"][:, :, 0:2], 0.0).then_inc(s("sc_zero"), 1)
            dve.wait_ge(rrow_ready, SUM["sc"] + 1)
            with dve.Fori(0, 2) as i:
                for u in range(4):
                    for c, dst in enumerate(("cb", "cc", "cx")):
                        t = Tile(T_SC + 3 * u + c, i * 3)
                        scaled(A[dst][:, u % 2], t, t.slot)
                        if c < 2:
                            split_lo(t)
                    dve.wait_ge(evac_done, t.count)
                    dve.wait_ge(s("sc_zero"), 1)
                    uc, cy = A["uc"][:, u % 2], A["cy"][:, u % 2]
                    at = i * 16 + 4 * u
                    dve.tensor_tensor(uc[:, 2:], A["cc"][:, u % 2], A["cx"][:, u % 2], ALU.mult).then_inc(s("sc_u"), 1)
                    for k in range(3):
                        dve.wait_ge(s("sc_u"), at + (k + 1))
                        w = vec[:, bass.ds(i * 12 + (_cols["conv_w"] + 3 * u + k), 1)]
                        if k == 0:
                            dve.tensor_scalar(cy, uc[:, 0:T], w, None, ALU.mult).then_inc(s("sc_u"), 1)
                        else:
                            dve.scalar_tensor_tensor(cy, uc[:, k:k + T], w, cy, ALU.mult, ALU.add)\
                               .then_inc(s("sc_u"), 1)
                    dve.wait_ge(s("sc_u"), at + 4)
                    dve.tensor_tensor(cy, cy, A["cb"][:, u % 2], ALU.mult).then_inc(s("sc_y"), 1)
                    dve.wait_ge(yh_ready, i * 4 + (Y0["sc"] + u + 1))
                    dve.wait_ge(s("sc_y"), i * 4 + (u + 1))
                    yat = bass.ds(i * 4 + u, 1)
                    dve.tensor_tensor(yl[:, yat].rearrange("p a t -> p (a t)"), cy,
                                      yh[:, yat].rearrange("p a t -> p (a t)").bitcast(F32), ALU.subtract)\
                       .then_inc(y_ready, 1)
                    split_lo(t)
            for k in range(KB):
                set_m(Tile(T_SCO + k), k)
            post_norm("sc")
            mlp(1, T_MLP1)

        @block.gpsimd
        def _(pool):
            def sum_squares(name):
                for k in range(KB - 1):
                    pool.wait_ge(sq_ready, (SUM[name] - (SUM[name] > 3)) * KB + k + 1)
                    if k == 0:
                        if SUM[name]:
                            pool.wait_ge(sum_ready, SUM[name])
                            pool.wait_ge(acc_ready, ACC[name])
                        pool.tensor_copy(acc[:], sq[:, 0]).then_inc(acc_ready, 1)
                    else:
                        pool.wait_ge(acc_ready, ACC[name] + k)
                        pool.tensor_tensor(acc[:], acc[:], sq[:, k % 2], ALU.add).then_inc(acc_ready, 1)

            sum_squares("hyb")
            with pool.Fori(0, 2) as i:
                def stage(e):
                    if e == 0:
                        pool.wait_ge(s("sb_o"), i * 4 + CREDIT)
                    else:
                        pool.wait_ge(s("sb_o"), i * 4 + 1 + CREDIT)
                    pool.wait_ge(evac_done, T_SB)
                    pool.wait_ge(y_ready, GLA_HEADS)
                    pool.tensor_copy(A["vp"][:, e], A["sv"][:, :, bass.ds(i * 256 + e * 128, P)]).then_inc(s("sb_vp"), 1)

                def mask(e, hh):
                    n = 2 * e + hh
                    pool.wait_ge(s("sb_sp"), i * 4 + (n + 1))
                    for r in (0, 512, 896, 1024):
                        last = pool.tensor_tensor(A["sp"][:, hh, r:r + P], A["sp"][:, hh, r:r + P], cst("mask_sb"),
                                                  ALU.mult)
                    last.then_inc(s("sb_mask"), 1)

                stage(0)
                mask(0, 0)
                mask(0, 1)
                stage(1)
                mask(1, 0)
                mask(1, 1)
            sum_squares("ff0")
            sum_squares("pw")
            with pool.Fori(0, 4) as i:
                for u in (0, 1):
                    pool.wait_ge(s("cv_pe"), i * 2 + CREDIT)
                    pool.tensor_copy(A["wt"][:, u], vec[:, bass.ds(i * (2 * TAPS) + (_cols["w_dw"] + u * TAPS), TAPS_PE)])\
                        .then_inc(s("wt_ready"), 1)
                    pool.wait_ge(s("wt_ready"), i * 2 + (u + 1))
                    shape = [P, TAPS_PE, P]
                    last = pool.tensor_tensor(A["dg"][:, u], cst("ident").unsqueeze(1).to_broadcast(shape),
                                              A["wt"][:, u].unsqueeze(2).to_broadcast(shape), ALU.mult)
                    last.then_inc(s("dg_ready"), 1)
            pool.wait_ge(s("cv_done"), 1)
            pool.tensor_copy(A["mu"][:], A["cv"][:, 0]).then_inc(s("mu_acc"), 1)
            for k in range(1, KB - 1):
                pool.wait_ge(s("cv_done"), k + 1)
                pool.wait_ge(s("mu_acc"), k)
                pool.tensor_tensor(A["mu"][:], A["mu"][:], A["cv"][:, k], ALU.add).then_inc(s("mu_acc"), 1)
            sum_squares("ff1")
            sum_squares("da")

            def stage(pair, e):
                if not isinstance(pair, int) or pair:
                    pool.wait_ge(s("da_o"), pair * 2 + (e - 1) + CREDIT)
                pool.wait_ge(evac_done, T_DA)
                pool.tensor_copy(A["vh"][:, e], A["dv"][:, :, bass.ds(pair * 256 + e * 128, P)])\
                    .then_inc(s("da_vh"), 1)

            def rotated(pair, e, c):
                done = pair * 4 + (2 * e + c + 1)
                if not isinstance(pair, int) or pair:
                    pool.wait_ge(s("da_s"), pair * 8 + (4 * e - 4))
                pool.wait_ge(evac_done, done + T_DA)
                pool.tensor_tensor(A["dq"][:, e, c], A["draw"][:, c], cst("cos"), ALU.mult).then_inc(s("da_rc"), 1)
                pool.wait_ge(s("da_rc"), done)
                pool.wait_ge(s("da_shs"), done)
                pool.tensor_tensor(A["dq"][:, e, c], A["dq"][:, e, c], A["dsh"][:, c], ALU.add)\
                    .then_inc(s("da_qn"), 1)

            def pair_inputs(pair):
                for e in (0, 1):
                    rotated(pair, e, 0)
                    rotated(pair, e, 1)
                    stage(pair, e)

            pair_inputs(0)
            with pool.Fori(1, 4) as pair:
                pair_inputs(pair)
            for name in ("da_post", "mlp0", "mlp0_post", "sc", "sc_post", "mlp1", "mlp1_post"):
                sum_squares(name)

        @block.tensor
        def _(pe):
            def passes(out, t_hi, t_lo, a_hi, a_lo, first, last, stationary_is_weight=True):
                w = ((t_hi, a_hi), (t_hi, a_lo), (t_lo, a_hi))
                for n, (wt, ac) in enumerate(w):
                    lhs, rhs = (wt, ac) if stationary_is_weight else (ac, wt)
                    mm = pe.matmul(out, lhs, rhs, start=first and n == 0, stop=last and n == 2)
                return mm

            def tile(t, bank, hi, lo, ready=None, base=0, blocks=KB, free=None):
                pe.wait_ge(wlo_ready, t.count)
                if free is None:
                    if t.n >= RING:
                        pe.wait_ge(evac_done, t.count - RING)
                else:
                    pe.wait_ge(evac_done, free)
                w_h = whi[:, t.slot].rearrange("p (k n) -> p k n", k=KB)
                w_l = wlo[:, t.slot].rearrange("p (k n) -> p k n", k=KB)
                for k in range(blocks):
                    if ready is not None:
                        pe.wait_ge(ready, base + (k + 1))
                    mm = passes(ps[:, bank], w_h[:, k], w_l[:, k], hi[:, k], lo[:, k], k == 0, k == blocks - 1)
                mm.then_inc(tile_done, 1)

            def part(t, bank, hi, lo, blocks, free=None, ready=None, base=0):
                if blocks[0] == 0:
                    pe.wait_ge(wlo_ready, t.count)
                    if free is not None:
                        pe.wait_ge(evac_done, free)
                w_h = whi[:, t.slot].rearrange("p (k n) -> p k n", k=KB)
                w_l = wlo[:, t.slot].rearrange("p (k n) -> p k n", k=KB)
                for k in blocks:
                    if ready is not None:
                        pe.wait_ge(ready, base + (k + 1))
                    mm = passes(ps[:, bank], w_h[:, k], w_l[:, k], hi[:, k], lo[:, k], k == 0, k == KB - 1)
                if blocks[-1] == KB - 1:
                    mm.then_inc(tile_done, 1)

            def wide(t, j, rows, cols):
                pe.wait_ge(wlo_ready, t.count)
                w_h = whi[:, t.slot].rearrange("p (k n) -> p k n", k=rows)
                w_l = wlo[:, t.slot].rearrange("p (k n) -> p k n", k=rows)
                for tb in range(TB):
                    tok = slice(tb * P, (tb + 1) * P)
                    for k in range(rows):
                        kk = j * rows + k
                        mm = passes(ps[:, tb, 0:cols], w_h[:, k], w_l[:, k], xh[:, kk, tok], xl[:, kk, tok],
                                    kk == 0, kk == KB - 1, stationary_is_weight=False)
                mm.then_inc(tile_done, 1)

            def row_sum(name):
                pe.wait_ge(acc_ready, ACC[name] + KB - 1)
                pe.matmul(ps[:, 4], cst("ones"), acc[:], start=True, stop=False)
                pe.wait_ge(sq_ready, (SUM[name] - (SUM[name] > 3) + 1) * KB)
                pe.matmul(ps[:, 4], cst("ones"), sq[:, 1], start=False, stop=True).then_inc(sum_ready, 1)

            def col_sum(name):
                pe.wait_ge(acc_ready, ACC[name] + KB - 1)
                pe.wait_ge(sq_ready, (SUM[name] - (SUM[name] > 3) + 1) * KB)
                for tb in range(TB):
                    tok = slice(tb * P, (tb + 1) * P)
                    pe.matmul(ps[:, 5, tb:tb + 1], acc[:, tok], cst("ones", cols=1), start=True, stop=False)
                    mm = pe.matmul(ps[:, 5, tb:tb + 1], sq[:, 1, tok], cst("ones", cols=1), start=False, stop=True)
                mm.then_inc(colsum_ready, 1)

            def first_round(t0, hi, lo, ready, base, blocks=KB):
                pe.wait_ge(wlo_ready, t0.plus(FIRST - 1).count)
                pe.wait_ge(evac_done, t0.count - 1)
                for k in range(blocks):
                    pe.wait_ge(ready, base + (k + 1))
                    for j in range(FIRST):
                        w_h = whi[:, j].rearrange("p (k n) -> p k n", k=KB)
                        w_l = wlo[:, j].rearrange("p (k n) -> p k n", k=KB)
                        mm = passes(ps[:, j], w_h[:, k], w_l[:, k], hi[:, k], lo[:, k], k == 0, k == blocks - 1)
                        if k == blocks - 1:
                            mm.then_inc(tile_done, 1)

            pe.wait_ge(s("wglr_lo"), 1)
            g_h = A["wgh"][:].rearrange("p (k n) -> p k n", k=KB)
            g_l = A["wgl"][:].rearrange("p (k n) -> p k n", k=KB)
            for k in range(KB):
                pe.wait_ge(x_ready, k + 1)
                mm = passes(ps[:, 6], g_h[:, k], g_l[:, k], xh[:, k], xl[:, k], k == 0, k == KB - 1)
            mm.then_inc(s("glr_done"), 1)
            pe.wait_ge(small_in[1], 16)
            col_sum("hyb")
            row_sum("hyb")
            wide(Tile(0), 0, 4, 256)
            wide(Tile(1), 1, 4, 256)
            tile(Tile(2), 2, xh, xl, free=2)
            tile(Tile(3), 3, xh, xl, free=2)
            pe.wait_ge(s("glr_evac"), 2)
            pe.wait_ge(small_in[2], 16)
            for tb in range(TB):
                mm = pe.matmul(ps[:, 6 + tb // 2, (tb % 2) * 256:(tb % 2 + 1) * 256], A["glr"][0:17, tb * P:(tb + 1) * P],
                               A["wg2"][0:17, :], start=True, stop=True)
            mm.then_inc(s("gate_x"), 1)
            pe.wait_ge(evac_done, T_GV)
            for j in range(4):
                wide(Tile(T_GV + j), j, 2, 512)
            pe.wait_ge(s("la_ready"), 1)
            pe.wait_ge(rcol_ready, 1)
            pe.wait_ge(rrow_ready, 1)
            for tb in range(TB):
                pe.matmul(ps[:, 4 + tb // 2, (tb % 2) * 256:(tb % 2 + 1) * 256], cst("later64"), A["la"][:, tb],
                          start=True, stop=True)
            for j in range(2):
                for tb in range(TB):
                    mm = pe.matmul(ps[:, 6, j * 8 + 2 * tb:j * 8 + 2 * tb + 2], A["la"][:, tb, j * P:(j + 1) * P],
                                   cst("chunk"), start=True, stop=True)
            mm.then_inc(s("suf_ready"), 1)
            for j in range(4):
                tile(Tile(T_GR + j), j, xh, xl)
            pe.wait_ge(s("kend_ready"), 1)
            pe.wait_ge(s("dec_ready"), 1)
            for tb in range(TB):
                for c in range(2):
                    tok = slice(64 * c, 64 * c + 64)
                    for j in range(2):
                        u = 2 * tb + j
                        for e in range(2):
                            hd = 2 * j + e
                            mm = pe.matmul(ps[64 * e:64 * e + 64, 4 + 2 * c + u // 4, (u % 4) * P:(u % 4 + 1) * P],
                                           A["gk"][tok, tb, hd * 64:hd * 64 + 64], A["gv"][tok, tb, hd * P:(hd + 1) * P],
                                           start=True, stop=True)
                            mm_last = mm
            mm_last.then_inc(s("upd_ready"), 4)
            pe.wait_ge(evac_done, T_SV)
            for j in range(4):
                wide(Tile(T_SV + j), j, 2, 512)
            pe.wait_ge(evac_done, T_SB)
            pe.wait_ge(s("state_ready"), 16)
            for hd in range(GLA_HEADS):
                j, r = hd // 2, slice(64 * (hd % 2), 64 * (hd % 2) + 64)
                for n in range(8):
                    tok = slice(n * 64, n * 64 + 64)
                    mm = pe.matmul(ps[:, hd, tok], A["S"][r, n, j], A["gq"][r, j, tok], start=True, stop=True)
                mm.then_inc(s("go_ready"), 1)
            for hd in range(GLA_HEADS):
                pe.wait_ge(s("gsq_ready"), hd + 1)
                pe.matmul(ps[:, 4 + hd], cst("ones"), A["gt"][:, (hd % 2) * T:(hd % 2 + 1) * T], start=True, stop=True)\
                  .then_inc(s("gsum_ready"), 1)

            start_of = {0: 0, 1: 512, 2: 1024, 3: 896}
            pe.wait_ge(y_ready, 4)
            with pe.Fori(0, 2) as i:
                def qk_tile(e, c):
                    n = 2 * e + c
                    pe.wait_ge(s("sb_rr"), i * 4 + max(n - 1, 0) + CREDIT)
                    if n == 1:
                        pass
                    tile(Tile(T_SB + n, i), c, xh, xl, free=i * 4 + (T_SB + n - 1))

                def qk_sum(e, c):
                    n = 2 * e + c
                    pe.wait_ge(s("sb_sq"), i * 4 + (n + 1))
                    pe.matmul(ps[:, c], cst("blk64"), A["ssq"][:, c], start=True, stop=True).then_inc(s("sb_sum"), 1)

                def scores(e, hh):
                    n, b, r = 2 * e + hh, 2 + 3 * hh, slice(64 * hh, 64 * hh + 64)
                    pe.wait_ge(s("sb_qn"), i * 4 + (2 * e + 2) + CREDIT)
                    if n >= 2:
                        pe.wait_ge(s("sb_yl"), i * 4 + (n - 1) + CREDIT)
                    else:
                        pe.wait_ge(s("sb_yl"), i * 4 + CREDIT)
                    for kb in (0, 1, 3, 2):
                        a, w = start_of[kb], 512 - kb * P
                        mm = pe.matmul(flat[:, b * 512 + a:b * 512 + a + w], A["sqn"][r, e, 1, kb * P:(kb + 1) * P],
                                       A["sqn"][r, e, 0, kb * P:512], start=kb != 3, stop=True, skip_group_check=True)
                    mm.then_inc(s("sb_z"), 1)

                def accumulate(e, hh):
                    n, b = 2 * e + hh, 2 + 3 * hh
                    pe.wait_ge(s("sb_mask"), i * 4 + (n + 1))
                    for kb in range(TB):
                        a, w = b * 512 + start_of[kb], 512 - kb * P
                        for k2 in range(kb, TB):
                            off, w2 = (k2 - kb) * P, 512 - k2 * P
                            pe.matmul(flat[:, a + off:a + off + w2], cst("negtri" if k2 == kb else "negones"),
                                      A["sp"][:, hh, start_of[k2]:start_of[k2] + w2], start=False, stop=True,
                                      skip_group_check=True)
                        mm = pe.matmul(flat[:, a:a + P], cst("ident"), cst("neg_sb"), start=False, stop=True,
                                       skip_group_check=True)
                    mm.then_inc(s("sb_acc"), 1)

                def values(e, hh):
                    n, b, r = 2 * e + hh, 2 + 3 * hh, slice(64 * hh, 64 * hh + 64)
                    pe.wait_ge(s("sb_w"), i * 4 + (n + 1))
                    pe.wait_ge(s("sb_vp"), i * 2 + (e + 1))
                    for kb in range(TB):
                        a, w = start_of[kb], 512 - kb * P
                        mm = pe.matmul(ps[r, b, kb * P:512], A["vp"][:, e, kb, r], A["sl"][:, hh, a:a + w],
                                       start=kb == 0, stop=kb == TB - 1)
                    mm.then_inc(s("sb_o"), 1)

                qk_tile(0, 0)
                qk_tile(0, 1)
                qk_sum(0, 0)
                qk_sum(0, 1)
                scores(0, 0)
                scores(0, 1)
                qk_tile(1, 0)
                qk_tile(1, 1)
                accumulate(0, 0)
                accumulate(0, 1)
                qk_sum(1, 0)
                qk_sum(1, 1)
                values(0, 0)
                values(0, 1)
                scores(1, 0)
                scores(1, 1)
                accumulate(1, 0)
                accumulate(1, 1)
                values(1, 0)
                values(1, 1)

            pe.wait_ge(s("sb_yl"), SB_HEADS + CREDIT)
            pe.wait_ge(s("sb_rr"), SB_HEADS + CREDIT)
            for k in range(KB):
                tile(Tile(T_WO + k), k % RING, yh, yl)

            def down(t, y, blocks=KB):
                for j in range(KB):
                    tile(t.plus(j), j % RING, yh, yl, y_ready, y, blocks=blocks)

            def swiglu(f, t0, y0):
                name = f"ff{f}"
                tile(Tile(t0), 0, xh, xl, x_ready, 8 * PRE[name])
                row_sum(name)
                for j in range(1, RING):
                    tile(Tile(t0 + j), j, xh, xl)

                def up(t):
                    for j in range(RING):
                        tile(t.plus(j), j, xh, xl)

                with pe.Fori(1, 4) as i:
                    up(Tile(t0, i))
                down(Tile(t0 + 16), y0)
                with pe.Fori(0, 4) as i:
                    up(Tile(t0 + 24, i))
                down(Tile(t0 + 40), y0 + 8)
                with pe.Fori(0, 3) as i:
                    up(Tile(t0 + 48, i))
                down(Tile(t0 + 60), y0 + 16, FF_GROUPS[2])

            swiglu(0, T_FF0, Y0["ff0"])

            def conv(i, u):
                pe.wait_ge(s("dg_ready"), i * 2 + (u + 1))
                pe.wait_ge(s("pw_u"), i * 2 + (u + 1))
                if u or not isinstance(i, int):
                    pe.wait_ge(s("cv_done"), i * 2 + (u - 1))
                for k in range(TAPS_PE):
                    mm = pe.matmul(ps[:, 5 + u], A["dg"][:, u, k], A["ub"][:, u, k:k + T], start=k == 0,
                                   stop=k == TAPS_PE - 1)
                mm.then_inc(s("cv_pe"), 1)

            tile(Tile(T_PW1), 0, xh, xl, x_ready, 8 * PRE["pw"])
            row_sum("pw")
            tile(Tile(T_PW1 + 1), 1, xh, xl)
            tile(Tile(T_PW1 + 2), 2, xh, xl)
            conv(0, 0)
            tile(Tile(T_PW1 + 3), 3, xh, xl)
            with pe.Fori(1, 4) as i:
                tile(Tile(T_PW1, i), 0, xh, xl)
                conv(i - 1, 1)
                tile(Tile(T_PW1 + 1, i), 1, xh, xl)
                tile(Tile(T_PW1 + 2, i), 2, xh, xl)
                conv(i, 0)
                tile(Tile(T_PW1 + 3, i), 3, xh, xl)
            conv(3, 1)
            pe.wait_ge(s("mu_acc"), KB - 1)
            pe.matmul(ps[:, 7], cst("ones"), A["mu"][:], start=True, stop=False)
            pe.wait_ge(s("cv_done"), KB)
            pe.matmul(ps[:, 7], cst("ones"), A["cv"][:, KB - 1], start=False, stop=True).then_inc(s("mu_sum"), 1)
            for k in range(KB):
                pe.wait_ge(s("cen_sq"), k + 1)
                mm = pe.matmul(ps[:, 4], cst("ones"), sq[:, k % 2], start=k == 0, stop=k == KB - 1)
                if k < KB - 1:
                    mm.then_inc(s("var_mm"), 1)
            mm.then_inc(sum_ready, 1)
            first_round(Tile(T_PW2), yh, yl, y_ready, Y0["pw"])
            for j in range(FIRST, KB):
                tile(Tile(T_PW2 + j), j % RING, yh, yl)

            swiglu(1, T_FF1, Y0["ff1"])

            pe.wait_ge(s("lam_p"), 1)
            pe.matmul(ps[:, 6, 0:2], cst("ones"), lamt[:, 0], start=True, stop=True).then_inc(s("lam_s"), 1)
            pe.wait_ge(x_ready, 8 * PRE["da"] + 8)
            col_sum("da")
            row_sum("da")
            with pe.Fori(0, 2) as r:
                pe.wait_ge(evac_done, r * 4 + T_DV)
                for j in range(4):
                    wide(Tile(T_DV + j, r), j, 2, 512)
            pe.wait_ge(evac_done, T_DA)
            pe.wait_ge(rrow_ready, SUM["da"] + 1)
            pe.wait_ge(rcol_ready, 2)

            def head_pair(i, before, fill):
                def scores(e, u):
                    n, p, kv = 4 * e + u, u % 2, (u + 1) * P
                    pe.wait_ge(s("da_qn"), i * 4 + (2 * e + 2) + CREDIT)
                    if n >= 2:
                        pe.wait_ge(s("da_exp"), i * 16 + 2 * (n - 1) + CREDIT)
                    else:
                        pe.wait_ge(s("da_exp"), i * 16 + CREDIT)
                    for c in (0, 1):
                        r, b = slice(64 * c, 64 * c + 64), 2 + 2 * p + c
                        pe.matmul(ps[:, b, 0:kv], A["dq"][r, e, 0, u * P:(u + 1) * P], A["dq"][r, e, 1, 0:kv],
                                  start=True, stop=True)
                        mm = pe.matmul(ps[:, b, kv - P:kv], cst("ident"), cst("neg_da"), start=False, stop=True,
                                       skip_group_check=True)
                    mm.then_inc(s("da_s"), 1)

                def transposes(e, u):
                    n = 4 * e + u
                    pe.wait_ge(s("da_a"), i * 8 + (n + 1))
                    pe.wait_ge(s("da_aT"), i * 8 + n + CREDIT)
                    if u == 0:
                        pe.wait_ge(s("da_rr"), i * 2 + e + CREDIT)
                    for b in range(u + 1):
                        mm = pe.transpose(ps[:, 6, b * P:(b + 1) * P], A["da"][:, u % 2, b * P:(b + 1) * P], cst("ident"))
                    mm.then_inc(s("da_T"), 1)

                def values(e, u):
                    n, at = 4 * e + u, P * u * (u + 1) // 2
                    pe.wait_ge(s("da_aT"), i * 8 + (n + 1) + CREDIT)
                    if u == 0:
                        pe.wait_ge(s("da_vh"), i * 2 + (e + 1))
                        pe.wait_ge(s("da_ot"), i * 2 + e + CREDIT)
                    for b in range(u + 1):
                        mm = pe.matmul(ps[:, 7, u * P:(u + 1) * P], A["vh"][:, e, b], A["aT"][:, at + b * P:at + b * P + P],
                                       start=b == 0, stop=b == u)
                    if u == 3:
                        mm.then_inc(s("da_o"), 1)

                def norm_sum(done):
                    pe.wait_ge(s("da_sq"), done)
                    pe.matmul(ps[:, 6], cst("ones"), sq[:, 0], start=True, stop=True).then_inc(s("da_sum"), 1)

                def between(e, c, blocks):
                    if fill:
                        part(Tile(T_DA + 4 + 2 * e + c, i), c, xh, xl, blocks, free=i * 4 + (T_DA + 4 + 2 * e + c - 1))
                    elif c == 0:
                        part(Tile(T_DO + e), e, yh, yl, [k for k in blocks if k < 6], free=T_DO, ready=y_ready,
                             base=Y0["da"])

                for e in (0, 1):
                    scores(e, 0)
                    scores(e, 1)
                    if e or before:
                        norm_sum(i * 2 + e)
                    between(e, 0, range(0, 4))
                    transposes(e, 0)
                    scores(e, 2)
                    between(e, 0, range(4, 8))
                    transposes(e, 1)
                    scores(e, 3)
                    between(e, 1, range(0, 4))
                    transposes(e, 2)
                    values(e, 0)
                    values(e, 1)
                    between(e, 1, range(4, 6))
                    transposes(e, 3)
                    values(e, 2)
                    values(e, 3)
                    between(e, 1, range(6, 8))
                if not fill:
                    pe.wait_ge(s("da_exp"), 2 * 4 * DA_HEADS + CREDIT)
                    for j in (2, 3):
                        part(Tile(T_DO + j), j, yh, yl, range(0, 6))
                        if j == 2:
                            norm_sum(DA_HEADS)

            for n in range(4):
                tile(Tile(T_DA + n), n % 2, xh, xl, free=T_DA + n - 1)
            head_pair(0, False, True)
            with pe.Fori(1, 3) as i:
                head_pair(i, True, True)
            head_pair(3, True, False)
            for j in range(4):
                part(Tile(T_DO + j), j, yh, yl, range(6, 8), ready=y_ready, base=Y0["da"])
            for j in range(4, KB):
                tile(Tile(T_DO + j), j % RING, yh, yl)
            row_sum("da_post")

            def to_m(t0, which, y0):
                down(Tile(t0), y0)
                row_sum(which + "_post")

            def mlp(f, t0, y0):
                name = f"mlp{f}"
                first_round(Tile(t0), xh, xl, x_ready, 8 * PRE[name])
                row_sum(name)
                tile(Tile(t0 + FIRST), FIRST, xh, xl)

                def up(t):
                    for j in range(RING):
                        tile(t.plus(j), j, xh, xl)

                up(Tile(t0 + 4))
                down(Tile(t0 + 8), y0)
                with pe.Fori(1, MLP_GROUPS - 1) as g:
                    with pe.Fori(0, 2) as i:
                        up(Tile(t0, g * 4 + i))
                    down(Tile(t0 + 8, g * 4), g * 8 + y0)
                with pe.Fori(0, 2) as i:
                    up(Tile(t0 + 48, i))
                to_m(t0 + 56, name, y0 + 24)

            mlp(0, T_MLP0, Y0["mlp0"])

            first_round(Tile(T_SC), xh, xl, x_ready, 8 * PRE["sc"])
            row_sum("sc")
            tile(Tile(T_SC + FIRST), FIRST, xh, xl)
            with pe.Fori(1, 6) as i:
                for j in range(RING):
                    tile(Tile(T_SC + j, i), j, xh, xl)
            to_m(T_SCO, "sc", Y0["sc"])
            mlp(1, T_MLP1, Y0["mlp1"])


Y0 = {"ff0": 4, "pw": 26, "ff1": 34, "da": 56, "mlp0": 64, "sc": 96, "mlp1": 104}


def _narrow(w, k0, n):
    rows = w[k0:k0 + D, n * P:(n + 1) * P]
    if rows.shape[0] < D:
        rows = np.concatenate([rows, np.zeros((D - rows.shape[0], P), rows.dtype)])
    return rows.reshape(KB, P, P).transpose(1, 0, 2).reshape(P, D)


def _wide(w, j, rows, c0, cols):
    return w[j * rows * P:(j + 1) * rows * P, c0:c0 + cols].reshape(rows, P, cols).transpose(1, 0, 2).reshape(P, D)


def _stream(a):
    w = a["hy_w_in"][0]
    c_glr, c_sq, c_sk, c_sv = 1536, 1552, 2064, 2576
    gr, sbw = w[:, 1024:1536], w[:, c_sq:]
    tiles = [_wide(w, j, 4, 256, 256) for j in range(2)]
    tiles += [_narrow(w, 0, j) for j in range(2)]
    tiles += [_wide(w, j, 2, 512, 512) for j in range(4)]
    tiles += [_narrow(gr, 0, j) for j in range(4)]
    tiles += [_wide(w, j, 2, c_sv, 512) for j in range(4)]
    for p in range(4):
        tiles += [_narrow(sbw, 0, p), _narrow(sbw, 0, 4 + p)]
    tiles += [_narrow(a["hy_w_out"][0], 0, n) for n in range(KB)]

    def swiglu(f):
        out, at = [], 0
        for g in FF_GROUPS:
            for q in range(at, at + g):
                out += [_narrow(a["ffn_w_gate"][f], 0, q), _narrow(a["ffn_w_up"][f], 0, q)]
            rows = a["ffn_w_down"][f][at * P:(at + g) * P]
            out += [_narrow(rows, 0, n) for n in range(KB)]
            at += g
        return out

    tiles += swiglu(0)
    for j in range(KB):
        tiles += [_narrow(a["cv_w_pw1"][0], 0, j), _narrow(a["cv_w_pw1"][0], 0, KB + j)]
    tiles += [_narrow(a["cv_w_pw2"][0], 0, n) for n in range(KB)]
    tiles += swiglu(1)
    qkv = a["attn_w_qkv_2"][0]
    for r in range(2):
        tiles += [_wide(qkv, j, 2, 2048 + 512 * r, 512) for j in range(4)]
    for q in range(DA_HEADS):
        tiles += [_narrow(qkv, 0, q), _narrow(qkv, 0, KB + q)]
    tiles += [_narrow(a["attn_w_o_2"][0], 0, n) for n in range(KB)]

    def mlp(f):
        out = []
        for g in range(MLP_GROUPS):
            out += [_narrow(a["mlp_w_up_2"][f], 0, 8 * g + j) for j in range(8)]
            out += [_narrow(a["mlp_w_down_2"][f], g * D, n) for n in range(KB)]
        return out

    tiles += mlp(0)
    for j in range(KB):
        tiles += [_narrow(a["conv_w_in_2"][0], 0, c * KB + j) for c in range(3)]
    tiles += [_narrow(a["conv_w_out_2"][0], 0, n) for n in range(KB)]
    tiles += mlp(1)
    assert len(tiles) == NT
    return np.stack(tiles)


def _vectors(a):
    f = np.zeros((P, NVEC), a["x"].dtype)

    def put(name, v, at=0):
        cols = np.asarray(v).reshape(-1, P).T
        f[:, _cols[name] + at:_cols[name] + at + cols.shape[1]] = cols

    for n, v in enumerate((a["mix_norm"][0], a["ffn_norm"][0], a["mix_norm"][1], a["ffn_norm"][1],
                           a["norm_mixer_pre_2"][0], a["norm_mlp_pre_2"][0], a["norm_mixer_pre_2"][1],
                           a["norm_mlp_pre_2"][1])):
        put("pre", v, 8 * n)
    for n, v in enumerate((a["norm_mixer_post_2"][0], a["norm_mlp_post_2"][0], a["norm_mixer_post_2"][1],
                           a["norm_mlp_post_2"][1])):
        put("post", v, 8 * n)
    put("b_pw1", a["cv_b_pw1"][0])
    f[:, _cols["w_dw"]:_cols["w_dw"] + TAPS * KB] = \
        a["cv_w_dw"][0].reshape(TAPS, KB, P).transpose(2, 1, 0).reshape(P, -1)
    put("b_dw", a["cv_b_dw"][0])
    put("ln_g", a["cv_ln_g"][0])
    put("ln_b", a["cv_ln_b"][0])
    put("b_pw2", a["cv_b_pw2"][0])
    put("gla", a["hy_gla_norm"][0])
    put("sbq", np.tile(a["hy_sb_q_norm"][0], 2))
    put("sbk", np.tile(a["hy_sb_k_norm"][0], 2))
    put("subln", a["attn_subln_g_2"][0])
    f[:, _cols["conv_w"]:_cols["conv_w"] + 24] = a["conv_w_2"][0].reshape(3, KB, P).transpose(2, 1, 0).reshape(P, -1)
    for n, v in enumerate(("q1", "k1", "q2", "k2")):
        f[:64, _cols["lam"] + n] = a[f"attn_lambda_{v}_2"][0]
    return f


def _constants():
    f = np.zeros((P, NCONST), np.float32)
    p, c = np.arange(P)[:, None], np.arange(P)[None, :]

    def put(name, v):
        at, n = _consts[name]
        f[:, at:at + n] = v

    put("ident", p == c)
    put("ones", 1.0)
    put("blk64", p // 64 == c // 64)
    put("negtri", -1.0 * (p >= c))
    put("negones", -1.0)
    put("later64", (p > c) & (p // 64 == c // 64))
    put("neg_sb", np.where(p < c, 0.0, NEG))
    put("neg_da", np.where(c <= p, 0.0, NEG))
    put("mask_sb", p < c)
    put("chunk", p // 64 == np.arange(2)[None, :])
    half = 8
    inv = 500000.0 ** (-np.arange(0, 16, 2, dtype=np.float32) / np.float32(16))
    ang = (np.arange(T, dtype=np.float32)[:, None] * inv[None, :].astype(np.float32)).astype(np.float32)
    cos, sin = np.ones((64, T), np.float32), np.zeros((64, T), np.float32)
    cos[:half] = cos[half:16] = np.cos(ang).T
    sin[:half], sin[half:16] = -np.sin(ang).T, np.sin(ang).T
    put("cos", np.tile(cos, (2, 1)))
    put("sin", np.tile(sin, (2, 1)))
    return f


def kernel(**inputs):
    import concourse.bacc as bacc
    from concourse.bass_utils import run_bass_kernel_spmd

    a = {k: np.asarray(v) for k, v in inputs.items()}
    w_in = a["hy_w_in"][0]
    glr = np.concatenate([w_in[:, 1536:1552], np.zeros((D, P - 16), w_in.dtype)], axis=1)
    arrays = {
        "x_t": np.ascontiguousarray(a["x"][0].T),
        "stream": _stream(a),
        "w_glr": np.ascontiguousarray(_narrow(glr, 0, 0)),
        "w_gate": np.ascontiguousarray(np.concatenate([a["hy_w_gate2"][0], a["hy_b_gate"]], axis=0)),
        "vecs": _vectors(a),
        "consts": _constants(),
    }
    nc = bacc.Bacc("TRN2", target_bir_lowering=False, num_devices=1)
    args = [nc.dram_tensor(n, v.shape, mybir.dt.from_np(v.dtype), kind="ExternalInput").ap() for n, v in arrays.items()]
    out_t = nc.dram_tensor("out_t", (D, T), F32, kind="ExternalOutput").ap()
    build(nc, *args, out_t)
    got = run_bass_kernel_spmd(nc, [arrays], core_ids=[0]).results[0]["out_t"]
    return np.ascontiguousarray(np.asarray(got).T)[None]
```

```python
from contextlib import ExitStack

import numpy as np

import concourse.bass as bass
from concourse import mybir

F32 = mybir.dt.float32
F32R = mybir.dt.float32r
ACT = mybir.ActivationFunctionType
ALU = mybir.AluOpType
AX = mybir.AxisListType

P = 128
T = 512
D = 1024
KB = D // P
TB = T // P
EPS = 1e-6
NEG = -1e30
LN_EXP = "natural_log_exp_and_others"
RING = 4
FIRST = 3
TAPS = 31
TAPS_PE = 6
TAPS_POOL = 10
PAD = TAPS - 1
FF_GROUPS = (8, 8, 6)
MLP_GROUPS = 4
SB_HEADS, DA_HEADS, GLA_HEADS = 8, 8, 4
SB_PAIRS = SB_HEADS // 2
CREDIT = 1
CREDITED = "da_ln cv_padd da_qn cv_pe da_o da_exp da_aT da_rr da_ot".split()
LAMBDA_INIT = 0.2

T_GK, T_GQ, T_GV, T_GR, T_SV, T_SB, T_WO = 0, 2, 4, 8, 12, 16, 24
T_FF0 = T_WO + 8
T_PW1 = T_FF0 + 68
T_PW2 = T_PW1 + 16
T_FF1 = T_PW2 + 8
T_DV = T_FF1 + 68
T_DA = T_DV + 8
T_DO = T_DA + 16
T_MLP0 = T_DO + 8
T_SC = T_MLP0 + 64
T_SCO = T_SC + 24
T_MLP1 = T_SCO + 8
NT = T_MLP1 + 64
assert T_SB + 8 == T_WO and NT % RING == 0

_cols = {}
_at = 0
for _name, _n in (("pre", 64), ("post", 32), ("b_pw1", 16), ("w_dw", TAPS * KB), ("b_dw", 8), ("ln_g", 8),
                  ("ln_b", 8), ("b_pw2", 8), ("gla", 1), ("sbq", 1), ("sbk", 1), ("subln", 1),
                  ("conv_w", 24), ("lam", 4)):
    _cols[_name] = _at
    _at += _n
NVEC = _at

_consts = {}
_at = 0
for _name, _n in (("ident", P), ("negtri", P), ("negones", P), ("neg_sb", P), ("neg_da", P),
                  ("ones", P), ("blk64", P), ("later64", P), ("mask_sb", P), ("chunk", 2), ("cos", T), ("sin", T)):
    _consts[_name] = (_at, _n)
    _at += _n
NCONST = _at
NEXACT = 5 * P


class Tile:

    def __init__(self, n, rounds=0):
        self.n, self.rounds = n, rounds
        self.slot = n % RING

    def plus(self, d):
        return Tile(self.n + d, self.rounds)

    @property
    def count(self):
        return self.rounds * RING + (self.n + 1)

    @property
    def loaded(self):
        return self.rounds * 16 + 16 * (self.n // RING + 1)


def build(nc, x_t, stream, w_glr, w_gate, vecs, consts, out_t):
    with ExitStack() as ctx:
        def sem(name):
            return ctx.enter_context(nc.semaphore(name))

        def sb(name, shape, dt=F32, where=ctx):
            return where.enter_context(nc.sbuf_tensor(name, shape, dt))

        ps = ctx.enter_context(nc.psum_tensor("ps", [P, 8, 512], F32))
        flat = ps[:].rearrange("p b c -> p (b c)")

        h = sb("h", [P, KB, T])
        xh, xl = sb("xh", [P, KB, T], F32R), sb("xl", [P, KB, T], F32R)
        yh, yl = sb("yh", [P, KB, T], F32R), sb("yl", [P, KB, T], F32R)
        raw = sb("raw", [P, RING, D])
        whi, wlo = sb("whi", [P, RING, D], F32R), sb("wlo", [P, RING, D], F32R)
        vec = sb("vec", [P, NVEC])
        const = sb("const", [P, NCONST])
        exact = sb("exact", [P, NEXACT], F32R)
        sq = sb("sq", [P, 2, T])
        acc = sb("acc", [P, T])
        lnb = sb("lnb", [P, T])
        rrow = sb("rrow", [P, T])
        lncol = sb("lncol", [P, TB])
        rcol = sb("rcol", [P, TB])
        nlam = sb("nlam", [P, 1])
        lamt = sb("lamt", [P, 2, 2])

        def cst(name, rows=slice(None), cols=None):
            a, n = _consts[name]
            return const[rows, a:a + (cols or n)]

        def cst_r(name):
            a, n = _consts[name]
            return exact[:, a:a + n]

        def col(name, j=0):
            a = _cols[name] + j
            return vec[:, a:a + 1] if isinstance(a, int) else vec[:, bass.ds(a, 1)]

        def block_of(x, q):
            return x[:, q] if isinstance(q, int) else x[:, bass.ds(q, 1)].rearrange("p a t -> p (a t)")

        def arena(**shapes):
            scope = ExitStack()
            with scope:
                return {k: scope.enter_context(nc.sbuf_tensor(k, [P] + list(v[:-1] if v[-1] is F32R else v),
                                                              F32R if v[-1] is F32R else F32))
                        for k, v in shapes.items()}

        A = {}
        hyb = ExitStack()
        with hyb:
            A["sv"] = sb("sv", [P, TB, T], F32, hyb)
            A.update(arena(glr=(T,), wg2=(256,), la=(TB, 256), gk=(TB, 256), gq=(2, T), wgl=(D, F32R),
                           gv=(TB, T), sr=(4, T), gt=(D,), dec=(2, 8), wgr=(D,), wgh=(D, F32R)))
            A.update(arena(_glr=(T,), _wg2=(256,), _la=(TB, 256), _gk=(TB, 256), _gq=(2, T), _wgl=(D,),
                           _gv=(TB, T), _sr=(4, T), _gt=(D,), _dec=(2, 8), S=(8, 2, P)))
            A.update(arena(sraw=(2, T), ssq=(2, T), srr=(2, T), sqn=(2, T), vp=(TB, P), _pad=(256,),
                           sl=(2, 1280), sp=(2, 1280), spl=(2, 1280, F32R)))
            A.update(arena(_sraw=(2, T), _ssq=(2, T), _srr=(2, T), _sqn=(2, T), _vp=(TB, P), _pad2=(256,),
                           sph=(2, 1280, F32R)))
        A.update(arena(tg=(2, T), ts=(2, T), tu=(2, T), th=(2, T)))
        A.update(arena(t1=(2, T), t2=(2, T), t3=(2, T), ub=(2, T + PAD), pr=(4, T), pa=(2, T), odd=(2, T),
                       dg=(2, TAPS_PE, P), wt=(2, TAPS_PE), cv=(KB, T), mu=(T,)))
        A.update(arena(dv=(TB, D), draw=(2, T), dsh=(2, T), dq=(2, 2, T), vh=(2, TB, P), ex=(2, 2, T),
                       da=(2, T), aT=(1280,), dot=(T,), nm=(2, 2), sm=(2, 2), rc=(2, 2),
                       r1=(2, 1)))
        A.update(arena(m=(KB, T), mr=(2, T), mh=(2, T), cb=(2, T), cc=(2, T), cx=(2, T), uc=(2, T + 2),
                       cy=(2, T)))

        loaded = [sem(f"weight_loaded{s}") for s in range(RING)]
        whi_ready = sem("whi_ready")
        wlo_ready = sem("wlo_ready")
        tile_done = sem("tile_done")
        evac_done = sem("evac_done")
        x_in = [sem(f"x_in{k}") for k in range(KB)]
        small_in = [sem(f"small_in{k}") for k in range(4)]
        xh_ready, x_ready = sem("xh_ready"), sem("x_ready")
        yh_ready, y_ready = sem("yh_ready"), sem("y_ready")
        sq_ready, acc_ready = sem("sq_ready"), sem("acc_ready")
        sum_ready = sem("sum_ready")
        colsum_ready = sem("colsum_ready")
        ln_ready, rrow_ready, rcol_ready = sem("ln_ready"), sem("rrow_ready"), sem("rcol_ready")
        lncol_ready = sem("lncol_ready")
        h_added = sem("h_added")
        h_added_pool = sem("h_added_pool")
        post_t = sem("post_t")
        stored = sem("stored")

        S = {}

        def s(name):
            if name not in S:
                S[name] = sem(name)
            return S[name]

        for n in ("exact_ready sb_sph sb_spl wglr_in wglr_hi wglr_lo glr_done glr_evac gate_x gate_abs gate_exp "
                  "gate_ln la_ready suf_ready "
                  "kd_ready kend_ready dec_ready upd_ready state_ready go_ready gsq_ready gsum_ready "
                  "gln_ready grr_ready gt_ready gy_ready silu_r "
                  "sb_sq sb_sum sb_ln sb_rr sb_qn sb_vp sb_z sb_abs sb_exp sb_ln2 sb_sp sb_mask sb_acc sb_w "
                  "sb_o sb_yh sb_yl "
                  "var_mm cen_sq wt_ready pw_sg pw_u pw_zero dg_ready cv_pe cv_prod cv_padd cv_chain cv_done "
                  "mu_sum mu_copied cen_ready ln_t ln_s "
                  "lam_p lam_s lam_e lam_ready "
                  "da_sh da_shs da_rc da_qn da_vh da_s da_max da_exp da_rcp da_r1 da_t da_a da_T da_aT da_o da_sq da_sum "
                  "da_ln da_rr da_ot m_zero sc_u sc_y sc_zero").split():
            s(n)
        for f in (0, 1):
            for n in ("silu", "hid"):
                s(f"ff{f}_{n}")
            s(f"mlp{f}_hid")

        block = ctx.enter_context(nc.Block())

        SUM = {"hyb": 0, "ff0": 1, "pw": 2, "lnvar": 3, "ff1": 4, "da": 5, "da_post": 6, "mlp0": 7, "mlp0_post": 8,
               "sc": 9, "sc_post": 10, "mlp1": 11, "mlp1_post": 12}
        BY_PE = ("hyb", "da_post", "mlp0_post", "sc_post", "mlp1_post")
        ACC, at = {}, 0
        for n in SUM:
            if n != "lnvar":
                ACC[n] = at
                at += KB - (n in BY_PE)
        PRE = {"hyb": 0, "ff0": 1, "pw": 2, "ff1": 3, "da": 4, "mlp0": 5, "sc": 6, "mlp1": 7}
        POST = {"da": 0, "mlp0": 1, "sc": 2, "mlp1": 3}

        @block.sync
        def _(sp):
            for name in CREDITED:
                sp.sem_inc(s(name), CREDIT)
            sp.dma_start(vec[:], vecs).then_inc(small_in[0], 16)
            sp.dma_start(A["wgr"][:], w_glr).then_inc(s("wglr_in"), 16)
            for k in range(KB):
                sp.dma_start(h[:, k], x_t[k * P:(k + 1) * P, :]).then_inc(x_in[k], 16)
            for j in range(RING):
                if j == 2:
                    sp.dma_start(const[:], consts).then_inc(small_in[1], 16)
                    sp.dma_start(A["wg2"][0:17, :], w_gate).then_inc(small_in[2], 16)
                sp.dma_start(raw[:, j], stream[j]).then_inc(loaded[j], 16)
            with sp.Fori(1, NT // RING) as r:
                for j in range(RING):
                    sp.wait_ge(wlo_ready, r * RING + (j + 1 - RING))
                    sp.dma_start(raw[:, j], stream[bass.ds(r * RING + j, 1)].rearrange("a p c -> (a p) c"))\
                      .then_inc(loaded[j], 16)
            for k in range(KB):
                if k % 2:
                    sp.wait_ge(h_added, 8 * 3 + k // 2 + 1)
                else:
                    sp.wait_ge(h_added_pool, k // 2 + 1)
                sp.dma_start(out_t[k * P:(k + 1) * P, :], h[:, k]).then_inc(stored, 16)
            sp.wait_ge(stored, 16 * KB)

        @block.scalar
        def _(act):
            def split_hi(t):
                if t.n + RING >= NT:
                    return
                a = t.plus(RING)
                act.wait_ge(loaded[a.slot], a.loaded)
                act.wait_ge(tile_done, t.count)
                act.activation(whi[:, a.slot], raw[:, a.slot], ACT.Copy).then_inc(whi_ready, 1)

            def square_block(name, k, src):
                if k < 2 and SUM[name]:
                    act.wait_ge(sum_ready, SUM[name])
                    act.wait_ge(acc_ready, ACC[name])
                elif k >= 2:
                    act.wait_ge(acc_ready, ACC[name] + k - 1)
                act.activation(sq[:, k % 2], src, ACT.Square).then_inc(sq_ready, 1)

            def pre_block(name, k):
                act.activation(xh[:, k], h[:, k], ACT.Copy, scale=col("pre", 8 * PRE[name] + k)).then_inc(xh_ready, 1)
                square_block(name, k, h[:, k])

            def inv_rms(name, n, preload=True, bank=4):
                if preload:
                    act.preload_act_table_set(LN_EXP)
                act.wait_ge(sum_ready, SUM[name] + 1)
                if SUM[name]:
                    act.wait_ge(rrow_ready, SUM[name])
                act.activation(lnb[:], ps[:, bank], ACT.Ln, scale=1.0 / n, bias=EPS).then_inc(ln_ready, 1)
                act.wait_ge(ln_ready, SUM[name] + 1)
                act.activation(rrow[:], lnb[:], ACT.Exp, scale=-0.5).then_inc(rrow_ready, 1)

            def inv_rms_col(n, bank=5):
                act.wait_ge(colsum_ready, n)
                act.activation(lncol[:], ps[:, bank, 0:TB], ACT.Ln, scale=1.0 / D, bias=EPS).then_inc(lncol_ready, 1)
                act.wait_ge(lncol_ready, n)
                act.activation(rcol[:], lncol[:], ACT.Exp, scale=-0.5).then_inc(rcol_ready, 1)

            def down_tile(t, k, name):
                if name:
                    act.wait_ge(evac_done, t.count)
                    pre_block(name, k)
                split_hi(t)

            def post_stage(which, name):
                for k in range(KB):
                    act.wait_ge(h_added, 8 * POST[which] + k + 1)
                    pre_block(name, k)

            act.preload_act_table_set(LN_EXP)
            act.wait_ge(s("wglr_in"), 16)
            act.activation(A["wgh"][:], A["wgr"][:], ACT.Copy).then_inc(s("wglr_hi"), 1)
            act.wait_ge(small_in[0], 16)
            for k in range(KB):
                act.wait_ge(x_in[k], 16)
                pre_block("hyb", k)
            for j in range(RING):
                act.wait_ge(loaded[j], 16)
                act.activation(whi[:, j], raw[:, j], ACT.Copy).then_inc(whi_ready, 1)
            inv_rms("hyb", D)
            inv_rms_col(1)
            act.wait_ge(small_in[1], 16)
            act.activation(exact[:], const[:, 0:NEXACT], ACT.Copy).then_inc(s("exact_ready"), 1)
            for n in (0, 1, 2, 3):
                split_hi(Tile(n))
            act.wait_ge(s("gate_x"), 1)
            act.activation(A["gt"][:], flat[:, 6 * 512:8 * 512], ACT.Abs).then_inc(s("gate_abs"), 1)
            act.wait_ge(s("gate_abs"), 1)
            act.activation(A["gt"][:], A["gt"][:], ACT.Exp, scale=-1.0).then_inc(s("gate_exp"), 1)
            act.wait_ge(s("gate_exp"), 1)
            act.activation(A["gt"][:], A["gt"][:], ACT.Ln, bias=1.0).then_inc(s("gate_ln"), 1)
            for n in range(T_GV, T_GR):
                split_hi(Tile(n))
            act.wait_ge(s("suf_ready"), 1)
            act.activation(A["gt"][:], flat[:, 4 * 512:6 * 512], ACT.Exp, scale=1.0 / 16).then_inc(s("kd_ready"), 1)
            act.activation(A["dec"][:], ps[:, 6, 0:16].rearrange("p (j n) -> p j n", j=2), ACT.Exp,
                           scale=1.0 / 16).then_inc(s("dec_ready"), 1)
            for j in range(4):
                act.wait_ge(evac_done, T_GR + j + 1)
                act.activation(A["sr"][:, j], A["sr"][:, j], ACT.Silu).then_inc(s("silu_r"), 1)
                split_hi(Tile(T_GR + j))
            for n in range(T_SV, T_SV + 2):
                split_hi(Tile(n))
            for hh in range(GLA_HEADS):
                act.wait_ge(s("go_ready"), hh + 1)
                if hh >= 2:
                    act.wait_ge(s("gsum_ready"), hh - 1)
                act.activation(A["gt"][:, (hh % 2) * T:(hh % 2 + 1) * T], ps[:, 4 + hh], ACT.Square)\
                   .then_inc(s("gsq_ready"), 1)
                if hh < 2:
                    split_hi(Tile(T_SV + 2 + hh))

            def gla_rms(hh):
                act.wait_ge(s("gsum_ready"), hh + 1)
                if hh:
                    act.wait_ge(s("grr_ready"), hh)
                act.activation(lnb[:], ps[:, 2 + hh % 2], ACT.Ln, scale=1.0 / P, bias=EPS).then_inc(s("gln_ready"), 1)
                act.wait_ge(s("gln_ready"), hh + 1)
                act.activation(A["S"][:, 2 * hh:2 * hh + 2].rearrange("p a j v -> p (a j v)"), lnb[:], ACT.Exp,
                               scale=-0.5).then_inc(s("grr_ready"), 1)

            def square_qk(p, c):
                t = Tile(T_SB + 2 * p + c)
                act.wait_ge(evac_done, t.count)
                act.activation(A["ssq"][:, c], A["sraw"][:, c], ACT.Square).then_inc(s("sb_sq"), 1)
                split_hi(t)

            def rms_qk(p, c):
                n = 2 * p + c
                act.wait_ge(s("sb_sum"), n + 1)
                act.wait_ge(s("grr_ready"), GLA_HEADS)
                if n:
                    act.wait_ge(s("sb_rr"), n)
                act.activation(lnb[:], ps[:, c], ACT.Ln, scale=1.0 / 64, bias=EPS).then_inc(s("sb_ln"), 1)
                act.wait_ge(s("sb_ln"), n + 1)
                if p:
                    act.wait_ge(s("sb_qn"), n - 1)
                act.activation(A["srr"][:, c], lnb[:], ACT.Exp, scale=-0.5,
                               bias=float(-np.log(8.0)) if c == 0 else 0.0).then_inc(s("sb_rr"), 1)

            def soft_exp(p, hh):
                n, b = 2 * p + hh, 2 + 3 * hh
                act.wait_ge(s("sb_z"), n + 1)
                act.activation(A["sl"][:, hh], flat[:, b * 512:b * 512 + 1280], ACT.Abs).then_inc(s("sb_abs"), 1)
                act.wait_ge(s("sb_abs"), n + 1)
                act.activation(A["sl"][:, hh], A["sl"][:, hh], ACT.Exp, scale=-1.0).then_inc(s("sb_exp"), 1)

            def soft_ln(p, hh):
                act.wait_ge(s("sb_exp"), 2 * p + hh + 1)
                act.activation(A["sl"][:, hh], A["sl"][:, hh], ACT.Ln, bias=1.0).then_inc(s("sb_ln2"), 1)

            def soft_hi(p, hh):
                act.wait_ge(s("sb_mask"), 2 * p + hh + 1)
                act.activation(A["sph"][:, hh], A["sp"][:, hh], ACT.Copy).then_inc(s("sb_sph"), 1)

            def weights(p, hh):
                n, b = 2 * p + hh, 2 + 3 * hh
                act.wait_ge(s("sb_acc"), n + 1)
                act.activation(A["sl"][:, hh], flat[:, b * 512:b * 512 + 1280], ACT.Exp).then_inc(s("sb_w"), 1)

            def out_hi(p, hh):
                b, r = 2 + 3 * hh, slice(64 * hh, 64 * hh + 64)
                act.wait_ge(s("sb_o"), 2 * p + hh + 1)
                act.activation(yh[r, 4 + p], ps[r, b], ACT.Copy).then_inc(s("sb_yh"), 1)

            act.preload_act_table_set(LN_EXP)
            gla_rms(0)
            gla_rms(1)
            square_qk(0, 0)
            gla_rms(2)
            gla_rms(3)
            rms_qk(0, 0)
            square_qk(0, 1)
            rms_qk(0, 1)
            for hh in range(GLA_HEADS):
                act.wait_ge(s("gy_ready"), hh + 1)
                act.activation(yh[:, hh], A["gv"][:, hh], ACT.Copy).then_inc(yh_ready, 1)
            act.wait_ge(y_ready, GLA_HEADS)
            for p in range(SB_PAIRS):
                soft_exp(p, 0)
                soft_ln(p, 0)
                soft_exp(p, 1)
                soft_hi(p, 0)
                soft_ln(p, 1)
                if p < SB_PAIRS - 1:
                    square_qk(p + 1, 0)
                soft_hi(p, 1)
                weights(p, 0)
                if p < SB_PAIRS - 1:
                    square_qk(p + 1, 1)
                weights(p, 1)
                if p < SB_PAIRS - 1:
                    rms_qk(p + 1, 0)
                    rms_qk(p + 1, 1)
                out_hi(p, 0)
                out_hi(p, 1)

            for k in range(KB):
                down_tile(Tile(T_WO + k), k, "ff0")

            def swiglu(f, t0, following):
                name = f"ff{f}"
                inv_rms(name, D)

                def up(g, i):
                    for u in (0, 1):
                        tg = Tile(t0 + 2 * u, g * 6 + i)
                        act.wait_ge(evac_done, tg.count)
                        act.activation(A["ts"][:, u], A["tg"][:, u], ACT.Silu).then_inc(s(name + "_silu"), 1)
                        split_hi(tg)
                        done = g * 8 + i * 2 + (u + 1)
                        act.wait_ge(s(name + "_hid"), done)
                        act.activation(block_of(yh, i * 2 + u), A["th"][:, u],
                                       ACT.Copy).then_inc(yh_ready, 1)
                        split_hi(tg.plus(1))

                with act.Fori(0, 2) as g:
                    with act.Fori(0, 4) as i:
                        up(g, i)
                    for k in range(KB):
                        split_hi(Tile(t0 + 16 + k, g * 6))
                with act.Fori(0, 3) as i:
                    up(2, i)
                for k in range(KB):
                    down_tile(Tile(t0 + 60 + k), k, following)

            swiglu(0, T_FF0, "pw")

            inv_rms("pw", D)
            with act.Fori(0, 4) as i:
                act.preload_act_table_set("sigmoid_and_others")
                for u in (0, 1):
                    split_hi(Tile(T_PW1 + 2 * u, i))
                    t = Tile(T_PW1 + 2 * u + 1, i)
                    act.wait_ge(evac_done, t.count)
                    act.activation(A["t3"][:, u], A["t2"][:, u], ACT.Sigmoid,
                                   bias=vec[:, bass.ds(i * 2 + (_cols["b_pw1"] + 8 + u), 1)]).then_inc(s("pw_sg"), 1)
                    split_hi(t)
                    act.wait_ge(s("pw_u"), i * 2 + (u + 1))
                    adds = TAPS_POOL - 1
                    for m in range(TAPS_POOL):
                        k = TAPS_PE + m
                        free = max(m - 4, 1) if m >= 4 else 0
                        act.wait_ge(s("cv_padd"), i * (2 * adds) + (u * adds + free) + CREDIT)
                        act.activation(A["pr"][:, (u * TAPS_POOL + m) % 4], A["ub"][:, u, k:k + T], ACT.Copy,
                                       scale=vec[:, bass.ds(i * (2 * TAPS) + (_cols["w_dw"] + u * TAPS + k), 1)])\
                           .then_inc(s("cv_prod"), 1)
            act.preload_act_table_set(LN_EXP)
            for k in range(KB):
                act.wait_ge(s("cen_ready"), k + 1)
                if k >= 2:
                    act.wait_ge(s("var_mm"), k - 1)
                else:
                    act.wait_ge(sum_ready, SUM["lnvar"])
                act.activation(sq[:, k % 2], A["cv"][:, k], ACT.Square).then_inc(s("cen_sq"), 1)
            inv_rms("lnvar", D, preload=False)
            for k in range(KB):
                act.wait_ge(s("ln_t"), k + 1)
                if k >= 2:
                    act.wait_ge(y_ready, Y0["pw"] + k - 1)
                act.activation(A["t2"][:, k % 2], A["t1"][:, k % 2], ACT.Silu, bias=col("ln_b", k))\
                   .then_inc(s("ln_s"), 1)
                act.wait_ge(s("ln_s"), k + 1)
                act.activation(yh[:, k], A["t2"][:, k % 2], ACT.Copy).then_inc(yh_ready, 1)
            for k in range(KB):
                down_tile(Tile(T_PW2 + k), k, "ff1")

            swiglu(1, T_FF1, "da")

            act.preload_act_table_set(LN_EXP)
            for j in range(3):
                if j == 2:
                    act.wait_ge(s("lam_s"), 1)
                    act.activation(lamt[:, 1], ps[:, 2, 0:2], ACT.Exp).then_inc(s("lam_e"), 1)
                split_hi(Tile(T_DV + j))
            inv_rms("da", D, bank=0)
            inv_rms_col(2, bank=1)
            for j in range(3, 8):
                split_hi(Tile(T_DV + j))

            def head_pair(i, before, fill):
                def exps(e, u):
                    n, p, kv = 4 * e + u, u % 2, (u + 1) * P
                    act.wait_ge(s("da_max"), i * 8 + (n + 1))
                    for c in (0, 1):
                        act.activation(A["ex"][:, p, c, 0:kv], ps[:, 2 + 2 * p + c, 0:kv], ACT.Exp,
                                       bias=A["nm"][:, p, c:c + 1], accum_out=A["sm"][:, p, c:c + 1])\
                           .then_inc(s("da_exp"), 1)

                def copy_T(e, u):
                    n, kv, at = 4 * e + u, (u + 1) * P, P * u * (u + 1) // 2
                    act.wait_ge(s("da_T"), i * 8 + (n + 1))
                    act.activation(A["aT"][:, at:at + kv], ps[:, 6, 0:kv], ACT.Copy).then_inc(s("da_aT"), 1)

                def out_square(e):
                    act.wait_ge(s("da_o"), i * 2 + (e + 1) + CREDIT)
                    act.activation(sq[:, 0], ps[:, 7], ACT.Square).then_inc(s("da_sq"), 1)

                def out_rms(done):
                    act.wait_ge(s("da_sum"), done)
                    act.activation(lnb[:], ps[:, 6], ACT.Ln, scale=1.0 / P, bias=EPS).then_inc(s("da_ln"), 1)
                    act.wait_ge(s("da_ln"), done + CREDIT)
                    act.activation(lnb[:], lnb[:], ACT.Exp, scale=-0.5).then_inc(s("da_rr"), 1)

                def out_hi(done, q):
                    act.wait_ge(s("da_ot"), done + CREDIT)
                    act.activation(block_of(yh, q), A["dot"][:], ACT.Copy, scale=1.0 - LAMBDA_INIT)\
                       .then_inc(yh_ready, 1)

                act.preload_act_table_set(LN_EXP)
                for e in (0, 1):
                    exps(e, 0)
                    if e or before:
                        out_rms(i * 2 + e)
                    exps(e, 1)
                    copy_T(e, 0)
                    if e or before:
                        out_hi(i * 2 + e, i * 2 + (e - 1))
                    exps(e, 2)
                    if fill:
                        split_hi(Tile(T_DA + 4 + 2 * e, i))
                    copy_T(e, 1)
                    exps(e, 3)
                    copy_T(e, 2)
                    copy_T(e, 3)
                    out_square(e)
                    if fill:
                        split_hi(Tile(T_DA + 4 + 2 * e + 1, i))
                if not fill:
                    out_rms(DA_HEADS)
                    out_hi(DA_HEADS, DA_HEADS - 1)

            for j in range(4):
                split_hi(Tile(T_DA + j))
            head_pair(0, False, True)
            with act.Fori(1, 3) as i:
                head_pair(i, True, True)
            head_pair(3, True, False)

            def to_m(t0, which):
                act.preload_act_table_set(LN_EXP)
                for k in range(KB):
                    t = Tile(t0 + k)
                    act.wait_ge(evac_done, t.count)
                    square_block(which + "_post", k, A["m"][:, k])
                    split_hi(t)
                inv_rms(which + "_post", D, preload=False)

            to_m(T_DO, "da")
            post_stage("da", "mlp0")

            def mlp(f, t0):
                name = f"mlp{f}"
                inv_rms(name, D)

                def up(g, i):
                    for j in range(4):
                        t = Tile(t0 + j, g * 4 + i)
                        act.wait_ge(evac_done, t.count)
                        act.activation(block_of(yh, i * 4 + j), A["mr"][:, j % 2],
                                       ACT.Square).then_inc(yh_ready, 1)
                        split_hi(t)

                with act.Fori(0, MLP_GROUPS - 1) as g:
                    with act.Fori(0, 2) as i:
                        up(g, i)
                    with act.Fori(0, 2) as i:
                        for j in range(4):
                            split_hi(Tile(t0 + 8 + j, g * 4 + i))
                with act.Fori(0, 2) as i:
                    up(MLP_GROUPS - 1, i)
                to_m(t0 + 56, name)

            mlp(0, T_MLP0)
            post_stage("mlp0", "sc")

            inv_rms("sc", D)
            with act.Fori(0, 2) as i:
                for u in range(4):
                    for c in range(2):
                        split_hi(Tile(T_SC + 3 * u + c, i * 3))
                    act.wait_ge(s("sc_y"), i * 4 + (u + 1))
                    act.activation(block_of(yh, i * 4 + u), A["cy"][:, u % 2],
                                   ACT.Copy).then_inc(yh_ready, 1)
                    split_hi(Tile(T_SC + 3 * u + 2, i * 3))
            to_m(T_SCO, "sc")
            post_stage("sc", "mlp1")
            mlp(1, T_MLP1)

        @block.vector
        def _(dve):
            def split_lo(t):
                if t.n + RING >= NT:
                    return
                a = t.plus(RING)
                dve.wait_ge(whi_ready, a.count)
                dve.tensor_tensor(wlo[:, a.slot], raw[:, a.slot], whi[:, a.slot].bitcast(F32), ALU.subtract)\
                   .then_inc(wlo_ready, 1)

            def pre_lo(name, k):
                dve.wait_ge(xh_ready, 8 * PRE[name] + k + 1)
                dve.scalar_tensor_tensor(xl[:, k], h[:, k], col("pre", 8 * PRE[name] + k), xh[:, k].bitcast(F32),
                                         ALU.mult, ALU.subtract).then_inc(x_ready, 1)

            def scaled(dst, t, bank):
                dve.wait_ge(tile_done, t.count)
                dve.tensor_tensor(dst, ps[:, bank], rrow[:], ALU.mult).then_inc(evac_done, 1)

            def post_norm(which):
                a = POST[which]
                following = {"da": "mlp0", "mlp0": "sc", "sc": "mlp1"}.get(which)
                dve.wait_ge(rrow_ready, SUM[which + "_post"] + 1)
                for k in range(KB):
                    q = 8 * a + k
                    dve.scalar_tensor_tensor(A["m"][:, k], A["m"][:, k], col("post", q), rrow[:], ALU.mult,
                                             ALU.mult).then_inc(post_t, 1)
                    if following or k % 2:
                        dve.wait_ge(post_t, q + 1)
                        dve.tensor_tensor(h[:, k], h[:, k], A["m"][:, k], ALU.add).then_inc(h_added, 1)
                    if following and k:
                        pre_lo(following, k - 1)
                if following:
                    pre_lo(following, KB - 1)

            dve.memset(A["glr"][0:32, :], 1.0).then_inc(s("glr_evac"), 1)
            dve.wait_ge(s("wglr_hi"), 1)
            dve.tensor_tensor(A["wgl"][:], A["wgr"][:], A["wgh"][:].bitcast(F32), ALU.subtract)\
               .then_inc(s("wglr_lo"), 1)
            dve.wait_ge(small_in[0], 16)
            for k in range(KB):
                pre_lo("hyb", k)
            for j in range(RING):
                dve.wait_ge(whi_ready, j + 1)
                dve.tensor_tensor(wlo[:, j], raw[:, j], whi[:, j].bitcast(F32), ALU.subtract).then_inc(wlo_ready, 1)
            dve.wait_ge(rrow_ready, 1)
            dve.wait_ge(s("glr_done"), 1)
            dve.wait_ge(s("glr_evac"), 1)
            dve.tensor_tensor(A["glr"][0:16, :], ps[0:16, 6], rrow[0:16, :], ALU.mult).then_inc(s("glr_evac"), 1)
            dve.wait_ge(rcol_ready, 1)
            dve.wait_ge(tile_done, 2)
            for t in range(TB):
                last = dve.tensor_scalar(A["gk"][:, t], ps[:, t, 0:256], rcol[:, t:t + 1], None, ALU.mult)
                if t % 2:
                    last.then_inc(evac_done, 1)
            split_lo(Tile(0))
            split_lo(Tile(1))
            for j in range(2):
                dve.wait_ge(tile_done, T_GQ + j + 1)
                dve.scalar_tensor_tensor(A["gq"][:, j], ps[:, 2 + j], 64 ** -0.5, rrow[:], ALU.mult, ALU.mult)\
                   .then_inc(evac_done, 1)
                split_lo(Tile(T_GQ + j))
            dve.wait_ge(s("gate_ln"), 1)
            dve.scalar_tensor_tensor(A["la"][:].rearrange("p t k -> p (t k)"), flat[:, 6 * 512:8 * 512], 0.0,
                                     A["gt"][:], ALU.min, ALU.subtract).then_inc(s("la_ready"), 1)
            for n in range(T_GV, T_GR):
                split_lo(Tile(n))
            dve.wait_ge(tile_done, T_GR)
            for t in range(TB):
                dve.tensor_scalar(A["gv"][:, t], ps[:, t], rcol[:, t:t + 1], None, ALU.mult).then_inc(evac_done, 1)
            dve.wait_ge(s("kd_ready"), 1)
            gkf = A["gk"][:].rearrange("p t k -> p (t k)")
            dve.tensor_tensor(gkf, gkf, A["gt"][:], ALU.mult).then_inc(s("kend_ready"), 1)
            for j in range(4):
                scaled(A["sr"][:, j], Tile(T_GR + j), j)
                split_lo(Tile(T_GR + j))
            dve.wait_ge(s("dec_ready"), 1)
            for n in range(8):
                if n % 2 == 0:
                    dve.wait_ge(s("upd_ready"), n // 2 + 1)
                for j in range(2):
                    u = 2 * (n // 2) + j
                    upd = ps[:, 4 + 2 * (n % 2) + u // 4, (u % 4) * P:(u % 4 + 1) * P]
                    if n == 0:
                        dve.tensor_copy(A["S"][:, n, j], upd).then_inc(s("state_ready"), 1)
                    else:
                        dve.wait_ge(s("state_ready"), 2 * (n - 1) + j + 1)
                        dve.scalar_tensor_tensor(A["S"][:, n, j], A["S"][:, n - 1, j], A["dec"][:, j, n:n + 1], upd,
                                                 ALU.mult, ALU.add).then_inc(s("state_ready"), 1)
            for n in range(T_SV, T_SB - 1):
                split_lo(Tile(n))
            dve.wait_ge(tile_done, T_SB)
            for t in (2, 3, 0, 1):
                dve.tensor_scalar(A["sv"][:, t], ps[:, t], rcol[:, t:t + 1], None, ALU.mult).then_inc(evac_done, 1)
            split_lo(Tile(T_SB - 1))

            def gla_out(hh):
                dve.wait_ge(s("grr_ready"), hh + 1)
                dve.scalar_tensor_tensor(A["gv"][:, hh], ps[:, 4 + hh], col("gla"),
                                         A["S"][:, 2 * hh:2 * hh + 2].rearrange("p a j v -> p (a j v)"), ALU.mult,
                                         ALU.mult).then_inc(s("gt_ready"), 1)
                dve.wait_ge(s("gt_ready"), hh + 1)
                dve.wait_ge(s("silu_r"), 4)
                dve.tensor_tensor(A["gv"][:, hh], A["gv"][:, hh], A["sr"][:, hh], ALU.mult).then_inc(s("gy_ready"), 1)

            def take(p, c):
                t = Tile(T_SB + 2 * p + c)
                scaled(A["sraw"][:, c], t, c)
                split_lo(t)

            def norm_qk(p, c):
                dve.wait_ge(s("sb_rr"), 2 * p + c + 1)
                dve.wait_ge(evac_done, T_SB + 2 * p + c + 1)
                dve.scalar_tensor_tensor(A["sqn"][:, c], A["sraw"][:, c], col("sbk" if c else "sbq"),
                                         A["srr"][:, c], ALU.mult, ALU.mult).then_inc(s("sb_qn"), 1)

            def softplus(p, hh):
                b = 2 + 3 * hh
                dve.wait_ge(s("sb_ln2"), 2 * p + hh + 1)
                dve.scalar_tensor_tensor(A["sp"][:, hh], flat[:, b * 512:b * 512 + 1280], 0.0, A["sl"][:, hh],
                                         ALU.max, ALU.add).then_inc(s("sb_sp"), 1)

            def soft_lo(p, hh):
                dve.wait_ge(s("sb_sph"), 2 * p + hh + 1)
                dve.tensor_tensor(A["spl"][:, hh], A["sp"][:, hh], A["sph"][:, hh].bitcast(F32), ALU.subtract)\
                   .then_inc(s("sb_spl"), 1)

            def out_lo(p, hh):
                b, r = 2 + 3 * hh, slice(64 * hh, 64 * hh + 64)
                dve.wait_ge(s("sb_yh"), 2 * p + hh + 1)
                dve.tensor_tensor(yl[r, 4 + p], ps[r, b], yh[r, 4 + p].bitcast(F32), ALU.subtract)\
                   .then_inc(s("sb_yl"), 1)

            gla_out(0)
            gla_out(1)
            take(0, 0)
            gla_out(2)
            gla_out(3)
            norm_qk(0, 0)
            take(0, 1)
            norm_qk(0, 1)
            for hh in range(GLA_HEADS):
                dve.wait_ge(yh_ready, hh + 1)
                dve.wait_ge(s("gy_ready"), hh + 1)
                dve.tensor_tensor(yl[:, hh], A["gv"][:, hh], yh[:, hh].bitcast(F32), ALU.subtract).then_inc(y_ready, 1)
            for p in range(SB_PAIRS):
                softplus(p, 0)
                soft_lo(p, 0)
                softplus(p, 1)
                if p < SB_PAIRS - 1:
                    take(p + 1, 0)
                soft_lo(p, 1)
                if p < SB_PAIRS - 1:
                    take(p + 1, 1)
                    norm_qk(p + 1, 0)
                    norm_qk(p + 1, 1)
                out_lo(p, 0)
                out_lo(p, 1)

            def add_to_h(t, k, following, bias=None):
                dve.wait_ge(tile_done, t.count)
                if bias:
                    dve.scalar_tensor_tensor(h[:, k], ps[:, t.slot], col(bias, k), h[:, k], ALU.add, ALU.add)\
                       .then_inc(evac_done, 1)
                else:
                    dve.tensor_tensor(h[:, k], ps[:, t.slot], h[:, k], ALU.add).then_inc(evac_done, 1)
                if following:
                    dve.wait_ge(evac_done, t.count)
                    pre_lo(following, k)
                split_lo(t)

            for k in range(KB):
                add_to_h(Tile(T_WO + k), k, "ff0")

            def swiglu(f, t0, following):
                name = f"ff{f}"
                dve.wait_ge(rrow_ready, SUM[name] + 1)

                def up(g, i):
                    for u in (0, 1):
                        tg = Tile(t0 + 2 * u, g * 6 + i)
                        tu = tg.plus(1)
                        scaled(A["tg"][:, u], tg, tg.slot)
                        split_lo(tg)
                        scaled(A["tu"][:, u], tu, tu.slot)
                        done = g * 8 + i * 2 + (u + 1)
                        dve.wait_ge(s(name + "_silu"), done)
                        dve.wait_ge(evac_done, tu.count)
                        dve.tensor_tensor(A["th"][:, u], A["ts"][:, u], A["tu"][:, u], ALU.mult)\
                           .then_inc(s(name + "_hid"), 1)
                        dve.wait_ge(yh_ready, g * 8 + i * 2 + (yh0 + u + 1))
                        at = bass.ds(i * 2 + u, 1)
                        dve.wait_ge(s(name + "_hid"), done)
                        dve.tensor_tensor(yl[:, at].rearrange("p a t -> p (a t)"), A["th"][:, u],
                                          yh[:, at].rearrange("p a t -> p (a t)").bitcast(F32), ALU.subtract)\
                           .then_inc(y_ready, 1)
                        split_lo(tu)

                yh0 = Y0[name]
                with dve.Fori(0, 2) as g:
                    with dve.Fori(0, 4) as i:
                        up(g, i)
                    for k in range(KB):
                        add_to_h(Tile(t0 + 16 + k, g * 6), k, None)
                with dve.Fori(0, 3) as i:
                    up(2, i)
                for k in range(KB):
                    add_to_h(Tile(t0 + 60 + k), k, following)

            swiglu(0, T_FF0, "pw")

            dve.memset(A["ub"][:, :, 0:PAD], 0.0).then_inc(s("pw_zero"), 1)
            dve.wait_ge(rrow_ready, SUM["pw"] + 1)
            first_own = TAPS_PE + TAPS_POOL
            own = TAPS - first_own
            steps = own + 2

            def gated(i, u):
                ta = Tile(T_PW1 + 2 * u, i)
                scaled(A["t1"][:, u], ta, ta.slot)
                split_lo(ta)
                scaled(A["t2"][:, u], ta.plus(1), ta.slot + 1)
                dve.wait_ge(s("pw_sg"), i * 2 + (u + 1))
                dve.wait_ge(evac_done, ta.count)
                dve.wait_ge(s("pw_zero"), 1)
                dve.scalar_tensor_tensor(A["ub"][:, u, PAD:], A["t1"][:, u],
                                         vec[:, bass.ds(i * 2 + (_cols["b_pw1"] + u), 1)], A["t3"][:, u],
                                         ALU.add, ALU.mult).then_inc(s("pw_u"), 1)
                split_lo(ta.plus(1))

            def own_taps(i, u):
                cvb, at = block_of(A["cv"], i * 2 + u), i * (2 * steps) + u * steps
                dve.wait_ge(s("pw_u"), i * 2 + (u + 1))
                for n in range(own):
                    k, chain = first_own + n, A["odd"][:, u] if n % 2 else cvb
                    tap = vec[:, bass.ds(i * (2 * TAPS) + (_cols["w_dw"] + u * TAPS + k), 1)]
                    if n == 0:
                        dve.tensor_scalar(chain, A["ub"][:, u, k:k + T], tap,
                                          vec[:, bass.ds(i * 2 + (_cols["b_dw"] + u), 1)], ALU.mult, ALU.add)\
                           .then_inc(s("cv_chain"), 1)
                    elif n == 1:
                        dve.tensor_scalar(chain, A["ub"][:, u, k:k + T], tap, None, ALU.mult)\
                           .then_inc(s("cv_chain"), 1)
                    else:
                        dve.wait_ge(s("cv_chain"), at + (n - 1))
                        dve.scalar_tensor_tensor(chain, A["ub"][:, u, k:k + T], tap, chain, ALU.mult, ALU.add)\
                           .then_inc(s("cv_chain"), 1)

            def join_taps(i, u):
                cvb, at, done = block_of(A["cv"], i * 2 + u), i * (2 * steps) + u * steps, i * 2 + (u + 1)
                dve.wait_ge(s("cv_chain"), at + own)
                dve.wait_ge(s("cv_pe"), done + CREDIT)
                dve.tensor_tensor(cvb, ps[:, 5 + u], cvb, ALU.add).then_inc(s("cv_chain"), 1)
                dve.wait_ge(s("cv_padd"), done * (TAPS_POOL - 1) + CREDIT)
                dve.tensor_tensor(A["odd"][:, u], A["pa"][:, u], A["odd"][:, u], ALU.add).then_inc(s("cv_chain"), 1)
                dve.wait_ge(s("cv_chain"), at + steps)
                dve.tensor_tensor(cvb, A["odd"][:, u], cvb, ALU.add).then_inc(s("cv_done"), 1)

            gated(0, 0)
            with dve.Fori(0, 3) as i:
                own_taps(i, 0)
                gated(i, 1)
                join_taps(i, 0)
                own_taps(i, 1)
                gated(i + 1, 0)
                join_taps(i, 1)
            own_taps(3, 0)
            gated(3, 1)
            join_taps(3, 0)
            own_taps(3, 1)
            join_taps(3, 1)
            dve.wait_ge(s("mu_sum"), 1)
            dve.wait_ge(s("cv_done"), KB)
            dve.tensor_scalar(A["mu"][:], ps[:, 7], 1.0 / D, None, ALU.mult).then_inc(s("mu_copied"), 1)
            dve.wait_ge(s("mu_copied"), 1)
            for k in range(KB):
                dve.tensor_tensor(A["cv"][:, k], A["cv"][:, k], A["mu"][:], ALU.subtract).then_inc(s("cen_ready"), 1)
            dve.wait_ge(rrow_ready, SUM["lnvar"] + 1)

            def ln_lo(k):
                dve.wait_ge(yh_ready, Y0["pw"] + k + 1)
                dve.tensor_tensor(yl[:, k], A["t2"][:, k % 2], yh[:, k].bitcast(F32), ALU.subtract).then_inc(y_ready, 1)

            for k in range(KB):
                dve.wait_ge(s("cen_ready"), k + 1)
                if k >= 2:
                    dve.wait_ge(s("ln_s"), k - 1)
                dve.scalar_tensor_tensor(A["t1"][:, k % 2], A["cv"][:, k], col("ln_g", k), rrow[:], ALU.mult,
                                         ALU.mult).then_inc(s("ln_t"), 1)
                if k:
                    ln_lo(k - 1)
            ln_lo(KB - 1)
            for k in range(KB):
                add_to_h(Tile(T_PW2 + k), k, "ff1", "b_pw2")

            swiglu(1, T_FF1, "da")

            a = _cols["lam"]
            dve.tensor_tensor(lamt[:, 0], vec[:, a:a + 4:2], vec[:, a + 1:a + 4:2], ALU.mult).then_inc(s("lam_p"), 1)
            for j in range(3):
                split_lo(Tile(T_DV + j))
            dve.wait_ge(s("lam_e"), 1)
            dve.scalar_tensor_tensor(nlam[:], lamt[:, 1, 1:2], -LAMBDA_INIT, lamt[:, 1, 0:1], ALU.add, ALU.subtract)\
               .then_inc(s("lam_ready"), 1)
            dve.wait_ge(rrow_ready, SUM["da"] + 1)
            dve.wait_ge(rcol_ready, 2)
            for r in range(2):
                if r:
                    for j in range(3):
                        split_lo(Tile(T_DV + 4 + j))
                dve.wait_ge(tile_done, T_DV + 4 * r + 4)
                for t in range(TB):
                    dve.tensor_scalar(A["dv"][:, t, 512 * r:512 * r + 512], ps[:, 4 * (1 - r) + t], rcol[:, t:t + 1], None,
                                      ALU.mult).then_inc(evac_done, 1)
                split_lo(Tile(T_DV + 4 * r + 3))
            swap = [d ^ 8 if d < 16 else d for d in range(32)]

            def rope(c, t, done, split=True):
                dve.wait_ge(tile_done, t.count)
                if not isinstance(done, int) or done > 2:
                    dve.wait_ge(s("da_qn"), done - 2 + CREDIT)
                dve.scalar_tensor_tensor(A["draw"][:, c], ps[:, c], 1.0 if c else 64 ** -0.5, rrow[:], ALU.mult,
                                         ALU.mult).then_inc(evac_done, 1)
                dve.wait_ge(s("lam_ready"), 1)
                dve.wait_ge(evac_done, t.count)
                dve.stream_shuffle(A["dsh"][:, c], A["draw"][:, c], swap).then_inc(s("da_sh"), 1)
                dve.wait_ge(s("da_sh"), done)
                dve.tensor_tensor(A["dsh"][:, c], A["dsh"][:, c], cst("sin"), ALU.mult).then_inc(s("da_shs"), 1)
                if split:
                    split_lo(t)

            def head_pair(i, before, fill):
                def row_max(e, u):
                    n, p, kv = 4 * e + u, u % 2, (u + 1) * P
                    dve.wait_ge(s("da_s"), i * 8 + (n + 1))
                    dve.reduce_max(A["nm"][:, p], ps[:, 2 + 2 * p:4 + 2 * p, 0:kv], AX.X, negate=True)\
                       .then_inc(s("da_max"), 1)

                def combine(e, u):
                    n, p, kv = 4 * e + u, u % 2, (u + 1) * P
                    done = i * 8 + (n + 1)
                    dve.wait_ge(s("da_exp"), i * 16 + 2 * (n + 1) + CREDIT)
                    dve.reciprocal(A["rc"][:, p], A["sm"][:, p]).then_inc(s("da_rcp"), 1)
                    dve.wait_ge(s("da_rcp"), done)
                    dve.tensor_tensor(A["r1"][:, p], A["rc"][:, p, 1:2], nlam[:], ALU.mult).then_inc(s("da_r1"), 1)
                    dve.wait_ge(s("da_r1"), done)
                    dve.tensor_scalar(acc[:, 0:kv], A["ex"][:, p, 1, 0:kv], A["r1"][:, p], None, ALU.mult)\
                       .then_inc(s("da_t"), 1)
                    dve.wait_ge(s("da_t"), done)
                    if u >= 2:
                        dve.wait_ge(s("da_T"), i * 8 + (n - 1))
                    dve.scalar_tensor_tensor(A["da"][:, p, 0:kv], A["ex"][:, p, 0, 0:kv], A["rc"][:, p, 0:1],
                                             acc[:, 0:kv], ALU.mult, ALU.add).then_inc(s("da_a"), 1)

                def out(done):
                    dve.wait_ge(s("da_rr"), done + CREDIT)
                    dve.scalar_tensor_tensor(A["dot"][:], ps[:, 7], col("subln"), lnb[:], ALU.mult, ALU.mult)\
                       .then_inc(s("da_ot"), 1)

                def out_lo(done, q):
                    dve.wait_ge(s("da_ot"), done + CREDIT)
                    dve.wait_ge(yh_ready, done + Y0["da"])
                    dve.scalar_tensor_tensor(block_of(yl, q), A["dot"][:], 1.0 - LAMBDA_INIT,
                                             block_of(yh, q).bitcast(F32), ALU.mult, ALU.subtract)\
                       .then_inc(y_ready, 1)

                for e in (0, 1):
                    row_max(e, 0)
                    row_max(e, 1)
                    combine(e, 0)
                    if e or before:
                        out(i * 2 + e)
                    row_max(e, 2)
                    if e or before:
                        out_lo(i * 2 + e, i * 2 + (e - 1))
                    combine(e, 1)
                    combine(e, 2)
                    if fill:
                        rope(0, Tile(T_DA + 4 + 2 * e, i), i * 4 + (4 + 2 * e + 1), False)
                    row_max(e, 3)
                    combine(e, 3)
                    if fill:
                        split_lo(Tile(T_DA + 4 + 2 * e, i))
                        rope(1, Tile(T_DA + 4 + 2 * e + 1, i), i * 4 + (4 + 2 * e + 2))
                if not fill:
                    out(DA_HEADS)
                    out_lo(DA_HEADS, DA_HEADS - 1)

            for n in range(4):
                rope(n % 2, Tile(T_DA + n), n + 1)
            head_pair(0, False, True)
            with dve.Fori(1, 3) as i:
                head_pair(i, True, True)
            head_pair(3, True, False)

            def add_to_m(t, k):
                dve.wait_ge(tile_done, t.count)
                dve.tensor_tensor(block_of(A["m"], k), ps[:, t.slot], block_of(A["m"], k), ALU.add)\
                   .then_inc(evac_done, 1)
                split_lo(t)

            def set_m(t, k):
                dve.wait_ge(tile_done, t.count)
                dve.tensor_copy(A["m"][:, k], ps[:, t.slot]).then_inc(evac_done, 1)
                split_lo(t)

            for k in range(KB):
                set_m(Tile(T_DO + k), k)
            post_norm("da")

            def mlp(f, t0):
                name = f"mlp{f}"
                yh0 = Y0[name]
                dve.memset(A["m"][:], 0.0).then_inc(s("m_zero"), 1)
                dve.wait_ge(rrow_ready, SUM[name] + 1)

                def up(g, i):
                    for j in range(4):
                        t = Tile(t0 + j, g * 4 + i)
                        dve.wait_ge(tile_done, t.count)
                        dve.scalar_tensor_tensor(A["mr"][:, j % 2], ps[:, t.slot], 0.0, rrow[:], ALU.max, ALU.mult)\
                           .then_inc(evac_done, 1)
                        dve.wait_ge(evac_done, t.count)
                        dve.tensor_tensor(A["mh"][:, j % 2], A["mr"][:, j % 2], A["mr"][:, j % 2], ALU.mult)\
                           .then_inc(s(name + "_hid"), 1)
                        done = g * 8 + i * 4 + (j + 1)
                        dve.wait_ge(s(name + "_hid"), done)
                        dve.wait_ge(yh_ready, g * 8 + i * 4 + (yh0 + j + 1))
                        at = bass.ds(i * 4 + j, 1)
                        dve.tensor_tensor(yl[:, at].rearrange("p a t -> p (a t)"), A["mh"][:, j % 2],
                                          yh[:, at].rearrange("p a t -> p (a t)").bitcast(F32), ALU.subtract)\
                           .then_inc(y_ready, 1)
                        split_lo(t)

                with dve.Fori(0, MLP_GROUPS - 1) as g:
                    with dve.Fori(0, 2) as i:
                        up(g, i)
                    dve.wait_ge(s("m_zero"), f + 1)
                    with dve.Fori(0, 2) as i:
                        for j in range(4):
                            add_to_m(Tile(t0 + 8 + j, g * 4 + i), i * 4 + j)
                with dve.Fori(0, 2) as i:
                    up(MLP_GROUPS - 1, i)
                for k in range(KB):
                    add_to_m(Tile(t0 + 56 + k), k)
                post_norm(name)

            mlp(0, T_MLP0)

            dve.memset(A["uc"][:, :, 0:2], 0.0).then_inc(s("sc_zero"), 1)
            dve.wait_ge(rrow_ready, SUM["sc"] + 1)
            with dve.Fori(0, 2) as i:
                for u in range(4):
                    tc, tx, tb = (Tile(T_SC + 3 * u + c, i * 3) for c in range(3))
                    scaled(A["cc"][:, u % 2], tc, tc.slot)
                    split_lo(tc)
                    scaled(A["cx"][:, u % 2], tx, tx.slot)
                    split_lo(tx)
                    dve.wait_ge(evac_done, tx.count)
                    dve.wait_ge(s("sc_zero"), 1)
                    uc, cy = A["uc"][:, u % 2], A["cy"][:, u % 2]
                    at = i * 16 + 4 * u
                    dve.tensor_tensor(uc[:, 2:], A["cc"][:, u % 2], A["cx"][:, u % 2], ALU.mult).then_inc(s("sc_u"), 1)
                    for k in range(3):
                        dve.wait_ge(s("sc_u"), at + (k + 1))
                        w = vec[:, bass.ds(i * 12 + (_cols["conv_w"] + 3 * u + k), 1)]
                        if k == 0:
                            dve.tensor_scalar(cy, uc[:, 0:T], w, None, ALU.mult).then_inc(s("sc_u"), 1)
                        else:
                            dve.scalar_tensor_tensor(cy, uc[:, k:k + T], w, cy, ALU.mult, ALU.add)\
                               .then_inc(s("sc_u"), 1)
                    scaled(A["cb"][:, u % 2], tb, tb.slot)
                    dve.wait_ge(evac_done, tb.count)
                    dve.wait_ge(s("sc_u"), at + 4)
                    dve.tensor_tensor(cy, cy, A["cb"][:, u % 2], ALU.mult).then_inc(s("sc_y"), 1)
                    dve.wait_ge(yh_ready, i * 4 + (Y0["sc"] + u + 1))
                    dve.wait_ge(s("sc_y"), i * 4 + (u + 1))
                    yat = bass.ds(i * 4 + u, 1)
                    dve.tensor_tensor(yl[:, yat].rearrange("p a t -> p (a t)"), cy,
                                      yh[:, yat].rearrange("p a t -> p (a t)").bitcast(F32), ALU.subtract)\
                       .then_inc(y_ready, 1)
                    split_lo(tb)
            for k in range(KB):
                set_m(Tile(T_SCO + k), k)
            post_norm("sc")
            mlp(1, T_MLP1)

        @block.gpsimd
        def _(pool):
            def sum_squares(name):
                for k in range(KB - (name in BY_PE)):
                    pool.wait_ge(sq_ready, (SUM[name] - (SUM[name] > 3)) * KB + k + 1)
                    if k == 0:
                        if SUM[name]:
                            pool.wait_ge(sum_ready, SUM[name])
                            pool.wait_ge(acc_ready, ACC[name])
                        pool.tensor_copy(acc[:], sq[:, 0]).then_inc(acc_ready, 1)
                    else:
                        pool.wait_ge(acc_ready, ACC[name] + k)
                        pool.tensor_tensor(acc[:], acc[:], sq[:, k % 2], ALU.add).then_inc(acc_ready, 1)

            sum_squares("hyb")
            for p in range(SB_PAIRS):
                if p == 0:
                    pool.wait_ge(evac_done, T_SB)
                else:
                    pool.wait_ge(s("sb_o"), 2 * p)
                pool.tensor_copy(A["vp"][:], A["sv"][:, :, p * P:(p + 1) * P]).then_inc(s("sb_vp"), 1)
                for hh in (0, 1):
                    pool.wait_ge(s("sb_sp"), 2 * p + hh + 1)
                    for r in (0, 512, 896, 1024):
                        last = pool.tensor_tensor(A["sp"][:, hh, r:r + P], A["sp"][:, hh, r:r + P], cst("mask_sb"),
                                                  ALU.mult)
                    last.then_inc(s("sb_mask"), 1)
            sum_squares("ff0")
            sum_squares("pw")
            adds, prods = TAPS_POOL - 1, TAPS_POOL

            def taps(i, u):
                pool.wait_ge(s("cv_pe"), i * 2 + CREDIT)
                pool.tensor_copy(A["wt"][:, u], vec[:, bass.ds(i * (2 * TAPS) + (_cols["w_dw"] + u * TAPS), TAPS_PE)])\
                    .then_inc(s("wt_ready"), 1)
                pool.wait_ge(s("wt_ready"), i * 2 + (u + 1))
                shape = [P, TAPS_PE, P]
                pool.tensor_tensor(A["dg"][:, u], cst("ident").unsqueeze(1).to_broadcast(shape),
                                   A["wt"][:, u].unsqueeze(2).to_broadcast(shape), ALU.mult)\
                    .then_inc(s("dg_ready"), 1)
                for m in range(1, TAPS_POOL):
                    pool.wait_ge(s("cv_prod"), i * (2 * prods) + (u * prods + m + 1))
                    pool.wait_ge(s("cv_padd"), i * (2 * adds) + (u * adds + m - 1) + CREDIT)
                    product = A["pr"][:, (u * prods + m) % 4]
                    pool.tensor_tensor(A["pa"][:, u], A["pr"][:, u * prods % 4] if m == 1 else A["pa"][:, u],
                                       product, ALU.add).then_inc(s("cv_padd"), 1)

            with pool.Fori(0, 4) as i:
                taps(i, 0)
                taps(i, 1)
            sum_squares("ff1")
            sum_squares("da")

            def stage(pair, e):
                if not isinstance(pair, int) or pair:
                    pool.wait_ge(s("da_o"), pair * 2 + (e - 1) + CREDIT)
                pool.wait_ge(evac_done, T_DA)
                pool.tensor_copy(A["vh"][:, e], A["dv"][:, :, bass.ds(pair * 256 + e * 128, P)])\
                    .then_inc(s("da_vh"), 1)

            def rotated(pair, e, c):
                done = pair * 4 + (2 * e + c + 1)
                if not isinstance(pair, int) or pair:
                    pool.wait_ge(s("da_s"), pair * 8 + (4 * e - 4))
                pool.wait_ge(evac_done, done + T_DA)
                pool.tensor_tensor(A["dq"][:, e, c], A["draw"][:, c], cst("cos"), ALU.mult).then_inc(s("da_rc"), 1)
                pool.wait_ge(s("da_rc"), done)
                pool.wait_ge(s("da_shs"), done)
                pool.tensor_tensor(A["dq"][:, e, c], A["dq"][:, e, c], A["dsh"][:, c], ALU.add)\
                    .then_inc(s("da_qn"), 1)

            def pair_inputs(pair):
                for e in (0, 1):
                    rotated(pair, e, 0)
                    rotated(pair, e, 1)
                    stage(pair, e)

            pair_inputs(0)
            with pool.Fori(1, 4) as pair:
                pair_inputs(pair)
            for name in ("da_post", "mlp0", "mlp0_post", "sc", "sc_post", "mlp1", "mlp1_post"):
                sum_squares(name)
            for k in range(0, KB, 2):
                pool.wait_ge(post_t, 8 * POST["mlp1"] + k + 1)
                pool.tensor_tensor(h[:, k], h[:, k], A["m"][:, k], ALU.add).then_inc(h_added_pool, 1)

        @block.tensor
        def _(pe):
            def passes(out, t_hi, t_lo, a_hi, a_lo, first, last, stationary_is_weight=True):
                w = ((t_hi, a_hi), (t_hi, a_lo), (t_lo, a_hi))
                for n, (wt, ac) in enumerate(w):
                    lhs, rhs = (wt, ac) if stationary_is_weight else (ac, wt)
                    mm = pe.matmul(out, lhs, rhs, start=first and n == 0, stop=last and n == 2)
                return mm

            def tile(t, bank, hi, lo, ready=None, base=0, blocks=KB, free=None):
                pe.wait_ge(wlo_ready, t.count)
                if free is None:
                    if t.n >= RING:
                        pe.wait_ge(evac_done, t.count - RING)
                else:
                    pe.wait_ge(evac_done, free)
                w_h = whi[:, t.slot].rearrange("p (k n) -> p k n", k=KB)
                w_l = wlo[:, t.slot].rearrange("p (k n) -> p k n", k=KB)
                for k in range(blocks):
                    if ready is not None:
                        pe.wait_ge(ready, base + (k + 1))
                    mm = passes(ps[:, bank], w_h[:, k], w_l[:, k], hi[:, k], lo[:, k], k == 0, k == blocks - 1)
                mm.then_inc(tile_done, 1)

            def part(t, bank, hi, lo, blocks, free=None, ready=None, base=0):
                if blocks[0] == 0:
                    pe.wait_ge(wlo_ready, t.count)
                    if free is not None:
                        pe.wait_ge(evac_done, free)
                w_h = whi[:, t.slot].rearrange("p (k n) -> p k n", k=KB)
                w_l = wlo[:, t.slot].rearrange("p (k n) -> p k n", k=KB)
                for k in blocks:
                    if ready is not None:
                        pe.wait_ge(ready, base + (k + 1))
                    mm = passes(ps[:, bank], w_h[:, k], w_l[:, k], hi[:, k], lo[:, k], k == 0, k == KB - 1)
                if blocks[-1] == KB - 1:
                    mm.then_inc(tile_done, 1)

            def wide(t, j, rows, cols, bank=0):
                pe.wait_ge(wlo_ready, t.count)
                w_h = whi[:, t.slot].rearrange("p (k n) -> p k n", k=rows)
                w_l = wlo[:, t.slot].rearrange("p (k n) -> p k n", k=rows)
                for tb in range(TB):
                    tok = slice(tb * P, (tb + 1) * P)
                    for k in range(rows):
                        kk = j * rows + k
                        mm = passes(ps[:, bank + tb, 0:cols], w_h[:, k], w_l[:, k], xh[:, kk, tok], xl[:, kk, tok],
                                    kk == 0, kk == KB - 1, stationary_is_weight=False)
                mm.then_inc(tile_done, 1)

            def row_sum(name, bank=4):
                if name in BY_PE:
                    pe.wait_ge(acc_ready, ACC[name] + KB - 1)
                    pe.matmul(ps[:, bank], cst("ones"), acc[:], start=True, stop=False)
                    pe.wait_ge(sq_ready, (SUM[name] - (SUM[name] > 3) + 1) * KB)
                    mm = pe.matmul(ps[:, bank], cst("ones"), sq[:, 1], start=False, stop=True)
                else:
                    pe.wait_ge(acc_ready, ACC[name] + KB)
                    mm = pe.matmul(ps[:, bank], cst("ones"), acc[:], start=True, stop=True)
                mm.then_inc(sum_ready, 1)

            def col_sum(name, bank=5):
                last_by_pe = name in BY_PE
                pe.wait_ge(acc_ready, ACC[name] + KB - last_by_pe)
                if last_by_pe:
                    pe.wait_ge(sq_ready, (SUM[name] - (SUM[name] > 3) + 1) * KB)
                for tb in range(TB):
                    tok = slice(tb * P, (tb + 1) * P)
                    mm = pe.matmul(ps[:, bank, tb:tb + 1], acc[:, tok], cst("ones", cols=1), start=True,
                                   stop=not last_by_pe)
                    if last_by_pe:
                        mm = pe.matmul(ps[:, bank, tb:tb + 1], sq[:, 1, tok], cst("ones", cols=1), start=False, stop=True)
                mm.then_inc(colsum_ready, 1)

            def first_round(t0, hi, lo, hi_ready, ready, base):
                pe.wait_ge(wlo_ready, t0.plus(FIRST - 1).count)
                pe.wait_ge(evac_done, t0.count - 1)
                w_h = [whi[:, j].rearrange("p (k n) -> p k n", k=KB) for j in range(FIRST)]
                w_l = [wlo[:, j].rearrange("p (k n) -> p k n", k=KB) for j in range(FIRST)]
                pe.wait_ge(hi_ready, base + 1)
                for j in range(FIRST):
                    pe.matmul(ps[:, j], w_h[j][:, 0], hi[:, 0], start=True, stop=False)
                    pe.matmul(ps[:, j], w_l[j][:, 0], hi[:, 0], start=False, stop=False)
                pe.wait_ge(ready, base + 1)
                for j in range(FIRST):
                    pe.matmul(ps[:, j], w_h[j][:, 0], lo[:, 0], start=False, stop=False)
                for k in range(1, KB):
                    pe.wait_ge(ready, base + (k + 1))
                    for j in range(FIRST):
                        mm = passes(ps[:, j], w_h[j][:, k], w_l[j][:, k], hi[:, k], lo[:, k], False, k == KB - 1)
                        if k == KB - 1:
                            mm.then_inc(tile_done, 1)

            pe.wait_ge(s("wglr_lo"), 1)
            g_h = A["wgh"][:].rearrange("p (k n) -> p k n", k=KB)
            g_l = A["wgl"][:].rearrange("p (k n) -> p k n", k=KB)
            for k in range(KB):
                pe.wait_ge(x_ready, k + 1)
                mm = passes(ps[:, 6], g_h[:, k], g_l[:, k], xh[:, k], xl[:, k], k == 0, k == KB - 1)
            mm.then_inc(s("glr_done"), 1)
            pe.wait_ge(small_in[1], 16)
            col_sum("hyb")
            row_sum("hyb")
            wide(Tile(0), 0, 4, 256)
            wide(Tile(1), 1, 4, 256)
            tile(Tile(2), 2, xh, xl, free=2)
            tile(Tile(3), 3, xh, xl, free=2)
            pe.wait_ge(s("glr_evac"), 2)
            pe.wait_ge(small_in[2], 16)
            for tb in range(TB):
                mm = pe.matmul(ps[:, 6 + tb // 2, (tb % 2) * 256:(tb % 2 + 1) * 256], A["glr"][0:17, tb * P:(tb + 1) * P],
                               A["wg2"][0:17, :], start=True, stop=True)
            mm.then_inc(s("gate_x"), 1)
            pe.wait_ge(evac_done, T_GV)
            for j in range(4):
                wide(Tile(T_GV + j), j, 2, 512)
            pe.wait_ge(s("la_ready"), 1)
            pe.wait_ge(rcol_ready, 1)
            pe.wait_ge(rrow_ready, 1)
            for tb in range(TB):
                pe.matmul(ps[:, 4 + tb // 2, (tb % 2) * 256:(tb % 2 + 1) * 256], cst("later64"), A["la"][:, tb],
                          start=True, stop=True)
            for j in range(2):
                for tb in range(TB):
                    mm = pe.matmul(ps[:, 6, j * 8 + 2 * tb:j * 8 + 2 * tb + 2], A["la"][:, tb, j * P:(j + 1) * P],
                                   cst("chunk"), start=True, stop=True)
            mm.then_inc(s("suf_ready"), 1)
            for j in range(4):
                tile(Tile(T_GR + j), j, xh, xl)
            pe.wait_ge(s("kend_ready"), 1)
            pe.wait_ge(s("dec_ready"), 1)
            for tb in range(TB):
                for c in range(2):
                    tok = slice(64 * c, 64 * c + 64)
                    for j in range(2):
                        u = 2 * tb + j
                        for e in range(2):
                            hd = 2 * j + e
                            mm = pe.matmul(ps[64 * e:64 * e + 64, 4 + 2 * c + u // 4, (u % 4) * P:(u % 4 + 1) * P],
                                           A["gk"][tok, tb, hd * 64:hd * 64 + 64], A["gv"][tok, tb, hd * P:(hd + 1) * P],
                                           start=True, stop=True)
            mm.then_inc(s("upd_ready"), 4)
            pe.wait_ge(evac_done, T_SV)
            for j in range(2):
                wide(Tile(T_SV + j), j, 2, 512)
            pe.wait_ge(s("state_ready"), 16)
            for hd in range(GLA_HEADS):
                j, r = hd // 2, slice(64 * (hd % 2), 64 * (hd % 2) + 64)
                for n in range(8):
                    tok = slice(n * 64, n * 64 + 64)
                    mm = pe.matmul(ps[:, 4 + hd, tok], A["S"][r, n, j], A["gq"][r, j, tok], start=True, stop=True)
                mm.then_inc(s("go_ready"), 1)
            for j in range(2, 4):
                wide(Tile(T_SV + j), j, 2, 512)

            def gla_sum(hd):
                pe.wait_ge(evac_done, T_SV + 1 + hd % 2)
                if hd >= 2:
                    pe.wait_ge(s("gln_ready"), hd - 1)
                pe.wait_ge(s("gsq_ready"), hd + 1)
                pe.matmul(ps[:, 2 + hd % 2], cst("ones"), A["gt"][:, (hd % 2) * T:(hd % 2 + 1) * T], start=True,
                          stop=True).then_inc(s("gsum_ready"), 1)

            start_of = {0: 0, 1: 512, 2: 1024, 3: 896}

            def qk_part(p, c, blocks):
                if p and blocks[0] == 0:
                    pe.wait_ge(s("sb_ln"), 2 * p + c - 1)
                part(Tile(T_SB + 2 * p + c), c, xh, xl, blocks, free=T_SB + max(2 * p + c - 1, 0))

            def qk_sum(p, c):
                pe.wait_ge(s("sb_sq"), 2 * p + c + 1)
                pe.matmul(ps[:, c], cst("blk64"), A["ssq"][:, c], start=True, stop=True).then_inc(s("sb_sum"), 1)

            def scores(p, hh):
                b, r = 2 + 3 * hh, slice(64 * hh, 64 * hh + 64)
                pe.wait_ge(s("sb_qn"), 2 * p + 2)
                if p:
                    pe.wait_ge(s("sb_yl"), 2 * p + hh - 1)
                else:
                    pe.wait_ge(s("gt_ready"), GLA_HEADS)
                    pe.wait_ge(s("gln_ready"), GLA_HEADS)
                for kb in (0, 1, 3, 2):
                    a, w = start_of[kb], 512 - kb * P
                    mm = pe.matmul(flat[:, b * 512 + a:b * 512 + a + w], A["sqn"][r, 1, kb * P:(kb + 1) * P],
                                   A["sqn"][r, 0, kb * P:512], start=kb != 3, stop=True, skip_group_check=True)
                mm.then_inc(s("sb_z"), 1)

            def accumulate(p, hh):
                b = 2 + 3 * hh
                pe.wait_ge(s("sb_spl"), 2 * p + hh + 1)
                pe.wait_ge(s("exact_ready"), 1)
                for kb in range(TB):
                    a = b * 512 + start_of[kb]
                    for k2 in range(kb, TB):
                        off, w2 = (k2 - kb) * P, 512 - k2 * P
                        for part_of_sp in (A["sph"][:, hh], A["spl"][:, hh]):
                            pe.matmul(flat[:, a + off:a + off + w2], cst_r("negtri" if k2 == kb else "negones"),
                                      part_of_sp[:, start_of[k2]:start_of[k2] + w2], start=False, stop=True,
                                      skip_group_check=True)
                    mm = pe.matmul(flat[:, a:a + P], cst_r("ident"), cst_r("neg_sb"), start=False, stop=True,
                                   skip_group_check=True)
                mm.then_inc(s("sb_acc"), 1)

            def values(p, hh):
                b, r = 2 + 3 * hh, slice(64 * hh, 64 * hh + 64)
                pe.wait_ge(s("sb_w"), 2 * p + hh + 1)
                pe.wait_ge(s("sb_vp"), p + 1)
                for kb in range(TB):
                    a, w = start_of[kb], 512 - kb * P
                    mm = pe.matmul(ps[r, b, kb * P:512], A["vp"][:, kb, r], A["sl"][:, hh, a:a + w],
                                   start=kb == 0, stop=kb == TB - 1)
                mm.then_inc(s("sb_o"), 1)

            def between(p, c, blocks):
                if p < SB_PAIRS - 1:
                    qk_part(p + 1, c, blocks)
                else:
                    if blocks[0] == 0:
                        pe.wait_ge(y_ready, GLA_HEADS)
                        pe.wait_ge(s("sb_yl"), 2 * p)
                        pe.wait_ge(s("sb_ln"), SB_HEADS)
                    part(Tile(T_WO + c), c, yh, yl, [k for k in blocks if k < KB - 1], free=T_WO)

            gla_sum(0)
            gla_sum(1)
            pe.wait_ge(evac_done, T_SB)
            qk_part(0, 0, range(KB))
            gla_sum(2)
            gla_sum(3)
            qk_part(0, 1, range(0, 4))
            qk_sum(0, 0)
            qk_part(0, 1, range(4, 8))
            qk_sum(0, 1)
            for p in range(SB_PAIRS):
                scores(p, 0)
                scores(p, 1)
                between(p, 0, range(KB))
                between(p, 1, range(0, 4))
                accumulate(p, 0)
                between(p, 1, range(4, 8))
                accumulate(p, 1)
                if p < SB_PAIRS - 1:
                    qk_sum(p + 1, 0)
                    qk_sum(p + 1, 1)
                values(p, 0)
                values(p, 1)

            pe.wait_ge(s("sb_yl"), SB_HEADS - 1)
            part(Tile(T_WO + 2), 2, yh, yl, range(KB - 1))
            pe.wait_ge(s("sb_yl"), SB_HEADS)
            for k in range(3):
                part(Tile(T_WO + k), k, yh, yl, [KB - 1])
            for k in range(3, KB):
                tile(Tile(T_WO + k), k % RING, yh, yl)

            def down(t, y, blocks=KB):
                for j in range(KB):
                    tile(t.plus(j), j % RING, yh, yl, y_ready, y, blocks=blocks)

            def swiglu(f, t0, y0):
                name = f"ff{f}"
                tile(Tile(t0), 0, xh, xl, x_ready, 8 * PRE[name])
                row_sum(name)
                for j in range(1, RING):
                    tile(Tile(t0 + j), j, xh, xl)

                def up(t):
                    for j in range(RING):
                        tile(t.plus(j), j, xh, xl)

                with pe.Fori(1, 4) as i:
                    up(Tile(t0, i))
                down(Tile(t0 + 16), y0)
                with pe.Fori(0, 4) as i:
                    up(Tile(t0 + 24, i))
                down(Tile(t0 + 40), y0 + 8)
                with pe.Fori(0, 3) as i:
                    up(Tile(t0 + 48, i))
                down(Tile(t0 + 60), y0 + 16, FF_GROUPS[2])

            swiglu(0, T_FF0, Y0["ff0"])

            def conv(i, u):
                pe.wait_ge(s("dg_ready"), i * 2 + (u + 1))
                pe.wait_ge(s("pw_u"), i * 2 + (u + 1))
                if u or not isinstance(i, int):
                    pe.wait_ge(s("cv_done"), i * 2 + (u - 1))
                for k in range(TAPS_PE):
                    mm = pe.matmul(ps[:, 5 + u], A["dg"][:, u, k], A["ub"][:, u, k:k + T], start=k == 0,
                                   stop=k == TAPS_PE - 1)
                mm.then_inc(s("cv_pe"), 1)

            tile(Tile(T_PW1), 0, xh, xl, x_ready, 8 * PRE["pw"])
            row_sum("pw")
            tile(Tile(T_PW1 + 1), 1, xh, xl)
            tile(Tile(T_PW1 + 2), 2, xh, xl)
            conv(0, 0)
            tile(Tile(T_PW1 + 3), 3, xh, xl)
            with pe.Fori(1, 4) as i:
                tile(Tile(T_PW1, i), 0, xh, xl)
                conv(i - 1, 1)
                tile(Tile(T_PW1 + 1, i), 1, xh, xl)
                tile(Tile(T_PW1 + 2, i), 2, xh, xl)
                conv(i, 0)
                tile(Tile(T_PW1 + 3, i), 3, xh, xl)
            conv(3, 1)
            for k in range(KB):
                pe.wait_ge(s("cv_done"), k + 1)
                mm = pe.matmul(ps[:, 7], cst("ones"), A["cv"][:, k], start=k == 0, stop=k == KB - 1)
            mm.then_inc(s("mu_sum"), 1)
            for k in range(KB):
                pe.wait_ge(s("cen_sq"), k + 1)
                mm = pe.matmul(ps[:, 4], cst("ones"), sq[:, k % 2], start=k == 0, stop=k == KB - 1)
                if k < KB - 1:
                    mm.then_inc(s("var_mm"), 1)
            mm.then_inc(sum_ready, 1)
            first_round(Tile(T_PW2), yh, yl, yh_ready, y_ready, Y0["pw"])
            for j in range(FIRST, KB):
                tile(Tile(T_PW2 + j), j % RING, yh, yl)

            swiglu(1, T_FF1, Y0["ff1"])

            pe.wait_ge(rrow_ready, SUM["ff1"] + 1)
            for j in range(4):
                if j == 2:
                    pe.wait_ge(evac_done, T_DV)
                    pe.wait_ge(s("lam_p"), 1)
                    pe.matmul(ps[:, 2, 0:2], cst("ones"), lamt[:, 0], start=True, stop=True).then_inc(s("lam_s"), 1)
                if j == 3:
                    col_sum("da", bank=1)
                    row_sum("da", bank=0)
                pe.wait_ge(x_ready, 8 * PRE["da"] + 2 * j + 2)
                wide(Tile(T_DV + j), j, 2, 512, bank=4)
            pe.wait_ge(rrow_ready, SUM["da"] + 1)
            pe.wait_ge(rcol_ready, 2)
            pe.wait_ge(s("lam_e"), 1)
            for j in range(4):
                wide(Tile(T_DV + 4 + j), j, 2, 512)

            def head_pair(i, before, fill):
                def scores(e, u):
                    n, p, kv = 4 * e + u, u % 2, (u + 1) * P
                    pe.wait_ge(s("da_qn"), i * 4 + (2 * e + 2) + CREDIT)
                    if n >= 2:
                        pe.wait_ge(s("da_exp"), i * 16 + 2 * (n - 1) + CREDIT)
                    else:
                        pe.wait_ge(s("da_exp"), i * 16 + CREDIT)
                    for c in (0, 1):
                        r, b = slice(64 * c, 64 * c + 64), 2 + 2 * p + c
                        pe.matmul(ps[:, b, 0:kv], A["dq"][r, e, 0, u * P:(u + 1) * P], A["dq"][r, e, 1, 0:kv],
                                  start=True, stop=True)
                        mm = pe.matmul(ps[:, b, kv - P:kv], cst_r("ident"), cst_r("neg_da"), start=False, stop=True,
                                       skip_group_check=True)
                    mm.then_inc(s("da_s"), 1)

                def transposes(e, u):
                    n = 4 * e + u
                    pe.wait_ge(s("da_a"), i * 8 + (n + 1))
                    pe.wait_ge(s("da_aT"), i * 8 + n + CREDIT)
                    if u == 0:
                        pe.wait_ge(s("da_ln"), i * 2 + e + CREDIT)
                    for b in range(u + 1):
                        mm = pe.transpose(ps[:, 6, b * P:(b + 1) * P], A["da"][:, u % 2, b * P:(b + 1) * P], cst("ident"))
                    mm.then_inc(s("da_T"), 1)

                def values(e, u):
                    n, at = 4 * e + u, P * u * (u + 1) // 2
                    pe.wait_ge(s("da_aT"), i * 8 + (n + 1) + CREDIT)
                    if u == 0:
                        pe.wait_ge(s("da_vh"), i * 2 + (e + 1))
                        pe.wait_ge(s("da_ot"), i * 2 + e + CREDIT)
                    for b in range(u + 1):
                        mm = pe.matmul(ps[:, 7, u * P:(u + 1) * P], A["vh"][:, e, b], A["aT"][:, at + b * P:at + b * P + P],
                                       start=b == 0, stop=b == u)
                    if u == 3:
                        mm.then_inc(s("da_o"), 1)

                def norm_sum(done):
                    pe.wait_ge(s("da_sq"), done)
                    pe.matmul(ps[:, 6], cst("ones"), sq[:, 0], start=True, stop=True).then_inc(s("da_sum"), 1)

                def between(e, c, blocks):
                    if fill:
                        part(Tile(T_DA + 4 + 2 * e + c, i), c, xh, xl, blocks, free=i * 4 + (T_DA + 4 + 2 * e + c - 1))
                    else:
                        those = {(0, 0): [0, 1], (0, 4): [2], (1, 0): [3], (1, 4): [4, 5]}.get((c, blocks[0]))
                        if those:
                            part(Tile(T_DO + e), e, yh, yl, those, free=T_DO, ready=y_ready, base=Y0["da"])

                for e in (0, 1):
                    scores(e, 0)
                    scores(e, 1)
                    if e or before:
                        norm_sum(i * 2 + e)
                    between(e, 0, range(0, 4))
                    scores(e, 2)
                    transposes(e, 0)
                    between(e, 0, range(4, 8))
                    scores(e, 3)
                    transposes(e, 1)
                    between(e, 1, range(0, 4))
                    transposes(e, 2)
                    values(e, 0)
                    values(e, 1)
                    between(e, 1, range(4, 8))
                    transposes(e, 3)
                    values(e, 2)
                    values(e, 3)
                if not fill:
                    pe.wait_ge(s("da_exp"), 2 * 4 * DA_HEADS + CREDIT)
                    for j in (2, 3):
                        part(Tile(T_DO + j), j, yh, yl, range(0, 6))
                        if j == 2:
                            norm_sum(DA_HEADS)

            for n in range(4):
                tile(Tile(T_DA + n), n % 2, xh, xl, free=T_DV + 5 + n if n < 2 else T_DA + n - 1)
            head_pair(0, False, True)
            with pe.Fori(1, 3) as i:
                head_pair(i, True, True)
            head_pair(3, True, False)
            for j in range(4):
                part(Tile(T_DO + j), j, yh, yl, range(6, 8), ready=y_ready, base=Y0["da"])
            for j in range(4, KB):
                tile(Tile(T_DO + j), j % RING, yh, yl)
            row_sum("da_post")

            def to_m(t0, which, y0):
                down(Tile(t0), y0)
                row_sum(which + "_post")

            def mlp(f, t0, y0):
                name = f"mlp{f}"
                first_round(Tile(t0), xh, xl, xh_ready, x_ready, 8 * PRE[name])
                row_sum(name)
                tile(Tile(t0 + FIRST), FIRST, xh, xl)

                def up(t):
                    for j in range(RING):
                        tile(t.plus(j), j, xh, xl)

                up(Tile(t0 + 4))
                down(Tile(t0 + 8), y0)
                with pe.Fori(1, MLP_GROUPS - 1) as g:
                    with pe.Fori(0, 2) as i:
                        up(Tile(t0, g * 4 + i))
                    down(Tile(t0 + 8, g * 4), g * 8 + y0)
                with pe.Fori(0, 2) as i:
                    up(Tile(t0 + 48, i))
                to_m(t0 + 56, name, y0 + 24)

            mlp(0, T_MLP0, Y0["mlp0"])

            first_round(Tile(T_SC), xh, xl, xh_ready, x_ready, 8 * PRE["sc"])
            row_sum("sc")
            tile(Tile(T_SC + FIRST), FIRST, xh, xl)
            with pe.Fori(1, 6) as i:
                for j in range(RING):
                    tile(Tile(T_SC + j, i), j, xh, xl)
            to_m(T_SCO, "sc", Y0["sc"])
            mlp(1, T_MLP1, Y0["mlp1"])


Y0 = {"ff0": 4, "pw": 26, "ff1": 34, "da": 56, "mlp0": 64, "sc": 96, "mlp1": 104}


def _narrow(w, k0, n):
    rows = w[k0:k0 + D, n * P:(n + 1) * P]
    if rows.shape[0] < D:
        rows = np.concatenate([rows, np.zeros((D - rows.shape[0], P), rows.dtype)])
    return rows.reshape(KB, P, P).transpose(1, 0, 2).reshape(P, D)


def _wide(w, j, rows, c0, cols):
    return w[j * rows * P:(j + 1) * rows * P, c0:c0 + cols].reshape(rows, P, cols).transpose(1, 0, 2).reshape(P, D)


def _stream(a):
    w = a["hy_w_in"][0]
    c_glr, c_sq, c_sk, c_sv = 1536, 1552, 2064, 2576
    gr, sbw = w[:, 1024:1536], w[:, c_sq:]
    tiles = [_wide(w, j, 4, 256, 256) for j in range(2)]
    tiles += [_narrow(w, 0, j) for j in range(2)]
    tiles += [_wide(w, j, 2, 512, 512) for j in range(4)]
    tiles += [_narrow(gr, 0, j) for j in range(4)]
    tiles += [_wide(w, j, 2, c_sv, 512) for j in range(4)]
    for p in range(4):
        tiles += [_narrow(sbw, 0, p), _narrow(sbw, 0, 4 + p)]
    tiles += [_narrow(a["hy_w_out"][0], 0, n) for n in range(KB)]

    def swiglu(f):
        out, at = [], 0
        for g in FF_GROUPS:
            for q in range(at, at + g):
                out += [_narrow(a["ffn_w_gate"][f], 0, q), _narrow(a["ffn_w_up"][f], 0, q)]
            rows = a["ffn_w_down"][f][at * P:(at + g) * P]
            out += [_narrow(rows, 0, n) for n in range(KB)]
            at += g
        return out

    tiles += swiglu(0)
    for j in range(KB):
        tiles += [_narrow(a["cv_w_pw1"][0], 0, j), _narrow(a["cv_w_pw1"][0], 0, KB + j)]
    tiles += [_narrow(a["cv_w_pw2"][0], 0, n) for n in range(KB)]
    tiles += swiglu(1)
    qkv = a["attn_w_qkv_2"][0]
    for r in range(2):
        tiles += [_wide(qkv, j, 2, 2048 + 512 * r, 512) for j in range(4)]
    for q in range(DA_HEADS):
        tiles += [_narrow(qkv, 0, q), _narrow(qkv, 0, KB + q)]
    tiles += [_narrow(a["attn_w_o_2"][0], 0, n) for n in range(KB)]

    def mlp(f):
        out = []
        for g in range(MLP_GROUPS):
            out += [_narrow(a["mlp_w_up_2"][f], 0, 8 * g + j) for j in range(8)]
            out += [_narrow(a["mlp_w_down_2"][f], g * D, n) for n in range(KB)]
        return out

    tiles += mlp(0)
    for j in range(KB):
        tiles += [_narrow(a["conv_w_in_2"][0], 0, c * KB + j) for c in (1, 2, 0)]
    tiles += [_narrow(a["conv_w_out_2"][0], 0, n) for n in range(KB)]
    tiles += mlp(1)
    assert len(tiles) == NT
    return np.stack(tiles)


def _vectors(a):
    f = np.zeros((P, NVEC), a["x"].dtype)

    def put(name, v, at=0):
        cols = np.asarray(v).reshape(-1, P).T
        f[:, _cols[name] + at:_cols[name] + at + cols.shape[1]] = cols

    for n, v in enumerate((a["mix_norm"][0], a["ffn_norm"][0], a["mix_norm"][1], a["ffn_norm"][1],
                           a["norm_mixer_pre_2"][0], a["norm_mlp_pre_2"][0], a["norm_mixer_pre_2"][1],
                           a["norm_mlp_pre_2"][1])):
        put("pre", v, 8 * n)
    for n, v in enumerate((a["norm_mixer_post_2"][0], a["norm_mlp_post_2"][0], a["norm_mixer_post_2"][1],
                           a["norm_mlp_post_2"][1])):
        put("post", v, 8 * n)
    put("b_pw1", a["cv_b_pw1"][0])
    f[:, _cols["w_dw"]:_cols["w_dw"] + TAPS * KB] = \
        a["cv_w_dw"][0].reshape(TAPS, KB, P).transpose(2, 1, 0).reshape(P, -1)
    put("b_dw", a["cv_b_dw"][0])
    put("ln_g", a["cv_ln_g"][0])
    put("ln_b", a["cv_ln_b"][0])
    put("b_pw2", a["cv_b_pw2"][0])
    put("gla", a["hy_gla_norm"][0])
    put("sbq", np.tile(a["hy_sb_q_norm"][0], 2))
    put("sbk", np.tile(a["hy_sb_k_norm"][0], 2))
    put("subln", a["attn_subln_g_2"][0])
    f[:, _cols["conv_w"]:_cols["conv_w"] + 24] = a["conv_w_2"][0].reshape(3, KB, P).transpose(2, 1, 0).reshape(P, -1)
    for n, v in enumerate(("q1", "k1", "q2", "k2")):
        f[:64, _cols["lam"] + n] = a[f"attn_lambda_{v}_2"][0]
    return f


def _constants():
    f = np.zeros((P, NCONST), np.float32)
    p, c = np.arange(P)[:, None], np.arange(P)[None, :]

    def put(name, v):
        at, n = _consts[name]
        f[:, at:at + n] = v

    put("ident", p == c)
    put("ones", 1.0)
    put("blk64", p // 64 == c // 64)
    put("negtri", -1.0 * (p >= c))
    put("negones", -1.0)
    put("later64", (p > c) & (p // 64 == c // 64))
    put("neg_sb", np.where(p < c, 0.0, NEG))
    put("neg_da", np.where(c <= p, 0.0, NEG))
    put("mask_sb", p < c)
    put("chunk", p // 64 == np.arange(2)[None, :])
    half = 8
    inv = 500000.0 ** (-np.arange(0, 16, 2, dtype=np.float32) / np.float32(16))
    ang = (np.arange(T, dtype=np.float32)[:, None] * inv[None, :].astype(np.float32)).astype(np.float32)
    cos, sin = np.ones((64, T), np.float32), np.zeros((64, T), np.float32)
    cos[:half] = cos[half:16] = np.cos(ang).T
    sin[:half], sin[half:16] = -np.sin(ang).T, np.sin(ang).T
    put("cos", np.tile(cos, (2, 1)))
    put("sin", np.tile(sin, (2, 1)))
    return f


def kernel(**inputs):
    import concourse.bacc as bacc
    from concourse.bass_utils import run_bass_kernel_spmd

    a = {k: np.asarray(v) for k, v in inputs.items()}
    w_in = a["hy_w_in"][0]
    glr = np.concatenate([w_in[:, 1536:1552], np.zeros((D, P - 16), w_in.dtype)], axis=1)
    arrays = {
        "x_t": np.ascontiguousarray(a["x"][0].T),
        "stream": _stream(a),
        "w_glr": np.ascontiguousarray(_narrow(glr, 0, 0)),
        "w_gate": np.ascontiguousarray(np.concatenate([a["hy_w_gate2"][0], a["hy_b_gate"]], axis=0)),
        "vecs": _vectors(a),
        "consts": _constants(),
    }
    nc = bacc.Bacc("TRN2", target_bir_lowering=False, num_devices=1)
    args = [nc.dram_tensor(n, v.shape, mybir.dt.from_np(v.dtype), kind="ExternalInput").ap() for n, v in arrays.items()]
    out_t = nc.dram_tensor("out_t", (D, T), F32, kind="ExternalOutput").ap()
    build(nc, *args, out_t)
    got = run_bass_kernel_spmd(nc, [arrays], core_ids=[0]).results[0]["out_t"]
    return np.ascontiguousarray(np.asarray(got).T)[None]
```
